# Optimizing a Trainium2 kernel written in Bass

```python
import math
import jax
import jax.numpy as jnp
from jax import lax
import numpy as np

D_MODEL = 1024
BATCH = 1
SEQ = 256
DEPTH = 2

N_MIXERS = 4
D_FF = 2816
NORM_EPS = 1e-6
ROPE_THETA = 500000.0
ROPE_FRACTION = 4
BLOCK = 128
NEG_INF = -1e30

SWA_HEADS = 16
SWA_KV_HEADS = 2
SWA_HEAD_DIM = 64
SWA_WINDOW = 128

GDN_HEADS = 8
GDN_HEAD_DIM = 128
GDN_CONV = 4
GDN_CHUNK = 64

SSD_D_INNER = 2 * D_MODEL
SSD_HEAD_DIM = 64
SSD_HEADS = SSD_D_INNER // SSD_HEAD_DIM
SSD_GROUPS = 4
SSD_STATE = 128
SSD_CONV = 4
SSD_CHUNK = 128

DIL_PATTERN = ((128, 1), (512, 4), (2048, 16))
DIL_HEADS = 16
DIL_KV_HEADS = 4
DIL_HEAD_DIM = 64

kernel_name = "hybrid_interleaved_swa_gdn_ssd_dilated"

def rmsnorm(x, gain):
    xf = x.astype(jnp.float32)
    y = xf * lax.rsqrt(jnp.mean(xf * xf, axis=-1, keepdims=True) + NORM_EPS)
    return (y * gain.astype(jnp.float32)).astype(x.dtype)

def l2norm(x):
    xf = x.astype(jnp.float32)
    return xf * lax.rsqrt(jnp.sum(xf * xf, axis=-1, keepdims=True) + NORM_EPS)

def swiglu(x, w_in, w_out):
    gate, up = jnp.split(x @ w_in, 2, axis=-1)
    return (jax.nn.silu(gate) * up) @ w_out

def rope_tables(positions, head_dim):
    rot = head_dim // ROPE_FRACTION
    inv_freq = ROPE_THETA ** (-jnp.arange(0, rot, 2, dtype=jnp.float32) / rot)
    ang = positions.astype(jnp.float32)[..., None] * inv_freq
    return jnp.cos(ang), jnp.sin(ang)

def apply_partial_rope(x, cos, sin):
    half = cos.shape[-1]
    c = cos[:, :, None, :].astype(x.dtype)
    s = sin[:, :, None, :].astype(x.dtype)
    x1, x2, rest = x[..., :half], x[..., half:2 * half], x[..., 2 * half:]
    return jnp.concatenate([x1 * c - x2 * s, x2 * c + x1 * s, rest], axis=-1)

def causal_depthwise_conv(x, w):
    width, ch = w.shape
    return lax.conv_general_dilated(x, w[:, None, :], window_strides=(1,), padding=[(width - 1, 0)],
                                    dimension_numbers=("NWC", "WIO", "NWC"), feature_group_count=ch)

def to_chunks(t, size):
    b, s = t.shape[:2]
    return jnp.moveaxis(t.reshape(b, s // size, size, *t.shape[2:]), 1, 0)

def banded_attention(q, k, v, n_back):
    b, L, kvh, gq, dh = q.shape
    nb = L // BLOCK
    qb = q.reshape(b, nb, BLOCK, kvh, gq, dh)

    def with_prev(t):
        tb = t.reshape(b, nb, BLOCK, kvh, dh)
        prev = jnp.concatenate([jnp.zeros_like(tb[:, :1]), tb[:, :-1]], axis=1)
        return jnp.concatenate([prev, tb], axis=2)

    kb, vb = with_prev(k), with_prev(v)
    scores = jnp.einsum("bnqkgd,bnskd->bnqkgs", qb, kb).astype(jnp.float32) * (dh ** -0.5)
    q_idx = jnp.arange(BLOCK)[:, None] + BLOCK
    s_idx = jnp.arange(2 * BLOCK)[None, :]
    rel = q_idx - s_idx
    key_pos = (jnp.arange(nb) * BLOCK - BLOCK)[:, None, None] + s_idx[None]
    visible = (rel >= 0) & (rel <= n_back) & (key_pos >= 0)
    scores = jnp.where(visible[None, :, :, None, None, :], scores, NEG_INF)
    m = jnp.max(scores, axis=-1)
    p = jnp.exp(scores - m[..., None])
    l = jnp.sum(p, axis=-1)
    acc = jnp.einsum("bnqkgs,bnskd->bnqkgd", p.astype(v.dtype), vb).astype(jnp.float32)
    return acc.reshape(b, L, kvh, gq, dh), m.reshape(b, L, kvh, gq), l.reshape(b, L, kvh, gq)

def swa_sink_mixer(x, cos, sin, w_in, b_in, sinks, w_out):
    b, s, _ = x.shape
    nh, kvh, dh = SWA_HEADS, SWA_KV_HEADS, SWA_HEAD_DIM
    gq = nh // kvh
    q, k, v = jnp.split(x @ w_in + b_in, [nh * dh, (nh + kvh) * dh], axis=-1)
    q = apply_partial_rope(q.reshape(b, s, nh, dh), cos, sin).reshape(b, s, kvh, gq, dh)
    k = apply_partial_rope(k.reshape(b, s, kvh, dh), cos, sin)
    acc, m, l = banded_attention(q, k, v.reshape(b, s, kvh, dh), SWA_WINDOW - 1)
    sink = sinks.astype(jnp.float32).reshape(kvh, gq)
    m_all = jnp.maximum(m, sink)
    rescale = jnp.exp(m - m_all)
    out = acc * (rescale / (l * rescale + jnp.exp(sink - m_all)))[..., None]
    return out.reshape(b, s, nh * dh).astype(x.dtype) @ w_out

def gated_delta_rule_chunked(q, k, v, g, beta):
    b, s, nh, dk = q.shape
    dv = v.shape[-1]
    c = GDN_CHUNK
    causal = jnp.tril(jnp.ones((c, c), dtype=bool))
    strict = jnp.tril(jnp.ones((c, c), dtype=bool), -1)
    eye = jnp.eye(c, dtype=jnp.float32)

    def heads_first(t):
        return jnp.moveaxis(to_chunks(t.astype(jnp.float32), c), 3, 2)

    def step(state, inp):
        qi, ki, vi, gi, bi = inp
        gcum = jnp.cumsum(gi, axis=-1)
        decay = jnp.exp(jnp.where(causal, gcum[..., :, None] - gcum[..., None, :], -jnp.inf))
        a_mat = eye + jnp.where(strict, jnp.einsum("bhid,bhjd->bhij", ki, ki) * decay * bi[..., :, None], 0.0)
        rhs = jnp.concatenate([vi * bi[..., None], ki * (bi * jnp.exp(gcum))[..., None]], axis=-1)
        sol = lax.linalg.triangular_solve(a_mat, rhs, left_side=True, lower=True, unit_diagonal=True)
        u, w = sol[..., :dv], sol[..., dv:]
        v_new = u - jnp.einsum("bhik,bhkv->bhiv", w, state)
        intra = jnp.where(causal, jnp.einsum("bhid,bhjd->bhij", qi, ki) * decay, 0.0)
        out = (jnp.einsum("bhid,bhdv->bhiv", qi * jnp.exp(gcum)[..., None], state)
               + jnp.einsum("bhij,bhjv->bhiv", intra, v_new))
        g_last = gcum[..., -1]
        state = (state * jnp.exp(g_last)[..., None, None]
                 + jnp.einsum("bhid,bhiv->bhdv", ki * jnp.exp(g_last[..., None] - gcum)[..., None], v_new))
        return state, out

    state0 = jnp.zeros((b, nh, dk, dv), jnp.float32)
    _, o = lax.scan(step, state0, (heads_first(q), heads_first(k), heads_first(v), heads_first(g), heads_first(beta)))
    return o.transpose(1, 0, 3, 2, 4).reshape(b, s, nh, dv)

def gated_deltanet_mixer(x, w_in, conv_w, A_log, dt_bias, norm_w, w_out):
    b, s, _ = x.shape
    nh, dk = GDN_HEADS, GDN_HEAD_DIM
    width = nh * dk
    qkv, z, beta_raw, a_raw = jnp.split(x @ w_in, [3 * width, 4 * width, 4 * width + nh], axis=-1)
    qkv = jax.nn.silu(causal_depthwise_conv(qkv, conv_w))
    q, k, v = jnp.split(qkv, 3, axis=-1)
    q = l2norm(q.reshape(b, s, nh, dk)) * (dk ** -0.5)
    k = l2norm(k.reshape(b, s, nh, dk))
    beta = jax.nn.sigmoid(beta_raw.astype(jnp.float32))
    g = -jnp.exp(A_log.astype(jnp.float32)) * jax.nn.softplus(a_raw.astype(jnp.float32) + dt_bias.astype(jnp.float32))
    o = gated_delta_rule_chunked(q, k, v.reshape(b, s, nh, dk), g, beta)
    o = rmsnorm(o, norm_w) * jax.nn.silu(z.reshape(b, s, nh, dk).astype(jnp.float32))
    return o.reshape(b, s, width).astype(x.dtype) @ w_out

def ssd_chunked(xs, dt, a, bm, cm):
    b, s, g, r, p = xs.shape
    n = bm.shape[-1]
    c = SSD_CHUNK
    causal = jnp.tril(jnp.ones((c, c), dtype=bool))
    x_dt = to_chunks(xs.astype(jnp.float32) * dt[..., None], c)
    a_dt = jnp.moveaxis(to_chunks(dt * a, c), 2, -1)
    bc = to_chunks(bm.astype(jnp.float32), c)
    cc = to_chunks(cm.astype(jnp.float32), c)

    def step(state, inp):
        xi, ai, bi, ci = inp
        acum = jnp.cumsum(ai, axis=-1)
        seg = jnp.exp(jnp.where(causal, acum[..., :, None] - acum[..., None, :], -jnp.inf))
        y_diag = jnp.einsum("blgn,bsgn,bgrls,bsgrp->blgrp", ci, bi, seg, xi)
        y_off = jnp.einsum("blgn,bgrpn,bgrl->blgrp", ci, state, jnp.exp(acum))
        a_last = acum[..., -1]
        state = (state * jnp.exp(a_last)[..., None, None]
                 + jnp.einsum("bsgn,bgrs,bsgrp->bgrpn", bi, jnp.exp(a_last[..., None] - acum), xi))
        return state, y_diag + y_off

    state0 = jnp.zeros((b, g, r, p, n), jnp.float32)
    _, y = lax.scan(step, state0, (x_dt, a_dt, bc, cc))
    return jnp.moveaxis(y, 0, 1).reshape(b, s, g, r, p)

def mamba2_ssd_mixer(x, w_in, conv_w, conv_b, dt_bias, A_log, D_skip, norm_w, w_out):
    b, s, _ = x.shape
    g, r, p, n = SSD_GROUPS, SSD_HEADS // SSD_GROUPS, SSD_HEAD_DIM, SSD_STATE
    di = SSD_D_INNER
    z, xbc, dt_raw = jnp.split(x @ w_in, [di, 2 * di + 2 * g * n], axis=-1)
    xbc = jax.nn.silu(causal_depthwise_conv(xbc, conv_w) + conv_b)
    xs, bm, cm = jnp.split(xbc, [di, di + g * n], axis=-1)
    xs = xs.reshape(b, s, g, r, p)
    dt = jax.nn.softplus(dt_raw.astype(jnp.float32) + dt_bias.astype(jnp.float32)).reshape(b, s, g, r)
    a = -jnp.exp(A_log.astype(jnp.float32)).reshape(g, r)
    y = ssd_chunked(xs, dt, a, bm.reshape(b, s, g, n), cm.reshape(b, s, g, n))
    y = y + xs.astype(jnp.float32) * D_skip.astype(jnp.float32).reshape(g, r, 1)
    y = y.reshape(b, s, di) * jax.nn.silu(z.astype(jnp.float32))
    y = rmsnorm(y.reshape(b, s, g, di // g), norm_w.reshape(g, di // g))
    return y.reshape(b, s, di).astype(x.dtype) @ w_out

def to_residues(t, d):
    b, s = t.shape[:2]
    lsub = s // d
    lpad = -(-lsub // BLOCK) * BLOCK
    t = jnp.moveaxis(t.reshape(b, lsub, d, *t.shape[2:]), 2, 1).reshape(b * d, lsub, *t.shape[2:])
    return jnp.pad(t, [(0, 0), (0, lpad - lsub)] + [(0, 0)] * (t.ndim - 2))

def from_residues(t, d, b, s):
    lsub = s // d
    t = t[:, :lsub].reshape(b, d, lsub, *t.shape[2:])
    return jnp.moveaxis(t, 1, 2).reshape(b, s, *t.shape[3:])

def dilated_mixer(x, cos, sin, w_in, w_out):
    b, s, _ = x.shape
    nh, kvh, dh = DIL_HEADS, DIL_KV_HEADS, DIL_HEAD_DIM
    gq = nh // kvh
    per_group = (nh + 2 * kvh) * dh
    proj = x @ w_in
    outs, lses = [], []
    for gi, (window, dilation) in enumerate(DIL_PATTERN):
        q, k, v = jnp.split(proj[..., gi * per_group:(gi + 1) * per_group], [nh * dh, (nh + kvh) * dh], axis=-1)
        q = apply_partial_rope(q.reshape(b, s, nh, dh), cos, sin).reshape(b, s, kvh, gq, dh)
        k = apply_partial_rope(k.reshape(b, s, kvh, dh), cos, sin)
        v = v.reshape(b, s, kvh, dh)
        acc, m, l = banded_attention(to_residues(q, dilation), to_residues(k, dilation),
                                     to_residues(v, dilation), window // dilation)
        outs.append(from_residues(acc / l[..., None], dilation, b, s))
        lses.append(from_residues(m + jnp.log(l), dilation, b, s))
    weights = jax.nn.softmax(jnp.stack(lses, axis=0), axis=0)
    out = jnp.einsum("gbskh,gbskhd->bskhd", weights, jnp.stack(outs, axis=0))
    return out.reshape(b, s, nh * dh).astype(x.dtype) @ w_out

def setup_inputs(seed: int = 0) -> dict:
    key = jax.random.key(seed)
    keys = jax.random.split(key, 48)
    counter = [0]

    def nk():
        counter[0] += 1
        return keys[counter[0] - 1]

    def dense(shape, fan_in):
        return jax.random.normal(nk(), shape, jnp.float32) * fan_in ** -0.5

    def gains(shape):
        return 1.0 + 0.02 * jax.random.normal(nk(), shape, jnp.float32)

    def small(shape, scale):
        return scale * jax.random.normal(nk(), shape, jnp.float32)

    def dt_bias_init(nheads):
        dt = jnp.exp(jax.random.uniform(nk(), (nheads,), jnp.float32, math.log(1e-3), math.log(1e-1)))
        return dt + jnp.log(-jnp.expm1(-dt))

    def a_log_init(nheads):
        return jnp.log(jax.random.uniform(nk(), (nheads,), jnp.float32, 1.0, 16.0))

    inputs = {}
    inputs["x"] = jax.random.normal(nk(), (BATCH, SEQ, D_MODEL), jnp.float32)
    inputs["positions"] = (jax.random.randint(nk(), (BATCH, 1), 0, 4096, jnp.int32)
                           + jnp.arange(SEQ, dtype=jnp.int32)[None, :])

    def channel_mixer(i):
        inputs[f"l{i}_norms"] = gains((6, D_MODEL))
        inputs[f"l{i}_ffn_w_in"] = dense((2, D_MODEL, 2 * D_FF), D_MODEL)
        inputs[f"l{i}_ffn_w_out"] = dense((2, D_FF, D_MODEL), D_FF)

    channel_mixer(0)
    swa_cols = (SWA_HEADS + 2 * SWA_KV_HEADS) * SWA_HEAD_DIM
    inputs["a_w_in"] = dense((D_MODEL, swa_cols), D_MODEL)
    inputs["a_b_in"] = small((swa_cols,), 0.02)
    inputs["a_sinks"] = small((SWA_HEADS,), 1.0)
    inputs["a_w_out"] = dense((SWA_HEADS * SWA_HEAD_DIM, D_MODEL), SWA_HEADS * SWA_HEAD_DIM)

    channel_mixer(1)
    gdn_width = GDN_HEADS * GDN_HEAD_DIM
    inputs["b_w_in"] = dense((D_MODEL, 4 * gdn_width + 2 * GDN_HEADS), D_MODEL)
    inputs["b_conv_w"] = dense((GDN_CONV, 3 * gdn_width), GDN_CONV)
    inputs["b_A_log"] = a_log_init(GDN_HEADS)
    inputs["b_dt_bias"] = dt_bias_init(GDN_HEADS)
    inputs["b_norm"] = gains((GDN_HEAD_DIM,))
    inputs["b_w_out"] = dense((gdn_width, D_MODEL), gdn_width)

    channel_mixer(2)
    ssd_conv_ch = SSD_D_INNER + 2 * SSD_GROUPS * SSD_STATE
    inputs["c_w_in"] = dense((D_MODEL, SSD_D_INNER + ssd_conv_ch + SSD_HEADS), D_MODEL)
    inputs["c_conv_w"] = dense((SSD_CONV, ssd_conv_ch), SSD_CONV)
    inputs["c_conv_b"] = small((ssd_conv_ch,), 0.02)
    inputs["c_dt_bias"] = dt_bias_init(SSD_HEADS)
    inputs["c_A_log"] = a_log_init(SSD_HEADS)
    inputs["c_D"] = gains((SSD_HEADS,))
    inputs["c_norm"] = gains((SSD_D_INNER,))
    inputs["c_w_out"] = dense((SSD_D_INNER, D_MODEL), SSD_D_INNER)

    channel_mixer(3)
    dil_cols = len(DIL_PATTERN) * (DIL_HEADS + 2 * DIL_KV_HEADS) * DIL_HEAD_DIM
    inputs["d_w_in"] = dense((D_MODEL, dil_cols), D_MODEL)
    inputs["d_w_out"] = dense((DIL_HEADS * DIL_HEAD_DIM, D_MODEL), DIL_HEADS * DIL_HEAD_DIM)
    return inputs

def reference(x, positions,
              l0_norms, l0_ffn_w_in, l0_ffn_w_out, a_w_in, a_b_in, a_sinks, a_w_out,
              l1_norms, l1_ffn_w_in, l1_ffn_w_out, b_w_in, b_conv_w, b_A_log, b_dt_bias, b_norm, b_w_out,
              l2_norms, l2_ffn_w_in, l2_ffn_w_out, c_w_in, c_conv_w, c_conv_b, c_dt_bias, c_A_log, c_D, c_norm, c_w_out,
              l3_norms, l3_ffn_w_in, l3_ffn_w_out, d_w_in, d_w_out):
    cos, sin = rope_tables(positions, SWA_HEAD_DIM)
    mixers = (
        lambda h: swa_sink_mixer(h, cos, sin, a_w_in, a_b_in, a_sinks, a_w_out),
        lambda h: gated_deltanet_mixer(h, b_w_in, b_conv_w, b_A_log, b_dt_bias, b_norm, b_w_out),
        lambda h: mamba2_ssd_mixer(h, c_w_in, c_conv_w, c_conv_b, c_dt_bias, c_A_log, c_D, c_norm, c_w_out),
        lambda h: dilated_mixer(h, cos, sin, d_w_in, d_w_out),
    )
    layer_params = (
        (l0_norms, l0_ffn_w_in, l0_ffn_w_out),
        (l1_norms, l1_ffn_w_in, l1_ffn_w_out),
        (l2_norms, l2_ffn_w_in, l2_ffn_w_out),
        (l3_norms, l3_ffn_w_in, l3_ffn_w_out),
    )
    for i in range(DEPTH):
        norms, ffn_w_in, ffn_w_out = layer_params[i]
        mixer = mixers[i % N_MIXERS]
        x = x + 0.5 * rmsnorm(swiglu(rmsnorm(x, norms[0]), ffn_w_in[0], ffn_w_out[0]), norms[1])
        x = x + rmsnorm(mixer(rmsnorm(x, norms[2])), norms[3])
        x = x + 0.5 * rmsnorm(swiglu(rmsnorm(x, norms[4]), ffn_w_in[1], ffn_w_out[1]), norms[5])
    return x


_drawn_inputs = setup_inputs


def setup_inputs(seed=0):
    import zlib

    import numpy as np

    out = dict(_drawn_inputs(seed))
    spreads = {}
    factors = {}
    for name, (base, spread) in spreads.items():
        noise = np.random.default_rng([zlib.crc32(name.encode()), seed]).standard_normal(out[name].shape)
        drawn = base * np.exp(spread * noise) if base else spread * noise
        out[name] = jnp.asarray(drawn.astype(out[name].dtype))
    for name, factor in factors.items():
        out[name] = (out[name] * factor).astype(out[name].dtype)
    return out
```

```python
from contextlib import ExitStack

import numpy as np

import concourse.bass as bass
from concourse import mybir

F32 = mybir.dt.float32
F32R = mybir.dt.float32r
I32 = mybir.dt.int32
ALU = mybir.AluOpType
ACT = mybir.ActivationFunctionType
AX = mybir.AxisListType

P = 128
D = 1024
KT = D // P
TT = 2
S = TT * P
DFF = 2816
EPS = 1e-6
FC = 256
STEPS = DFF // FC
SLOTS = 3
UNIT = 2048

NH, KVH, DH = 16, 2, 64
GQ = NH // KVH
QC, QKVC = NH * DH, (NH + 2 * KVH) * DH
ROT = DH // 4
HALF = ROT // 2
NEG = -1e30

GH, GD = 8, 128
HG = 4
NG = GH // HG
TAPS = 4
CT = 3 * GH
LEVELS = 7

STAGES = ["ffn", "swa", "ffn", "ffn", "gdn", "ffn"]
UNITS = {"ffn": 3 * STEPS, "swa": 9, "gdn": 21}
INPUTS = {"ffn": 1, "swa": 2, "gdn": 2}
UBASE = [sum(UNITS[s] for s in STAGES[:n]) for n in range(len(STAGES) + 1)]
TBASE = [sum(INPUTS[s] for s in STAGES[:n]) for n in range(len(STAGES) + 1)]
TOTAL = UBASE[-1]
FFN_OF = {n: i for i, n in enumerate(n for n, s in enumerate(STAGES) if s == "ffn")}
PRE_GAIN = [0, 2, 4, 6, 8, 10]
COEF = [0.5, 1.0, 0.5, 0.5, 1.0, 0.5]

CHUNKS = {1: (1024, "k"), 2: (1536, "k"), 3: (0, "q"), 4: (512, "q"), 5: (2048, "v"), 6: (2560, "v"),
          7: (3072, "z"), 8: (3584, "z")}
PROJ_UNITS = 17
TWO_PI = 2 * np.pi
PI_BELOW = 3.1415925


def build(nc, x, positions, l0_norms, l0_ffn_w_in, l0_ffn_w_out, a_w_in, a_b_in, a_sinks, a_w_out,
          l1_norms, l1_ffn_w_in, l1_ffn_w_out, b_w_in, b_conv_w, b_A_log, b_dt_bias, b_norm, b_w_out,
          out, limit=len(STAGES)):
    stages = STAGES[:limit]
    total = UBASE[limit]
    with ExitStack() as ctx:
        def sb(name, shape, dt=F32):
            return ctx.enter_context(nc.sbuf_tensor(name, shape, dt))

        def sem(name):
            return ctx.enter_context(nc.semaphore(name))

        raw = sb("w_raw", [P, SLOTS, UNIT])
        whi = sb("w_high", [P, SLOTS, UNIT], F32R)
        wlo = sb("w_low", [P, SLOTS, UNIT], F32R)
        xh = sb("xT_high", [P, KT, S], F32R)
        xl = sb("xT_low", [P, KT, S], F32R)
        hTh = sb("hT_high", [P, 2, S], F32R)
        hTl = sb("hT_low", [P, 2, S], F32R)
        xs = sb("x_rows", [P, TT, D])
        xg = sb("x_gained", [P, TT, D])
        junk = sb("squares", [P, TT, D])
        gain = sb("gain_rows", [P, 2, D])
        arena = sb("mixer_arena", [P, 8 * 2048 + 1024])
        ident = sb("ident", [P, P])
        ones = sb("ones", [P, P])
        xss = sb("x_sumsq", [P, TT])
        yss = sb("y_sumsq", [P, TT])
        rstd = sb("rstd", [P, TT])
        yrs = sb("y_scale", [P, TT])
        pwv = sb("pow_base", [P, 2 * GH])
        mhalf = sb("minus_half", [P, 2 * GH])
        cs = sb("cos_rows", [P, TT, HALF])
        sn = sb("sin_rows", [P, TT, HALF])
        posi = sb("pos_int", [P, TT], I32)
        sink = sb("sinks", [P, NH])
        nsink = sb("minus_sinks", [P, NH])
        nm = sb("minus_rowmax", [P, TT, NH])
        rl = sb("row_sums", [P, TT, NH])
        es = sb("exp_sink", [P, TT, NH])
        cumU = sb("upper_ones", [P, P])
        negL = sb("mask_future", [P, P])
        lvl = sb("level_masks", [P, LEVELS, P])
        cw = sb("conv_w", [P, TAPS * CT])
        nrm = sb("gdn_norm", [P, GD])
        alog = sb("a_log", [P, GH])
        dtb = sb("dt_bias", [P, GH])
        small = sb("gdn_small", [P, 20, TT, GH])

        PS = ctx.enter_context(nc.psum_tensor("banks", [P, 8, 512], F32))

        def view(at, *shape):
            n = int(np.prod(shape))
            v = arena[:, at:at + n]
            if len(shape) == 2:
                v = v.rearrange("p (a b) -> p a b", a=shape[0])
            if len(shape) == 3:
                v = v.rearrange("p (a b c) -> p a b c", a=shape[0], b=shape[1])
            return v

        sg = view(14336, TT, FC)
        gated = view(14336 + 512, TT, FC)
        tmp = view(16384, 2, 512)
        qkv = view(0, TT, QKVC)
        kdup = view(2560, TT, 2 * P)
        kT = view(3072, KVH, S)
        qT = view(3584, NH // 2, S)
        sc = view(5632, 2, 384)
        pr = view(6400, 3, 384)
        pT = view(7552, 2, 384)
        bias = view(8320, QKVC)
        smask = view(9600, 384)
        rope = view(9984, 4, GQ * HALF)
        ang = view(10496, 4, TT * HALF)
        cwr = view(10752, P)
        gqT = view(0, GH, S)
        vb = view(2048, TT, D)
        khat = view(4096, TT, D)
        kb = view(6144, TT, D)
        Wm = view(6144, 2 * GH, P)
        khT = view(8192, GH, S)
        Tm = view(8192, 2 * GH, P)
        kbT = view(10240, GH, S)
        zs = view(12288, TT, D)
        stage = view(14336, TT, 512)
        Dm = view(14336, 2, 512)
        cacc = view(15360, 4, S)
        NM = view(15360, 2, 512)
        rT = view(16384, 4, S)
        R1 = view(16384, 2, 512)
        vn1v = [view(8192 + 512 * hg, 512) for hg in range(NG)]
        a1v = [view(9216 + 512 * hg, 512) for hg in range(NG)]
        kbTv = view(10240, TT, D)
        ov = [khat[:, 0, :], vb[:, 0, :]]
        Nm = xg[:, :, :].rearrange("p t d -> p (t d)").rearrange("p (b n) -> p b n", b=4)
        PTm = junk[:, :, :].rearrange("p t d -> p (t d)").rearrange("p (b n) -> p b n", b=4)

        x_in, const_in, out_done = sem("x_in"), sem("const_in"), sem("out_done")
        raw_in = [sem(f"raw_in{s}") for s in range(SLOTS)]
        gain_in = [sem(f"gain_in{s}") for s in range(2)]
        w_hi, w_lo, w_used = sem("w_hi"), sem("w_lo"), sem("w_used")
        masks = sem("masks_built")
        xg_ready, xT_ps, xT_hi, xT_lo = sem("xg_ready"), sem("xT_psum"), sem("xT_hi"), sem("xT_lo")
        xsq, rstd_ready = sem("x_squared"), sem("rstd_ready")
        y_ready, ysq, yrs_ready, x_new = sem("y_ready"), sem("y_squared"), sem("y_scale_ready"), sem("x_new")
        h_ready, silu_done, g_done = sem("h_ready"), sem("silu_done"), sem("gated_done")
        hT_ps, hT_hi, hT_lo = sem("hT_psum"), sem("hT_hi"), sem("hT_lo")
        dve_own, pool_own, act_own = sem("dve_own"), sem("pool_own"), sem("act_own")
        trig, dve_trig, cw_ps, cw_done = sem("trig"), sem("angles"), sem("conv_w_psum"), sem("conv_w")
        sp_ready, qkv_ready, rope_ready = sem("swa_proj"), sem("qkv_ready"), sem("rope_ready")
        sT_ps, sT_done = sem("qkT_psum"), sem("qkT_done")
        s_ready, s_masked, p_ready = sem("scores_ready"), sem("scores_masked"), sem("probs_ready")
        pT_ps, pT_done, pv_done = sem("probsT_psum"), sem("probsT_done"), sem("pv_done")
        snk_in, es_done, den_done = sem("sink_arg"), sem("exp_sink_done"), sem("den_done")
        ba_rows = sem("ba_rows")
        gate_arg, gate_exp, gate_u, gate_ln, g_ready, beta_ready = (
            sem("gate_arg"), sem("gate_exp"), sem("gate_u"), sem("gate_ln"), sem("g_ready"), sem("beta_ready"))
        gc_ps, gc_done, gdl, eg_done, ekd_done = (
            sem("gcum_psum"), sem("gcum_done"), sem("decay_left"), sem("exp_g"), sem("exp_left"))
        ch_ready, ch_evac, fT_ready = sem("chunk_ready"), sem("chunk_rows"), sem("chunkT_ready")
        tap_done, conv_step, conv_done, chan_done = (
            sem("tap_done"), sem("conv_step"), sem("conv_done"), sem("channels_done"))
        qsq_done, bT_ready, ksq, kss_done, rk_done, kh_done, kb_done = (
            sem("q_squared"), sem("rows_psum"), sem("k_squared"), sem("k_sumsq"), sem("k_scale"), sem("k_hat"),
            sem("k_beta"))
        qss_done, rq_done, v_done, z_done, zn_done, kd_done = (
            sem("q_sumsq"), sem("q_scale"), sem("v_beta"), sem("z_silu"), sem("z_normed"), sem("k_decayed"))
        kT_ps, kT_done = sem("kT_psum"), sem("kT_done")
        d_ps, d_exp, n_ps, np_done = sem("decay_psum"), sem("decay_exp"), sem("kk_kq_psum"), sem("n_p_done")
        nm_ready, w0_done, t0_ps, t0_done = sem("masked_n"), sem("w_init"), sem("t_init_psum"), sem("t_init")
        y_ps, y_cp, wt_ps, wt_done = sem("y_psum"), sem("y_copied"), sem("wt_psum"), sem("wt_updated")
        c3 = {k: sem("c3_" + k) for k in ("vn0p", "vn0", "o0p", "o0", "s1p", "s1", "zp", "r1", "ap", "a1",
                                         "vn1p", "vn1", "bp", "o1")}
        osq, oss_done, ro_done = sem("o_squared"), sem("o_sumsq"), sem("o_scale")

        def own(eng, s):
            n = [0]

            def link(ins, wait=True):
                n[0] += 1
                ins.then_inc(s, 1)
                if wait:
                    eng.wait_ge(s, n[0])
                return n[0]
            return link

        def tile_done(eng, t, first, n, used):
            if t == 0:
                eng.wait_ge(first, n)
            else:
                eng.wait_ge(w_used, used)

        def bc(ap, n):
            return ap.unsqueeze(2).to_broadcast([P, ap.shape[1], n])

        def rows(ap, n):
            return ap.unsqueeze(1).to_broadcast([P, n, ap.shape[1]])

        def heads(ap, n=HG):
            return ap.rearrange("p (h d) -> p h d", h=n)

        block = ctx.enter_context(nc.Block())

        @block.sync
        def _(sp):
            def slot(u, c, halves):
                if not (isinstance(u, int) and u < SLOTS):
                    sp.wait_ge(w_lo, u - SLOTS + 1)
                for dst, src in halves(raw[:, c % SLOTS, :]):
                    sp.dma_start(dst, src).then_inc(raw_in[c % SLOTS], 16)

            def up(w, j, k0):
                v = w.rearrange("(k p) (s n) -> p k s n", p=P, s=2)
                at = bass.ds(j * FC, FC)
                return lambda r: [(r.rearrange("p (k s n) -> p k s n", k=4, s=2)[:, :, s, :], v[:, k0:k0 + 4, s, at])
                                  for s in range(2)]

            def down(w, r0):
                return lambda r: [(r[:, k * D:(k + 1) * D], w[bass.ds(r0 + k * P, P), :]) for k in range(2)]

            def block(w, k0, nk, c0, nc_):
                v = w.rearrange("(k p) n -> p k n", p=P)
                h = nk // 2
                return lambda r: [(r[:, q * h * nc_:(q + 1) * h * nc_].rearrange("p (k n) -> p k n", k=h),
                                   v[:, k0 + q * h:k0 + (q + 1) * h, c0:c0 + nc_]) for q in range(2)]

            def ffn(base, wi, wo):
                slot(base, 0, up(wi, 0, 0))
                slot(base + 1, 1, up(wi, 0, 4))
                with sp.Fori(1, STEPS) as j:
                    slot(base + j * 3 - 1, 2, up(wi, j, 0))
                    slot(base + j * 3, 0, up(wi, j, 4))
                    slot(base + j * 3 + 1, 1, down(wo, j * FC - FC))
                slot(base + 3 * STEPS - 1, 2, down(wo, (STEPS - 1) * FC))

            for n, kind in enumerate(stages):
                base = UBASE[n]
                if kind == "ffn":
                    wi, wo = (l0_ffn_w_in, l0_ffn_w_out) if n < 3 else (l1_ffn_w_in, l1_ffn_w_out)
                    ffn(base, wi[0 if n % 3 == 0 else 1], wo[0 if n % 3 == 0 else 1])
                elif kind == "swa":
                    units = [block(a_w_in, 0, KT, QC, QKVC - QC)]
                    units += [block(a_w_in, 4 * h, 4, c * 512, 512) for c in range(2) for h in range(2)]
                    units += [down(a_w_out, 256 * i) for i in range(4)]
                    for c, u in enumerate(units):
                        slot(base + c, c, u)
                else:
                    units = [block(b_w_in, 0, KT, 4 * D, 2 * GH)]
                    units += [block(b_w_in, 4 * h, 4, CHUNKS[c][0], 512) for c in CHUNKS for h in range(2)]
                    units += [down(b_w_out, 256 * i) for i in range(4)]
                    for c, u in enumerate(units):
                        slot(base + c, c, u)
            for t in range(TT):
                sp.wait_ge(x_new, TT * (len(stages) - 1) + t + 1)
                sp.dma_start(out[0, t * P:(t + 1) * P, :], xs[:, t, :]).then_inc(out_done, 16)
            sp.wait_ge(out_done, 16 * TT)

        @block.gpsimd
        def _(pool):
            link = own(pool, pool_own)

            def gain_load(g):
                src = (l0_norms if g < 6 else l1_norms)[g % 6]
                pool.dma_start(gain[:, g % 2, :], src.partition_broadcast(P)).then_inc(gain_in[g % 2], 16)

            def select(v, op, fill, base, pattern, mult):
                link(pool.affine_select(out=v, in_=v, compare_op=op, fill=fill, base=base, pattern=pattern,
                                        channel_multiplier=mult))

            gain_load(0)
            gain_load(1)
            pool.memset(mhalf[:], -0.5)
            pool.memset(ones[:], 1.0)
            link(pool.memset(ident[:], 0.0))
            select(ident[:], ALU.not_equal, 1.0, 0, [[-1, P]], 1)
            link(pool.memset(smask[:], 0.0))
            for c0 in (0, 256):
                select(smask[:, c0:c0 + P], ALU.is_ge, NEG, 0, [[-1, P]], 1)
            select(smask[:, P:2 * P], ALU.is_gt, NEG, 0, [[1, P]], -1)
            link(pool.memset(cumU[:], 1.0))
            select(cumU[:], ALU.is_ge, 0.0, 0, [[1, P]], -1)
            link(pool.memset(negL[:], 0.0))
            select(negL[:], ALU.is_ge, NEG, 0, [[1, P]], -1)
            link(pool.memset(lvl[:], 0.0))
            for i in range(LEVELS):
                b = 1 << i
                nb = P // (2 * b)
                v = lvl[:, i, :].rearrange("p (B h r) -> p B h r", h=2, r=b)[:, :, 1, :]
                link(pool.memset(v, 1.0))
                select(v, ALU.is_ge, 0.0, 0, [[-2 * b, nb], [0, b]], 1)
                select(v, ALU.is_ge, 0.0, b - 1, [[2 * b, nb], [0, b]], -1)
            freq = (500000.0 ** (-np.arange(0, ROT, 2, dtype=np.float32) / ROT)).astype(np.float32)
            for i in range(HALF):
                last = pool.memset(es[:, 0, i:i + 1], float(freq[i]))
            last.then_inc(masks, 1)

            def power(out, src, scale, shift, n, final=None):
                v = pwv[:, 0:n]
                link(pool.tensor_scalar(v, src, scale, shift, ALU.mult, ALU.add))
                ins = pool.tensor_tensor(out if final is None else v, v, mhalf[:, 0:n], ALU.pow)
                if final is not None:
                    link(ins)
                    ins = pool.tensor_scalar(out, v, final, None, ALU.mult)
                return ins

            def rope_group(t, c0, nh):
                v = qkv[:, t, c0:c0 + nh * DH].rearrange("p (h d) -> p h d", h=nh)
                x1, x2 = v[:, :, 0:HALF], v[:, :, HALF:ROT]
                tm = [rope[:, i, 0:nh * HALF].rearrange("p (h d) -> p h d", h=nh) for i in range(4)]
                c, s = rows(cs[:, t, :], nh), rows(sn[:, t, :], nh)
                pool.tensor_tensor(tm[0], x1, c, ALU.mult)
                pool.tensor_tensor(tm[1], x2, s, ALU.mult)
                pool.tensor_tensor(tm[2], x2, c, ALU.mult)
                link(pool.tensor_tensor(tm[3], x1, s, ALU.mult))
                pool.tensor_tensor(x1, tm[0], tm[1], ALU.subtract)
                return pool.tensor_tensor(x2, tm[2], tm[3], ALU.add)

            def swa():
                pool.wait_ge(trig, 1)
                for g, (c0, nh) in enumerate([(QC, KVH), (0, GQ), (512, GQ)]):
                    for t in range(TT):
                        pool.wait_ge(qkv_ready, 2 * g + t + 1)
                        ins = rope_group(t, c0, nh)
                        if g == 0:
                            link(ins)
                            src = qkv[:, t, QC:QC + P].rearrange("p (k d) -> p k d", k=KVH)
                            for dup in range(2):
                                dst = kdup[:, t, :].rearrange("p (k u d) -> p k u d", k=KVH, u=2)[:, :, dup, :]
                                ins = pool.tensor_copy(dst, src)
                                if dup == 0:
                                    link(ins)
                        ins.then_inc(rope_ready, 1)
                        pool.wait_ge(rope_ready, 2 * g + t + 1)
                pool.wait_ge(s_masked, 2 * NH)
                pool.tensor_tensor(es[:, :, :], nm[:, :, :], rows(sink[:], TT), ALU.add).then_inc(snk_in, 1)
                pool.wait_ge(es_done, 1)
                pool.tensor_tensor(rl[:, :, :], rl[:, :, :], es[:, :, :], ALU.add).then_inc(den_done, 1)

            sm = [small[:, i, :, :] for i in range(20)]

            def fl(i):
                return small[:, i, :, :].rearrange("p t h -> p (t h)")

            def gdn():
                b_, a_ = sm[0], sm[1]
                pool.wait_ge(ba_rows, 2)
                link(pool.tensor_tensor(a_, a_, rows(dtb[:], TT), ALU.add))
                link(pool.tensor_scalar(sm[2], a_, 0.0, -2.0, ALU.max, ALU.mult))
                pool.tensor_tensor(sm[2], a_, sm[2], ALU.add).then_inc(gate_arg, 1)
                pool.wait_ge(gate_exp, 3)
                link(pool.tensor_scalar(sm[4], sm[4], 1.0, None, ALU.add))
                pool.tensor_scalar(sm[5], sm[3], 1.0, None, ALU.add).then_inc(gate_u, 1)
                pool.wait_ge(gate_u, 1)
                link(pool.tensor_scalar(sm[6], sm[5], -1.0, None, ALU.add))
                link(pool.tensor_tensor(sm[6], sm[3], sm[6], ALU.subtract))
                link(pool.tensor_scalar(a_, a_, 0.0, None, ALU.max))
                link(pool.tensor_tensor(a_, a_, sm[6], ALU.add))
                pool.wait_ge(gate_ln, 1)
                link(pool.tensor_tensor(a_, a_, sm[7], ALU.add))
                link(pool.tensor_tensor(a_, a_, rows(alog[:], TT), ALU.mult))
                pool.tensor_scalar(sm[8], a_, -1.0, None, ALU.mult).then_inc(g_ready, 1)
                pool.wait_ge(gc_done, 2)
                pool.tensor_tensor(sm[10], sm[10], sm[9], ALU.subtract).then_inc(gdl, 1)
                pool.wait_ge(gdl, 1)
                pool.tensor_scalar(sm[13], sm[9], -1.0, None, ALU.mult).then_inc(gdl, 1)
                for c in range(1, 7):
                    hg = (CHUNKS[c][0] % D) // 512
                    hs = slice(hg * HG, hg * HG + HG)
                    if CHUNKS[c][1] == "k":
                        pool.wait_ge(kss_done, 2 * c)
                        for t in range(TT):
                            power(small[:, 15, t, hs], small[:, 14, t, hs], 1.0, EPS, HG).then_inc(rk_done, 1)
                            pool.wait_ge(rk_done, 2 * (c - 1) + t + 1)
                        for t in range(TT):
                            pool.wait_ge(kh_done, 2 * (c - 1) + t + 1)
                            pool.wait_ge(beta_ready, 1)
                            cols = slice(hg * 512, hg * 512 + 512)
                            pool.tensor_tensor(heads(kb[:, t, cols]), heads(khat[:, t, cols]),
                                               bc(small[:, 12, t, hs], GD), ALU.mult).then_inc(kb_done, 1)
                    elif CHUNKS[c][1] == "q":
                        for i in range(4):
                            pool.wait_ge(chan_done, 4 * (c - 1) + i + 1)
                            pool.tensor_tensor(rT[:, i, :], gqT[:, hg * HG + i, :], gqT[:, hg * HG + i, :],
                                               ALU.mult).then_inc(qsq_done, 1)
                        pool.wait_ge(qss_done, c - 2)
                        for t in range(TT):
                            power(small[:, 17, t, hs], small[:, 16, t, hs], 1.0, EPS, HG,
                                  GD ** -0.5).then_inc(rq_done, 1)
                            pool.wait_ge(rq_done, 2 * (c - 3) + t + 1)
                pool.wait_ge(z_done, 4)
                for t in range(TT):
                    pool.tensor_tensor(heads(zs[:, t, :], GH), heads(zs[:, t, :], GH), rows(nrm[:], GH),
                                       ALU.mult).then_inc(zn_done, 1)
                pool.wait_ge(kT_ps, 8)
                pool.wait_ge(ekd_done, 1)
                pool.tensor_tensor(heads(khat[:, 1, :], GH), heads(khat[:, 0, :], GH),
                                   bc(small[:, 10, 0, :], GD), ALU.mult).then_inc(kd_done, 1)
                for q in range(4 * LEVELS):
                    level, b = divmod(q, 4)
                    if level == 0:
                        pool.wait_ge(np_done, 2 * (b + 1))
                    if q == 0:
                        pool.wait_ge(chan_done, 24)
                    elif 2 <= q < 6:
                        pool.wait_ge(w0_done, q - 1)
                    elif q >= 6:
                        pool.wait_ge(y_ps, q - 5)
                    pool.tensor_tensor(heads(NM[:, q % 2, :]), heads(Nm[:, b, :]), rows(lvl[:, level, :], HG),
                                       ALU.mult).then_inc(nm_ready, 1)
                for t in range(TT):
                    pool.wait_ge(oss_done, t + 1)
                    power(small[:, 19, t, :], small[:, 18, t, :], 1.0 / GD, EPS, GH).then_inc(ro_done, 1)
                    pool.wait_ge(ro_done, t + 1)

            for n, kind in enumerate(stages):
                pool.wait_ge(xsq, TT * (n + 1))
                power(rstd[:], xss[:], 1.0 / D, EPS, TT).then_inc(rstd_ready, 1)
                pool.wait_ge(rstd_ready, n + 1)
                if n:
                    pool.wait_ge(x_new, TT * n)
                    gain_load(2 * n + 1)
                if n + 1 < len(stages):
                    pool.wait_ge(xg_ready, 4 * TBASE[n] + 4)
                    gain_load(2 * n + 2)
                if kind == "swa":
                    swa()
                if kind == "gdn":
                    gdn()
                for t in range(TT):
                    pool.wait_ge(ysq, TT * n + t + 1)
                    power(yrs[:, t:t + 1], yss[:, t:t + 1], 1.0 / D, EPS, 1, COEF[n]).then_inc(yrs_ready, 1)
                    pool.wait_ge(yrs_ready, TT * n + t + 1)

        @block.scalar
        def _(act):
            for t in range(TT):
                act.dma_start(xs[:, t, :], x[0, t * P:(t + 1) * P, :]).then_inc(x_in, 16)
            act.dma_start(posi[:], positions.rearrange("a (t p) -> p (a t)", p=P),
                          allow_slow_non_contiguous=True).then_inc(const_in, 16)
            act.dma_start(bias, a_b_in.partition_broadcast(P)).then_inc(const_in, 16)
            act.dma_start(sink[:], a_sinks.partition_broadcast(P)).then_inc(const_in, 16)
            act.dma_start(alog[:], b_A_log.partition_broadcast(P)).then_inc(const_in, 16)
            act.dma_start(dtb[:], b_dt_bias.partition_broadcast(P)).then_inc(const_in, 16)
            act.dma_start(nrm[:], b_norm.partition_broadcast(P)).then_inc(const_in, 16)
            act.dma_start(cwr[0:TAPS * CT, :], b_conv_w.rearrange("t (c p) -> (t c) p", p=P)).then_inc(const_in, 16)

            def hi(u, c, n=UNIT):
                if isinstance(u, int) and u >= total:
                    return
                third = (u - c % 3) // 3 if isinstance(u, int) else None
                act.wait_ge(raw_in[c % 3], 32 * (third + 1))
                if u >= SLOTS:
                    act.wait_ge(w_used, u - SLOTS + 1)
                act.activation(whi[:, c % 3, 0:n], raw[:, c % 3, 0:n], ACT.Copy).then_inc(w_hi, 1)

            def hi_loop(base, j, c):
                act.wait_ge(raw_in[c % 3], j * 32 + 32 * (base // 3 + c // 3 + 1))
                act.wait_ge(w_used, j * 3 + (base + c - SLOTS + 1))
                act.activation(whi[:, c % 3, :], raw[:, c % 3, :], ACT.Copy).then_inc(w_hi, 1)

            def turned(ti):
                for m in range(4):
                    t, h = divmod(m, 2)
                    act.wait_ge(xT_ps, 4 * ti + m + 1)
                    act.activation(xh[:, 4 * h:4 * h + 4, t * P:(t + 1) * P], heads(PS[:, 6 + h, :]),
                                   ACT.Copy).then_inc(xT_hi, 1)

            def square_y(n):
                for t in range(TT):
                    tile_done(act, t, y_ready, n + 1, UBASE[n + 1])
                    act.wait_ge(xsq, TT * n + t + 1)
                    act.activation(junk[:, t, :].rearrange("p (a b) -> p a b", a=2), PS[:, 2 * t:2 * t + 2, :],
                                   ACT.Square, accum_out=yss[:, t:t + 1]).then_inc(ysq, 1)

            def square_x(n):
                for t in range(TT):
                    if n:
                        act.wait_ge(x_new, TT * (n - 1) + t + 1)
                        act.wait_ge(ysq, TT * (n - 1) + t + 1)
                    else:
                        act.wait_ge(x_in, 16 * TT)
                    act.activation(junk[:, t, :], xs[:, t, :], ACT.Square,
                                   accum_out=xss[:, t:t + 1]).then_inc(xsq, 1)

            def enter(n):
                if n:
                    square_y(n - 1)
                turned(TBASE[n])
                hi(UBASE[n] + 2, 2)
                square_x(n)

            def ffn(n):
                f, base = FFN_OF[n], UBASE[n]

                def silu(j):
                    for t in range(TT):
                        if t == 0:
                            act.wait_ge(h_ready, j + (STEPS * f + 1))
                        elif isinstance(j, int):
                            act.wait_ge(w_used, base + (3 * j + 1 if j else 2))
                        else:
                            act.wait_ge(w_used, j * 3 + (base + 1))
                        act.activation(sg[:, t, :], PS[:, 4 + t, 0:FC], ACT.Silu,
                                       scale=rstd[:, t:t + 1]).then_inc(silu_done, 1)

                def turn(j):
                    act.wait_ge(hT_ps, j + (STEPS * f + 1))
                    act.activation(hTh[:, :, :].rearrange("p k s -> p (k s)"), PS[:, 6, :],
                                   ACT.Copy).then_inc(hT_hi, 1)

                hi(base + 3, 3)
                act.wait_ge(rstd_ready, n + 1)
                silu(0)
                hi(base + 4, 4)
                with act.Fori(1, STEPS - 1) as j:
                    turn(j - 1)
                    hi_loop(base, j, 2)
                    silu(j)
                    hi_loop(base, j, 3)
                    hi_loop(base, j, 4)
                j = STEPS - 1
                turn(j - 1)
                hi(base + 3 * j + 2, 2)
                silu(j)
                hi(base + 3 * j + 3, 3)
                hi(base + 3 * j + 4, 4)
                turn(j)

            def swa(n):
                base = UBASE[n]
                hi(base + 3, 3)
                hi(base + 4, 4)
                hi(base + 5, 5)
                hi(base + 6, 6)

                def turn(e):
                    act.wait_ge(sT_ps, e + 1)
                    if e == 0:
                        act.activation(kT.rearrange("p k s -> p (k s)"), PS[:, 6, :], ACT.Copy).then_inc(sT_done, 1)
                    else:
                        act.activation(qT[:, 2 * e - 2:2 * e, :].rearrange("p k s -> p (k s)"),
                                       PS[:, 6 + e % 2, :], ACT.Copy).then_inc(sT_done, 1)
                turn(0)
                hi(base + 7, 7)
                turn(1)
                turn(2)
                for h in range(NH):
                    if h == 2:
                        turn(3)
                        turn(4)
                    act.wait_ge(s_masked, 2 * h + 2)
                    if h >= 3:
                        act.wait_ge(pT_ps, h - 2)
                    act.activation(pr[:, h % 3, 0:P], sc[:, h % 2, 0:P], ACT.Exp, scale=-1.0,
                                   bias=nm[:, 0, h:h + 1], accum_out=rl[:, 0, h:h + 1])
                    act.activation(pr[:, h % 3, P:384], sc[:, h % 2, P:384], ACT.Exp, scale=-1.0,
                                   bias=nm[:, 1, h:h + 1], accum_out=rl[:, 1, h:h + 1]).then_inc(p_ready, 1)
                act.wait_ge(snk_in, 1)
                act.activation(es[:, :, :], es[:, :, :], ACT.Exp).then_inc(es_done, 1)
                turned(TBASE[n] + 1)
                for c in range(8, 11):
                    hi(base + c, c)

            def gdn(n):
                base = UBASE[n]

                def f(i):
                    return small[:, i, :, :]
                hi(base + 3, 3)
                act.wait_ge(rstd_ready, n + 1)
                act.wait_ge(gate_arg, 1)
                act.activation(f(3), f(2), ACT.Exp).then_inc(gate_exp, 1)
                act.activation(f(4), f(0), ACT.Exp, scale=-1.0).then_inc(gate_exp, 1)
                act.wait_ge(const_in, 16 * 7)
                act.wait_ge(gate_exp, 2)
                act.activation(alog[:], alog[:], ACT.Exp).then_inc(gate_exp, 1)
                act.wait_ge(gate_u, 1)
                act.activation(f(7), f(5), ACT.Ln).then_inc(gate_ln, 1)
                for s in range(1, PROJ_UNITS):
                    c = s // 2
                    if s % 2 == 0 and c <= 6:
                        for t in range(TT):
                            tile_done(act, t, ch_ready, c, base + s + 1)
                            if c > 1:
                                act.wait_ge(fT_ready, 2 * (c - 1))
                            act.activation(stage[:, t, :], PS[:, (0 if c % 2 else 2) + t, :], ACT.Copy,
                                           scale=rstd[:, t:t + 1]).then_inc(ch_evac, 1)
                    elif s % 2 == 0:
                        for t in range(TT):
                            tile_done(act, t, ch_ready, c, base + s + 1)
                            act.activation(zs[:, t, (c - 7) * 512:(c - 6) * 512], PS[:, (0 if c % 2 else 2) + t, :],
                                           ACT.Silu, scale=rstd[:, t:t + 1]).then_inc(z_done, 1)
                    c = (s - 1) // 2
                    if s % 2 == 1 and 1 <= c <= 6:
                        for i in range(4):
                            act.wait_ge(fT_ready, 2 * (c - 1) + i // 2 + 1)
                            if c > 1:
                                act.wait_ge(chan_done, 4 * (c - 2) + i + 1)
                            tile = CHUNKS[c][0] // P + i
                            act.activation(cacc[:, i, :], PS[:, 6 + i // 2, (i % 2) * S:(i % 2 + 1) * S], ACT.Copy,
                                           scale=cw[:, 3 * CT + tile:3 * CT + tile + 1]).then_inc(tap_done, 1)
                    c = (s - 3) // 2
                    if s % 2 == 1 and c in (1, 2):
                        for t in range(TT):
                            act.wait_ge(bT_ready, 2 * (c - 1) + t + 1)
                            if c == 2:
                                act.wait_ge(kss_done, t + 1)
                            act.activation(junk[:, t, 0:512], PS[:, 4 + t, :], ACT.Square).then_inc(ksq, 1)
                    hi(base + s + 3, s + 3)
                    c = (s - 2) // 2
                    if s % 2 == 0 and 1 <= c <= 6:
                        kind, hg = CHUNKS[c][1], (CHUNKS[c][0] % D) // 512
                        for i in range(4):
                            act.wait_ge(conv_done, 4 * (c - 1) + i + 1)
                            if c > 1:
                                act.wait_ge(bT_ready, 2 * (c - 1))
                            dst = gqT[:, hg * HG + i, :] if kind == "q" else rT[:, i, :]
                            act.activation(dst, cacc[:, i, :], ACT.Silu).then_inc(chan_done, 1)
                    if s == 5:
                        act.wait_ge(gdl, 2)
                        act.activation(f(11), f(9), ACT.Exp).then_inc(eg_done, 1)
                        act.activation(f(10), f(10), ACT.Exp).then_inc(ekd_done, 1)
                for e in range(8):
                    hg, rest = divmod(e, 4)
                    what, t = divmod(rest, 2)
                    act.wait_ge(kT_ps, e + 1)
                    dst = (kbT if what else khT)[:, hg * HG:hg * HG + HG, t * P:(t + 1) * P]
                    act.activation(dst, heads(PS[:, 6 + e % 2, :]), ACT.Copy).then_inc(kT_done, 1)
                for b in range(4):
                    hg, t = divmod(b, 2)
                    act.wait_ge(d_ps, b + 1)
                    if b >= 2:
                        act.wait_ge(np_done, 2 * (b - 1))
                    for i in range(HG):
                        h = hg * HG + i
                        last = act.activation(Dm[:, b % 2, i * P:(i + 1) * P], PS[:, b % 2, i * P:(i + 1) * P],
                                              ACT.Exp, bias=small[:, 13, t, h:h + 1])
                    last.then_inc(d_exp, 1)
                for b in range(4):
                    act.wait_ge(t0_ps, b + 1)
                    act.activation(Tm[:, 4 * b:4 * b + 4, :], heads(PS[:, 6 + b % 2, :]), ACT.Copy).then_inc(t0_done, 1)
                for q in range(4 * (LEVELS - 1)):
                    act.wait_ge(y_ps, q + 1)
                    if q >= 2:
                        act.wait_ge(wt_ps, q - 1)
                    act.activation(Dm[:, q % 2, :], PS[:, q % 2, :], ACT.Copy).then_inc(y_cp, 1)
                for hg in range(NG):
                    act.wait_ge(c3["vn0p"], hg + 1)
                    act.activation(Dm[:, hg, :], PS[:, hg, :], ACT.Copy).then_inc(c3["vn0"], 1)
                for hg in range(NG):
                    act.wait_ge(c3["s1p"], hg + 1)
                    act.activation(NM[:, hg, :], PS[:, 4 + hg, :], ACT.Copy).then_inc(c3["s1"], 1)
                for hg in range(NG):
                    act.wait_ge(c3["vn1p"], hg + 1)
                    act.activation(vn1v[hg], PS[:, 2 + hg, :], ACT.Copy).then_inc(c3["vn1"], 1)
                for t in range(TT):
                    act.wait_ge(c3["o0"] if t == 0 else c3["o1"], NG)
                    act.activation(kbTv[:, t, :], ov[t], ACT.Square).then_inc(osq, 1)
                turned(TBASE[n] + 1)
                for c in range(20, 23):
                    hi(base + c, c)

            act.wait_ge(dve_trig, 1)
            act.activation(sn[:, :, :].rearrange("p t f -> p (t f)"), ang[:, 0, :], ACT.Sin)
            act.activation(cs[:, :, :].rearrange("p t f -> p (t f)"), ang[:, 1, :], ACT.Sin).then_inc(trig, 1)
            hi(0, 0)
            hi(1, 1)
            for n, kind in enumerate(stages):
                enter(n)
                (ffn if kind == "ffn" else swa if kind == "swa" else gdn)(n)
            square_y(len(stages) - 1)

        @block.tensor
        def _(pe):
            def mm3(dst, sh, sl, wh, wl, start, stop):
                pe.matmul(dst, sh, wh, start=start, stop=False)
                pe.matmul(dst, sh, wl, start=False, stop=False)
                return pe.matmul(dst, sl, wh, start=False, stop=stop)

            def turn_x(ti, m):
                t, h = divmod(m, 2)
                pe.wait_ge(xg_ready, 4 * ti + m + 1)
                if m >= 2:
                    pe.wait_ge(xT_lo, 4 * ti + m - 1)
                for k in range(4):
                    last = pe.transpose(PS[:, 6 + h, k * P:(k + 1) * P],
                                        xg[:, t, (4 * h + k) * P:(4 * h + k + 1) * P], ident[:])
                last.then_inc(xT_ps, 1)

            def wide(c, t, bank, ncol, nk, k0, start, stop):
                wh = whi[:, c % 3, 0:nk * ncol].rearrange("p (k n) -> p k n", k=nk)
                wl = wlo[:, c % 3, 0:nk * ncol].rearrange("p (k n) -> p k n", k=nk)
                for k in range(nk):
                    tok = slice(t * P, (t + 1) * P)
                    last = mm3(bank, xh[:, k0 + k, tok], xl[:, k0 + k, tok], wh[:, k, :], wl[:, k, :],
                               start and k == 0, stop and k == nk - 1)
                return last

            def down(c, t, sh, sl, start, stop):
                for k in range(2):
                    tok = slice(t * P, (t + 1) * P)
                    for h in range(2):
                        cols = slice(k * D + h * 512, k * D + h * 512 + 512)
                        pe.matmul(PS[:, 2 * t + h, :], sh[:, k, tok], whi[:, c % 3, cols],
                                  start=start and k == 0, stop=False)
                        pe.matmul(PS[:, 2 * t + h, :], sh[:, k, tok], wlo[:, c % 3, cols], start=False, stop=False)
                    for h in range(2):
                        cols = slice(k * D + h * 512, k * D + h * 512 + 512)
                        last = pe.matmul(PS[:, 2 * t + h, :], sl[:, k, tok], whi[:, c % 3, cols],
                                         start=False, stop=stop and k == 1)
                return last

            def ffn(n):
                f, base, ti = FFN_OF[n], UBASE[n], TBASE[n]

                def up(c, t, k0):
                    return wide(c, t, PS[:, 4 + t, :], 512, 4, k0, k0 == 0, k0 == 4)

                def turn(j):
                    pe.wait_ge(g_done, j * 2 + (2 * STEPS * f + 2))
                    for k in range(2):
                        for t in range(TT):
                            last = pe.transpose(PS[:, 6, k * S + t * P:k * S + (t + 1) * P],
                                                gated[:, t, k * P:(k + 1) * P], ident[:])
                    last.then_inc(hT_ps, 1)

                def step(j, first):
                    pe.wait_ge(w_lo, j * 3 + base)
                    pe.wait_ge(g_done, j * 2 + 2 * STEPS * f)
                    for t in range(TT):
                        last = up(2, t, 0)
                    last.then_inc(w_used, 1)
                    turn(j - 1)
                    pe.wait_ge(w_lo, j * 3 + (base + 1))
                    up(0, 0, 4).then_inc(h_ready, 1)
                    up(0, 1, 4).then_inc(w_used, 1)
                    pe.wait_ge(w_lo, j * 3 + (base + 2))
                    pe.wait_ge(hT_lo, j + STEPS * f)
                    for t in range(TT):
                        last = down(1, t, hTh, hTl, first, False)
                    last.then_inc(w_used, 1)

                turn_x(ti, 0)
                turn_x(ti, 1)
                pe.wait_ge(w_lo, base + 1)
                pe.wait_ge(xT_lo, 4 * ti + 1)
                up(0, 0, 0)
                turn_x(ti, 2)
                turn_x(ti, 3)
                pe.wait_ge(xT_lo, 4 * ti + 3)
                up(0, 1, 0).then_inc(w_used, 1)
                pe.wait_ge(w_lo, base + 2)
                up(1, 0, 4).then_inc(h_ready, 1)
                pe.wait_ge(xT_lo, 4 * ti + 4)
                up(1, 1, 4).then_inc(w_used, 1)
                step(1, True)
                with pe.Fori(2, STEPS) as j:
                    step(j, False)
                turn(STEPS - 1)
                pe.wait_ge(w_lo, base + 3 * STEPS)
                pe.wait_ge(hT_lo, STEPS * (f + 1))
                down(2, 0, hTh, hTl, False, True).then_inc(y_ready, 1)
                down(2, 1, hTh, hTl, False, True).then_inc(w_used, 1)

            def out_proj(n, c0):
                base, ti = UBASE[n], TBASE[n] + 1

                def part(i, t):
                    pe.wait_ge(xT_lo, 4 * ti + 2 * t + (1 if i < 2 else 2))
                    return down(c0 + i, t, xh[:, 2 * i:2 * i + 2, :], xl[:, 2 * i:2 * i + 2, :], i == 0, i == 3)

                pe.wait_ge(xg_ready, 4 * ti + 4)
                turn_x(ti, 0)
                turn_x(ti, 1)
                for i in range(4):
                    pe.wait_ge(w_lo, base + c0 + i + 1)
                    last = part(i, 0)
                    if i == 3:
                        last.then_inc(y_ready, 1)
                    if i == 0:
                        turn_x(ti, 2)
                        turn_x(ti, 3)
                    part(i, 1).then_inc(w_used, 1)

            def swa(n):
                base, ti = UBASE[n], TBASE[n]
                vcol = QC + P

                def turn_q(e):
                    for i in range(2):
                        for t in range(TT):
                            pair = 2 * e - 2 + i
                            last = pe.transpose(PS[:, 6 + e % 2, i * S + t * P:i * S + (t + 1) * P],
                                                qkv[:, t, pair * P:(pair + 1) * P], ident[:])
                    last.then_inc(sT_ps, 1)

                turn_x(ti, 0)
                turn_x(ti, 1)
                pe.wait_ge(w_lo, base + 1)
                pe.wait_ge(xT_lo, 4 * ti + 2)
                wide(0, 0, PS[:, 4, 0:2 * P], 2 * P, KT, 0, True, True).then_inc(sp_ready, 1)
                turn_x(ti, 2)
                turn_x(ti, 3)
                pe.wait_ge(xT_lo, 4 * ti + 4)
                wide(0, 1, PS[:, 5, 0:2 * P], 2 * P, KT, 0, True, True).then_inc(w_used, 1)
                for c in range(1, 5):
                    chunk, h = divmod(c - 1, 2)
                    pe.wait_ge(w_lo, base + c + 1)
                    last = wide(c, 0, PS[:, chunk, :], 512, 4, 4 * h, h == 0, h == 1)
                    if h:
                        last.then_inc(sp_ready, 1)
                    wide(c, 1, PS[:, 2 + chunk, :], 512, 4, 4 * h, h == 0, h == 1).then_inc(w_used, 1)
                    if c == 3:
                        pe.wait_ge(rope_ready, 2)
                        for kv in range(KVH):
                            for t in range(TT):
                                last = pe.transpose(PS[:, 6, kv * S + t * P:kv * S + (t + 1) * P],
                                                    kdup[:, t, kv * P:(kv + 1) * P], ident[:])
                        last.then_inc(sT_ps, 1)
                        pe.wait_ge(const_in, 16 * 7)
                        pe.transpose(PS[:, 7, 0:TAPS * CT], cwr[0:TAPS * CT, :],
                                     ident[0:TAPS * CT, 0:TAPS * CT]).then_inc(cw_ps, 1)
                pe.wait_ge(rope_ready, 4)
                pe.wait_ge(cw_done, 1)
                turn_q(1)
                pe.wait_ge(sT_done, 1)
                turn_q(2)
                for step in range(NH + 3):
                    if step == 2:
                        pe.wait_ge(rope_ready, 6)
                        pe.wait_ge(sT_done, 2)
                        turn_q(3)
                        pe.wait_ge(sT_done, 3)
                        turn_q(4)
                    h = step
                    if h < NH:
                        pair, po, kv = h // 2, (h % 2) * DH, h // GQ
                        pe.wait_ge(sT_done, 3 if h < GQ else 5)
                        if h < 2:
                            pe.wait_ge(qkv_ready, 6)
                        else:
                            pe.wait_ge(s_masked, 2 * (h - 1))
                        q, k = qT[po:po + DH, pair, :], kT[po:po + DH, kv, :]
                        pe.matmul(PS[:, h % 2, 0:P], q[:, 0:P], k[:, 0:P], start=True, stop=True)
                        pe.matmul(PS[:, h % 2, P:384], q[:, P:S], k, start=True, stop=True).then_inc(s_ready, 1)
                    g = step - 2
                    if 0 <= g < NH:
                        pe.wait_ge(p_ready, g + 1)
                        if g >= 2:
                            pe.wait_ge(pT_done, g - 1)
                        for i in range(3):
                            last = pe.transpose(PS[:, 2 + g % 2, i * P:(i + 1) * P], pr[:, g % 3, i * P:(i + 1) * P],
                                                ident[:])
                        last.then_inc(pT_ps, 1)
                    g = step - 3
                    if g >= 0:
                        pe.wait_ge(pT_done, g + 1)
                        if g == 0:
                            pe.wait_ge(sT_done, 5)
                        kv = g // GQ
                        v = slice(vcol + kv * DH, vcol + (kv + 1) * DH)
                        at = slice((g % GQ) * DH, (g % GQ + 1) * DH)
                        pe.matmul(PS[:, 4 + kv, at], pT[:, g % 2, 0:P], qkv[:, 0, v], start=True, stop=True)
                        pe.matmul(PS[:, 6 + kv, at], pT[:, g % 2, P:2 * P], qkv[:, 0, v], start=True, stop=False)
                        pe.matmul(PS[:, 6 + kv, at], pT[:, g % 2, 2 * P:384], qkv[:, 1, v],
                                  start=False, stop=True).then_inc(pv_done, 1)
                out_proj(n, 5)

            def gdn(n):
                base, ti = UBASE[n], TBASE[n]
                g_flat = small[:, 8, :, :].rearrange("p t h -> p (t h)")

                def col(i):
                    return slice(i * P, (i + 1) * P)

                def four(bank, lhs, rhs, start=True):
                    for i in range(HG):
                        last = pe.matmul(PS[:, bank, col(i)], lhs(i), rhs(i), start=start, stop=True)
                    return last

                def turn_chunk(c):
                    pe.wait_ge(ch_evac, 2 * c)
                    if c > 1:
                        pe.wait_ge(conv_done, 4 * (c - 1))
                    for i in range(4):
                        for t in range(TT):
                            at = (i % 2) * S + t * P
                            last = pe.transpose(PS[:, 6 + i // 2, at:at + P], stage[:, t, col(i)], ident[:])
                        if i % 2:
                            last.then_inc(fT_ready, 1)

                def turn_back(c):
                    pe.wait_ge(chan_done, 4 * c)
                    free = {1: (gc_done, 2), 2: (kh_done, 2), 3: (kh_done, 4), 4: (qss_done, 1), 5: (qss_done, 2),
                            6: (v_done, 2)}[c]
                    pe.wait_ge(*free)
                    if CHUNKS[c][1] == "q":
                        pe.wait_ge(qsq_done, 4 * (c - 2))
                        for t in range(TT):
                            for i in range(4):
                                last = pe.matmul(PS[:, 4, 4 * t + i:4 * t + i + 1], rT[:, i, t * P:(t + 1) * P],
                                                 ones[:, 0:1], start=True, stop=True)
                            last.then_inc(bT_ready, 1)
                    else:
                        for t in range(TT):
                            for i in range(4):
                                last = pe.transpose(PS[:, 4 + t, col(i)], rT[:, i, t * P:(t + 1) * P], ident[:])
                            last.then_inc(bT_ready, 1)

                def turn_k(e):
                    hg, rest = divmod(e, 4)
                    what, t = divmod(rest, 2)
                    pe.wait_ge(kb_done if what else kh_done, 2 * hg + t + 1)
                    if e < 2:
                        pe.wait_ge(conv_done, 24)
                    else:
                        pe.wait_ge(kT_done, e - 1)
                    src = kb if what else khat
                    for i in range(HG):
                        at = (hg * HG + i) * P
                        last = pe.transpose(PS[:, 6 + e % 2, col(i)], src[:, t, at:at + P], ident[:])
                    last.then_inc(kT_ps, 1)

                turn_x(ti, 0)
                turn_x(ti, 1)
                pe.wait_ge(w_lo, base + 1)
                pe.wait_ge(xT_lo, 4 * ti + 2)
                n2 = 2 * GH
                wide(0, 0, PS[:, 2, 0:n2], n2, KT, 0, True, True)
                turn_x(ti, 2)
                turn_x(ti, 3)
                pe.wait_ge(xT_lo, 4 * ti + 4)
                wide(0, 1, PS[:, 2, n2:2 * n2], n2, KT, 0, True, True).then_inc(w_used, 1)
                for s in range(1, PROJ_UNITS):
                    c, h = (s + 1) // 2, (s + 1) % 2
                    pe.wait_ge(w_lo, base + s + 1)
                    if h == 0 and c == 2:
                        pe.wait_ge(ba_rows, 2)
                    if h == 0 and c > 2:
                        pe.wait_ge(ch_evac, 2 * (c - 2))
                    bank = 0 if c % 2 else 2
                    last = wide(s, 0, PS[:, bank, :], 512, 4, 4 * h, h == 0, h == 1)
                    if h:
                        last.then_inc(ch_ready, 1)
                    wide(s, 1, PS[:, bank + 1, :], 512, 4, 4 * h, h == 0, h == 1).then_inc(w_used, 1)
                    if s == 4:
                        pe.wait_ge(g_ready, 1)
                        pe.matmul(PS[:, 4, 0:n2], cumU[:], g_flat, start=True, stop=True)
                        pe.matmul(PS[:, 4, n2:2 * n2], ones[:], g_flat, start=True, stop=True).then_inc(gc_ps, 1)
                    if s % 2 and 1 <= (s - 1) // 2 <= 6:
                        turn_chunk((s - 1) // 2)
                    if s % 2 and 1 <= (s - 3) // 2 <= 6:
                        turn_back((s - 3) // 2)
                    if s >= 15:
                        turn_k(2 * (s - 15))
                        turn_k(2 * (s - 15) + 1)
                for e in range(4, 8):
                    turn_k(e)
                pe.wait_ge(z_done, 4)
                pe.wait_ge(v_done, 4)
                for b in range(4):
                    hg, t = divmod(b, 2)
                    tok = slice(t * P, (t + 1) * P)
                    pe.wait_ge(kT_done, 4 * hg + 4)
                    if b >= 2:
                        pe.wait_ge(d_exp, b - 1)
                    pe.matmul(PS[:, b % 2, :], ident[:], rows(negL[:], HG), start=True, stop=False)
                    for i in range(HG):
                        h = hg * HG + i
                        last = pe.matmul(PS[:, b % 2, col(i)], small[:, 8, t, h:h + 1].to_broadcast([P, P]), cumU[:],
                                         start=False, stop=i == HG - 1)
                    last.then_inc(d_ps, 1)
                    if b >= 2:
                        pe.wait_ge(np_done, 2 * (b - 1))
                    four(2 + b % 2, lambda i: khT[:, hg * HG + i, tok], lambda i: kbT[:, hg * HG + i, tok]
                         ).then_inc(n_ps, 1)
                    four(4 + b % 2, lambda i: khT[:, hg * HG + i, tok], lambda i: gqT[:, hg * HG + i, tok]
                         ).then_inc(n_ps, 1)
                for b in range(4):
                    pe.wait_ge(w0_done, b + 1)
                    if b >= 2:
                        pe.wait_ge(t0_done, b - 1)
                    for i in range(HG):
                        last = pe.transpose(PS[:, 6 + b % 2, col(i)], Wm[:, 4 * b + i, :], ident[:])
                    last.then_inc(t0_ps, 1)
                nq = 4 * (LEVELS - 1)
                for q in range(nq + 1):
                    if q < nq:
                        b = q % 4
                        pe.wait_ge(nm_ready, q + 5)
                        if q < 4:
                            pe.wait_ge(t0_done, b + 1)
                        else:
                            pe.wait_ge(wt_done, q - 3)
                        if q < 2:
                            pe.wait_ge(d_exp, 4)
                        else:
                            pe.wait_ge(y_cp, q - 1)
                        four(q % 2, lambda i: NM[:, q % 2, col(i)], lambda i: Tm[:, 4 * b + i, :]).then_inc(y_ps, 1)
                    if q >= 1:
                        r = q - 1
                        b = r % 4
                        pe.wait_ge(y_cp, r + 1)
                        if r < 2:
                            pe.wait_ge(np_done, 8)
                        else:
                            pe.wait_ge(wt_done, r - 1)
                        last = four(2 + r % 2, lambda i: Dm[:, r % 2, col(i)], lambda i: Wm[:, 4 * b + i, :])
                        if r < nq - 4:
                            last = four(4 + r % 2, lambda i: Wm[:, 4 * b + i, :], lambda i: Dm[:, r % 2, col(i)])
                        last.then_inc(wt_ps, 1)
                pe.wait_ge(wt_done, nq)
                for hg in range(NG):
                    four(hg, lambda i: Wm[:, 8 * hg + i, :], lambda i: vb[:, 0, (hg * HG + i) * P:(hg * HG + i + 1) * P]
                         ).then_inc(c3["vn0p"], 1)
                pe.wait_ge(kd_done, 1)
                for hg in range(NG):
                    pe.wait_ge(c3["vn0"], hg + 1)
                    four(4 + hg, lambda i: khat[:, 1, (hg * HG + i) * P:(hg * HG + i + 1) * P],
                         lambda i: Dm[:, hg, col(i)]).then_inc(c3["s1p"], 1)
                for hg in range(NG):
                    four(2 + hg, lambda i: PTm[:, 2 * hg, col(i)], lambda i: Dm[:, hg, col(i)]).then_inc(c3["o0p"], 1)
                for hg in range(NG):
                    pe.wait_ge(c3["s1"], hg + 1)
                    four(6 + hg, lambda i: kbT[:, hg * HG + i, P:S], lambda i: NM[:, hg, col(i)]).then_inc(c3["zp"], 1)
                for hg in range(NG):
                    four(hg, lambda i: gqT[:, hg * HG + i, P:S], lambda i: NM[:, hg, col(i)]).then_inc(c3["ap"], 1)
                for hg in range(NG):
                    pe.wait_ge(c3["r1"], hg + 1)
                    pe.wait_ge(c3["o0"], hg + 1)
                    four(2 + hg, lambda i: Wm[:, 8 * hg + 4 + i, :], lambda i: R1[:, hg, col(i)]
                         ).then_inc(c3["vn1p"], 1)
                for hg in range(NG):
                    pe.wait_ge(c3["vn1"], hg + 1)
                    four(4 + hg, lambda i: PTm[:, 2 * hg + 1, col(i)], lambda i: vn1v[hg][:, col(i)]
                         ).then_inc(c3["bp"], 1)
                out_proj(n, PROJ_UNITS)

            pe.wait_ge(masks, 1)
            for n, kind in enumerate(stages):
                (ffn if kind == "ffn" else swa if kind == "swa" else gdn)(n)

        @block.vector
        def _(dve):
            link = own(dve, dve_own)

            def lo(u, c):
                if isinstance(u, int) and u >= total:
                    return
                dve.wait_ge(w_hi, u + 1)
                dve.tensor_tensor(wlo[:, c % 3, :], raw[:, c % 3, :], whi[:, c % 3, :], ALU.subtract).then_inc(w_lo, 1)

            def turned(ti, m):
                t, h = divmod(m, 2)
                dve.wait_ge(xT_hi, 4 * ti + m + 1)
                at = (slice(None), slice(4 * h, 4 * h + 4), slice(t * P, (t + 1) * P))
                dve.tensor_tensor(xl[at], heads(PS[:, 6 + h, :]), xh[at], ALU.subtract).then_inc(xT_lo, 1)

            def scaled(n, t):
                dve.wait_ge(yrs_ready, TT * n + t + 1)
                dve.wait_ge(gain_in[1], 16 * (n + 1))
                return [link(dve.scalar_tensor_tensor(out=tmp[:, h, :], in0=PS[:, 2 * t + h, :],
                                                      scalar=yrs[:, t:t + 1], in1=gain[:, 1, h * 512:h * 512 + 512],
                                                      op0=ALU.mult, op1=ALU.mult), wait=False) for h in range(2)]

            def added(n, t, steps):
                for h in range(2):
                    dve.wait_ge(dve_own, steps[h])
                    v = xs[:, t, h * 512:h * 512 + 512]
                    ins = dve.tensor_tensor(v, v, tmp[:, h, :], ALU.add)
                    if h:
                        ins.then_inc(x_new, 1)
                dve.wait_ge(x_new, TT * n + t + 1)

            def gained(n, t):
                dve.wait_ge(gain_in[0], 16 * (n + 1))
                for h in range(2):
                    cols = slice(h * 512, h * 512 + 512)
                    dve.tensor_tensor(xg[:, t, cols], xs[:, t, cols], gain[:, 0, cols], ALU.mult).then_inc(xg_ready, 1)

            def enter(n):
                ti = TBASE[n]
                if n:
                    added(n - 1, 0, scaled(n - 1, 0))
                else:
                    dve.wait_ge(x_in, 16 * TT)
                gained(n, 0)
                if n:
                    steps = scaled(n - 1, 1)
                turned(ti, 0)
                if n:
                    added(n - 1, 1, steps)
                turned(ti, 1)
                gained(n, 1)
                turned(ti, 2)
                turned(ti, 3)
                lo(UBASE[n] + 2, 2)

            def ffn(n):
                f, base = FFN_OF[n], UBASE[n]

                def mul(j):
                    for t in range(TT):
                        dve.wait_ge(silu_done, j * 2 + (2 * STEPS * f + t + 1))
                        dve.scalar_tensor_tensor(out=gated[:, t, :], in0=PS[:, 4 + t, FC:2 * FC],
                                                 scalar=rstd[:, t:t + 1], in1=sg[:, t, :],
                                                 op0=ALU.mult, op1=ALU.mult).then_inc(g_done, 1)

                def turn(j):
                    dve.wait_ge(hT_hi, j + (STEPS * f + 1))
                    flat = "p k s -> p (k s)"
                    dve.tensor_tensor(hTl[:, :, :].rearrange(flat), PS[:, 6, :], hTh[:, :, :].rearrange(flat),
                                      ALU.subtract).then_inc(hT_lo, 1)

                lo(base + 3, 3)
                mul(0)
                lo(base + 4, 4)
                with dve.Fori(1, STEPS - 1) as j:
                    turn(j - 1)
                    lo(j * 3 + (base + 2), 2)
                    mul(j)
                    lo(j * 3 + (base + 3), 3)
                    lo(j * 3 + (base + 4), 4)
                j = STEPS - 1
                turn(j - 1)
                lo(base + 3 * j + 2, 2)
                mul(j)
                lo(base + 3 * j + 3, 3)
                lo(base + 3 * j + 4, 4)
                turn(j)

            def swa(n):
                base = UBASE[n]
                scale = -DH ** -0.5

                def rows_out(g, bank, c0, nc_, used):
                    for t in range(TT):
                        tile_done(dve, t, sp_ready, g + 1, used)
                        dve.scalar_tensor_tensor(out=qkv[:, t, c0:c0 + nc_], in0=PS[:, bank(t), 0:nc_],
                                                 scalar=rstd[:, t:t + 1], in1=bias[:, c0:c0 + nc_],
                                                 op0=ALU.mult, op1=ALU.add).then_inc(qkv_ready, 1)

                dve.wait_ge(rstd_ready, n + 1)
                rows_out(0, lambda t: 4 + t, QC, QKVC - QC, base + 1)
                lo(base + 3, 3)
                lo(base + 4, 4)
                rows_out(1, lambda t: 2 * t, 0, 512, base + 3)
                lo(base + 5, 5)
                lo(base + 6, 6)
                dve.wait_ge(cw_ps, 1)
                dve.tensor_copy(cw[:], PS[:, 7, 0:TAPS * CT]).then_inc(cw_done, 1)
                rows_out(2, lambda t: 2 * t + 1, 512, 512, base + 5)
                lo(base + 7, 7)
                for step in range(NH + 2):
                    h = step
                    if h < NH:
                        dve.wait_ge(s_ready, h + 1)
                        if h >= 2:
                            dve.wait_ge(p_ready, h - 1)
                        for t, cols in enumerate((slice(0, P), slice(P, 384))):
                            dve.tensor_tensor_reduce(out=sc[:, h % 2, cols], in0=PS[:, h % 2, cols],
                                                     in1=smask[:, cols], scale=scale, scalar=nsink[:, h:h + 1],
                                                     op0=ALU.add, op1=ALU.min,
                                                     accum_out=nm[:, t, h:h + 1]).then_inc(s_masked, 1)
                    g = step - 2
                    if g >= 0:
                        dve.wait_ge(pT_ps, g + 1)
                        dve.tensor_copy(pT[:, g % 2, :], PS[:, 2 + g % 2, 0:384]).then_inc(pT_done, 1)
                dve.wait_ge(den_done, 1)
                link(dve.reciprocal(es[:, :, :], rl[:, :, :]))
                dve.wait_ge(pv_done, NH)
                for t in range(TT):
                    for h in range(2):
                        cols = slice(h * 512, h * 512 + 512)
                        dve.tensor_tensor(heads(xg[:, t, cols], GQ), heads(PS[:, 4 + 2 * t + h, :], GQ),
                                          bc(es[:, t, h * GQ:(h + 1) * GQ], DH), ALU.mult).then_inc(xg_ready, 1)
                for m in range(4):
                    turned(TBASE[n] + 1, m)
                for c in range(8, 11):
                    lo(base + c, c)

            def gdn(n):
                base = UBASE[n]

                def f(i):
                    return small[:, i, :, :]

                dve.wait_ge(rstd_ready, n + 1)
                dve.wait_ge(w_used, base + 1)
                for t in range(TT):
                    at = t * 2 * GH
                    dve.tensor_scalar(small[:, 0, t, :], PS[:, 2, at:at + GH], rstd[:, t:t + 1], None, ALU.mult)
                    dve.tensor_scalar(small[:, 1, t, :], PS[:, 2, at + GH:at + 2 * GH], rstd[:, t:t + 1], None,
                                      ALU.mult).then_inc(ba_rows, 1)
                lo(base + 3, 3)
                for s in range(1, PROJ_UNITS):
                    if s == 3:
                        dve.wait_ge(gate_u, 1)
                        dve.reciprocal(f(12), f(4)).then_inc(beta_ready, 1)
                    if s == 5:
                        dve.wait_ge(gc_ps, 1)
                        for i in range(2):
                            dve.tensor_copy(f(9 + i), PS[:, 4, i * 2 * GH:(i + 1) * 2 * GH].rearrange(
                                "p (t h) -> p t h", t=TT)).then_inc(gc_done, 1)
                    c = (s - 3) // 2 if s % 2 else 0
                    kind = CHUNKS[c][1] if 1 <= c <= 6 else None
                    hg = (CHUNKS[c][0] % D) // 512 if kind else 0
                    hs = slice(hg * HG, hg * HG + HG)
                    cols = slice(hg * 512, hg * 512 + 512)
                    if kind == "k":
                        for t in range(TT):
                            dve.wait_ge(ksq, 2 * (c - 1) + t + 1)
                            dve.tensor_reduce(small[:, 14, t, hs], heads(junk[:, t, 0:512]), AX.X,
                                              ALU.add).then_inc(kss_done, 1)
                    if kind == "q":
                        dve.wait_ge(bT_ready, 2 * c)
                        dve.tensor_copy(small[:, 16, :, hs], PS[:, 4, 0:2 * HG].rearrange("p (t h) -> p t h", t=TT)
                                        ).then_inc(qss_done, 1)
                    if kind == "v":
                        for t in range(TT):
                            dve.wait_ge(bT_ready, 2 * (c - 1) + t + 1)
                            dve.tensor_tensor(heads(vb[:, t, cols]), heads(PS[:, 4 + t, :]),
                                              bc(small[:, 12, t, hs], GD), ALU.mult).then_inc(v_done, 1)
                    lo(base + s + 3, s + 3)
                    if kind == "k":
                        for t in range(TT):
                            dve.wait_ge(rk_done, 2 * (c - 1) + t + 1)
                            dve.tensor_tensor(heads(khat[:, t, cols]), heads(PS[:, 4 + t, :]),
                                              bc(small[:, 15, t, hs], GD), ALU.mult).then_inc(kh_done, 1)
                    c = (s - 1) // 2
                    if s % 2 and 1 <= c <= 6:
                        for pair in range(2):
                            at = {}
                            for k in range(1, TAPS):
                                for i in (2 * pair, 2 * pair + 1):
                                    if k == 1:
                                        dve.wait_ge(tap_done, 4 * (c - 1) + i + 1)
                                    else:
                                        dve.wait_ge(dve_own, at[i])
                                    col = (TAPS - 1 - k) * CT + CHUNKS[c][0] // P + i
                                    x0 = (i % 2) * S
                                    ins = dve.scalar_tensor_tensor(
                                        out=cacc[:, i, k:], in0=PS[:, 6 + i // 2, x0:x0 + S - k],
                                        scalar=cw[:, col:col + 1], in1=cacc[:, i, k:], op0=ALU.mult, op1=ALU.add)
                                    if k == TAPS - 1:
                                        ins.then_inc(conv_done, 1)
                                    else:
                                        at[i] = link(ins, wait=False)
                for b in range(4):
                    for i, dst in enumerate((Nm, PTm)):
                        if i == 0:
                            dve.wait_ge(d_exp, b + 1)
                        dve.wait_ge(n_ps, 2 * b + i + 1)
                        dve.tensor_tensor(dst[:, b, :], PS[:, 2 + 2 * i + b % 2, :], Dm[:, b % 2, :],
                                          ALU.mult).then_inc(np_done, 1)
                for b in range(4):
                    dve.wait_ge(nm_ready, b + 1)
                    dve.tensor_tensor(Wm[:, 4 * b:4 * b + 4, :], rows(ident[:], HG), heads(NM[:, b % 2, :]),
                                      ALU.subtract).then_inc(w0_done, 1)
                nq = 4 * (LEVELS - 1)
                for r in range(nq):
                    b = r % 4
                    dve.wait_ge(wt_ps, r + 1)
                    if r < nq - 4:
                        v = Tm[:, 4 * b:4 * b + 4, :]
                        dve.tensor_tensor(v, v, heads(PS[:, 4 + r % 2, :]), ALU.subtract)
                    v = Wm[:, 4 * b:4 * b + 4, :]
                    dve.tensor_tensor(v, v, heads(PS[:, 2 + r % 2, :]), ALU.subtract).then_inc(wt_done, 1)
                dve.wait_ge(rq_done, 4)
                dve.wait_ge(eg_done, 1)
                for hg in range(NG):
                    hs, cols = slice(hg * HG, hg * HG + HG), slice(hg * 512, hg * 512 + 512)
                    dve.wait_ge(c3["o0p"], hg + 1)
                    dve.tensor_tensor(heads(khat[:, 0, cols]), heads(PS[:, 2 + hg, :]), bc(small[:, 17, 0, hs], GD),
                                      ALU.mult).then_inc(c3["o0"], 1)
                for hg in range(NG):
                    hs, cols = slice(hg * HG, hg * HG + HG), slice(hg * 512, hg * 512 + 512)
                    dve.wait_ge(c3["zp"], hg + 1)
                    link(dve.tensor_tensor(heads(R1[:, hg, :]), heads(PS[:, 6 + hg, :]), bc(small[:, 11, 1, hs], GD),
                                           ALU.mult))
                    dve.tensor_tensor(R1[:, hg, :], vb[:, 1, cols], R1[:, hg, :], ALU.subtract
                                      ).then_inc(c3["r1"], 1)
                for hg in range(NG):
                    hs = slice(hg * HG, hg * HG + HG)
                    dve.wait_ge(c3["ap"], hg + 1)
                    dve.tensor_tensor(heads(a1v[hg]), heads(PS[:, hg, :]), bc(small[:, 11, 1, hs], GD),
                                      ALU.mult).then_inc(c3["a1"], 1)
                for hg in range(NG):
                    hs, cols = slice(hg * HG, hg * HG + HG), slice(hg * 512, hg * 512 + 512)
                    dve.wait_ge(c3["bp"], hg + 1)
                    dve.wait_ge(c3["a1"], hg + 1)
                    link(dve.tensor_tensor(a1v[hg], PS[:, 4 + hg, :], a1v[hg], ALU.add))
                    dve.tensor_tensor(heads(vb[:, 0, cols]), heads(a1v[hg]), bc(small[:, 17, 1, hs], GD),
                                      ALU.mult).then_inc(c3["o1"], 1)
                for t in range(TT):
                    dve.wait_ge(osq, t + 1)
                    dve.tensor_reduce(small[:, 18, t, :], heads(kbTv[:, t, :], GH), AX.X, ALU.add
                                      ).then_inc(oss_done, 1)
                dve.wait_ge(zn_done, TT)
                for t in range(TT):
                    dve.wait_ge(ro_done, t + 1)
                    link(dve.tensor_tensor(heads(ov[t], GH), heads(ov[t], GH), bc(small[:, 19, t, :], GD), ALU.mult))
                    for h in range(2):
                        cols = slice(h * 512, h * 512 + 512)
                        dve.tensor_tensor(xg[:, t, cols], ov[t][:, cols], zs[:, t, cols], ALU.mult
                                          ).then_inc(xg_ready, 1)
                for m in range(4):
                    turned(TBASE[n] + 1, m)
                for c in range(20, 23):
                    lo(base + c, c)

            dve.wait_ge(const_in, 16 * 7)
            dve.wait_ge(masks, 1)
            dve.tensor_scalar(nsink[:], sink[:], -1.0, None, ALU.mult)
            link(dve.tensor_copy(ang[:, 2, 0:TT], posi[:]))
            for t in range(TT):
                last = dve.tensor_scalar(ang[:, 3, t * HALF:(t + 1) * HALF], es[:, 0, 0:HALF], ang[:, 2, t:t + 1], None,
                                         ALU.mult)
            link(last)
            magic = 1.5 * 2.0 ** 23
            c1 = 6.28125
            c2 = float(np.float32(TWO_PI - c1).view(np.uint32).__and__(np.uint32(0xfffff000)).view(np.float32))
            c3_ = TWO_PI - c1 - c2
            turns = ang[:, 2, :]
            for i, quarter in enumerate((0.0, 0.25)):
                r = ang[:, i, :]
                link(dve.tensor_scalar(turns, ang[:, 3, :], 1.0 / TWO_PI, quarter, ALU.mult, ALU.add))
                link(dve.tensor_scalar(turns, turns, magic, None, ALU.add))
                link(dve.tensor_scalar(turns, turns, magic, None, ALU.subtract))
                src = ang[:, 3, :]
                for part in (c1, c2, c3_):
                    link(dve.scalar_tensor_tensor(out=r, in0=turns, scalar=-part, in1=src, op0=ALU.mult, op1=ALU.add))
                    src = r
                if quarter:
                    link(dve.tensor_scalar(r, r, TWO_PI / 4, None, ALU.add))
                ins = dve.tensor_scalar(r, r, PI_BELOW, -PI_BELOW, ALU.min, ALU.max)
                if i == 0:
                    link(ins)
            ins.then_inc(dve_trig, 1)
            lo(0, 0)
            lo(1, 1)
            for n, kind in enumerate(stages):
                enter(n)
                (ffn if kind == "ffn" else swa if kind == "swa" else gdn)(n)
            n = len(stages) - 1
            for t in range(TT):
                added(n, t, scaled(n, t))


_INS = ["x", "positions", "l0_norms", "l0_ffn_w_in", "l0_ffn_w_out", "a_w_in", "a_b_in", "a_sinks", "a_w_out",
        "l1_norms", "l1_ffn_w_in", "l1_ffn_w_out", "b_w_in", "b_conv_w", "b_A_log", "b_dt_bias", "b_norm", "b_w_out"]


def kernel(**inputs):
    import numpy as _np
    import concourse.bacc as _bacc
    from concourse import mybir as _mybir
    from concourse.bass_utils import run_bass_kernel_spmd as _run

    nc = _bacc.Bacc("TRN2", target_bir_lowering=False, num_devices=1)
    arrays, args = {}, []
    for name in _INS:
        a = _np.ascontiguousarray(inputs[name])
        arrays[f"in_{name}"] = a
        args.append(nc.dram_tensor(f"in_{name}", a.shape, _mybir.dt.from_np(a.dtype), kind="ExternalInput").ap())
    o = nc.dram_tensor("out_0", (1, S, D), F32, kind="ExternalOutput").ap()
    build(nc, *args, o)
    r = _run(nc, [arrays], core_ids=[0])
    return _np.asarray(r.results[0]["out_0"])
```

```python
from contextlib import ExitStack

import numpy as np

import concourse.bass as bass
from concourse import mybir

F32 = mybir.dt.float32
F32R = mybir.dt.float32r
I32 = mybir.dt.int32
ALU = mybir.AluOpType
ACT = mybir.ActivationFunctionType
AX = mybir.AxisListType

P = 128
D = 1024
KT = D // P
TT = 2
S = TT * P
DFF = 2816
EPS = 1e-6
FC = 256
STEPS = DFF // FC
SLOTS = 3
UNIT = 2048

NH, KVH, DH = 16, 2, 64
GQ = NH // KVH
QC, QKVC = NH * DH, (NH + 2 * KVH) * DH
ROT = DH // 4
HALF = ROT // 2
NEG = -1e30

GH, GD = 8, 128
HG = 4
NG = GH // HG
TAPS = 4
CT = 3 * GH
LEVELS = 7

STAGES = ["ffn", "swa", "ffn", "ffn", "gdn", "ffn"]
UNITS = {"ffn": 3 * STEPS, "swa": 9, "gdn": 21}
INPUTS = {"ffn": 1, "swa": 2, "gdn": 2}
UBASE = [sum(UNITS[s] for s in STAGES[:n]) for n in range(len(STAGES) + 1)]
TBASE = [sum(INPUTS[s] for s in STAGES[:n]) for n in range(len(STAGES) + 1)]
TOTAL = UBASE[-1]
FFN_OF = {n: i for i, n in enumerate(n for n, s in enumerate(STAGES) if s == "ffn")}
COEF = [0.5, 1.0, 0.5, 0.5, 1.0, 0.5]

CHUNKS = {1: (1024, "k"), 2: (1536, "k"), 3: (0, "q"), 4: (512, "q"), 5: (2048, "v"), 6: (2560, "v"),
          7: (3072, "z"), 8: (3584, "z")}
PROJ_UNITS = 17
TWO_PI = 2 * np.pi
PI_BELOW = 3.1415925


def build(nc, x, positions, l0_norms, l0_ffn_w_in, l0_ffn_w_out, a_w_in, a_b_in, a_sinks, a_w_out,
          l1_norms, l1_ffn_w_in, l1_ffn_w_out, b_w_in, b_conv_w, b_A_log, b_dt_bias, b_norm, b_w_out,
          out, limit=len(STAGES)):
    stages = STAGES[:limit]
    total = UBASE[limit]
    with ExitStack() as ctx:
        def sb(name, shape, dt=F32):
            return ctx.enter_context(nc.sbuf_tensor(name, shape, dt))

        def sem(name):
            return ctx.enter_context(nc.semaphore(name))

        raw = sb("w_raw", [P, SLOTS, UNIT])
        whi = sb("w_high", [P, SLOTS, UNIT], F32R)
        wlo = sb("w_low", [P, SLOTS, UNIT], F32R)
        xh = sb("xT_high", [P, KT, S], F32R)
        xl = sb("xT_low", [P, KT, S], F32R)
        hTh = sb("hT_high", [P, 2, S], F32R)
        hTl = sb("hT_low", [P, 2, S], F32R)
        xs = sb("x_rows", [P, TT, D])
        xg = sb("x_gained", [P, TT, D])
        junk = sb("squares", [P, TT, D])
        gain = sb("gain_rows", [P, 2, D])
        arena = sb("mixer_arena", [P, 8 * 2048 + 1024])
        ident = sb("ident", [P, P])
        ones = sb("ones", [P, P])
        xss = sb("x_sumsq", [P, TT])
        yss = sb("y_sumsq", [P, TT])
        rstd = sb("rstd", [P, TT])
        yrs = sb("y_scale", [P, TT])
        pwv = sb("pow_base", [P, 2 * GH])
        mhalf = sb("minus_half", [P, 2 * GH])
        cs = sb("cos_rows", [P, TT, HALF])
        sn = sb("sin_rows", [P, TT, HALF])
        posi = sb("pos_int", [P, TT], I32)
        sink = sb("sinks", [P, NH])
        nsink = sb("minus_sinks", [P, NH])
        nm = sb("minus_rowmax", [P, TT, NH])
        rl = sb("row_sums", [P, TT, NH])
        es = sb("exp_sink", [P, TT, NH])
        cumU = sb("upper_ones", [P, P])
        negL = sb("mask_future", [P, P])
        lvl = sb("level_masks", [P, LEVELS, P])
        cw = sb("conv_w", [P, TAPS * CT])
        nrm = sb("gdn_norm", [P, GD])
        alog = sb("a_log", [P, GH])
        dtb = sb("dt_bias", [P, GH])
        small = sb("gdn_small", [P, 20, TT, GH])

        PS = ctx.enter_context(nc.psum_tensor("banks", [P, 8, 512], F32))

        def view(at, *shape):
            n = int(np.prod(shape))
            v = arena[:, at:at + n]
            if len(shape) == 2:
                v = v.rearrange("p (a b) -> p a b", a=shape[0])
            if len(shape) == 3:
                v = v.rearrange("p (a b c) -> p a b c", a=shape[0], b=shape[1])
            return v

        sg = view(14336, TT, FC)
        gated = view(14336 + 512, TT, FC)
        tmp = view(16384, 2, 512)
        qkv = view(0, TT, QKVC)
        kdup = view(2560, TT, 2 * P)
        kT = view(3072, KVH, S)
        qT = view(3584, NH // 2, S)
        sc = view(5632, 2, 384)
        pr = view(6400, 3, 384)
        pT = view(7552, 2, 384)
        bias = view(8320, QKVC)
        smask = view(9600, 384)
        rope = view(9984, 4, GQ * HALF)
        ang = view(10496, 4, TT * HALF)
        cwr = view(10752, P)
        gqT = view(0, GH, S)
        vb = view(2048, TT, D)
        khat = view(4096, TT, D)
        kb = view(6144, TT, D)
        Wm = view(6144, 2 * GH, P)
        khT = view(8192, GH, S)
        Tm = view(8192, 2 * GH, P)
        kbT = view(10240, GH, S)
        zs = view(12288, TT, D)
        stage = view(14336, TT, 512)
        Dm = view(14336, 2, 512)
        cacc = view(15360, 4, S)
        NM = view(15360, 2, 512)
        rT = view(16384, 4, S)
        R1 = view(16384, 2, 512)
        vn1v = [view(8192 + 512 * hg, 512) for hg in range(NG)]
        a1v = [view(9216 + 512 * hg, 512) for hg in range(NG)]
        kbTv = view(10240, TT, D)
        ov = [khat[:, 0, :], vb[:, 0, :]]
        lasth, lastl = xh[:, KT - 2:KT, :], xl[:, KT - 2:KT, :]
        baT = cacc[0:2 * GH, 0, :]
        gpair = {kind: view(11264, D) for kind in ("ffn", "swa")}
        gpair["gdn"] = vb[:, 1, :]
        Nm = xg[:, :, :].rearrange("p t d -> p (t d)").rearrange("p (b n) -> p b n", b=4)
        PTm = junk[:, :, :].rearrange("p t d -> p (t d)").rearrange("p (b n) -> p b n", b=4)

        x_in = [sem(f"x_in{t}") for t in range(TT)]
        const_in, out_done, x_out = sem("const_in"), sem("out_done"), sem("x_out")
        raw_in = [sem(f"raw_in{s}") for s in range(SLOTS)]
        gain_in = [sem(f"gain_in{s}") for s in range(2)]
        w_hi, w_lo, w_used = sem("w_hi"), sem("w_lo"), sem("w_used")
        ident_built, tables = sem("ident_built"), sem("tables_built")
        xg_ready, xT_ps, xT_hi, xT_lo = sem("xg_ready"), sem("xT_psum"), sem("xT_hi"), sem("xT_lo")
        xsq, rstd_ready = sem("x_squared"), sem("rstd_ready")
        y_ready, ysq, yrs_ready = sem("y_ready"), sem("y_squared"), sem("y_scale_ready")
        base_ready, ys_done = sem("x_base_ready"), sem("y_scaled")
        x_new = [sem(f"x_new{t}") for t in range(TT)]
        h_ready, silu_done, g_done = sem("h_ready"), sem("silu_done"), sem("gated_done")
        hT_ps, hT_hi, hT_lo = sem("hT_psum"), sem("hT_hi"), sem("hT_lo")
        dve_own, pool_own = sem("dve_own"), sem("pool_own")
        trig, dve_trig, cw_ps, cw_done = sem("trig"), sem("angles"), sem("conv_w_psum"), sem("conv_w")
        sp_ready, qkv_ready, rope_ready = sem("swa_proj"), sem("qkv_ready"), sem("rope_ready")
        sT_ps, sT_done = sem("qkT_psum"), sem("qkT_done")
        s_ready, s_masked, p_ready = sem("scores_ready"), sem("scores_masked"), sem("probs_ready")
        pT_ps, pT_done, pv_done = sem("probsT_psum"), sem("probsT_done"), sem("pv_done")
        snk_in, es_done, den_done = sem("sink_arg"), sem("exp_sink_done"), sem("den_done")
        ba_cols, ba_ps, ba_rows = sem("ba_cols"), sem("ba_psum"), sem("ba_rows")
        gate_arg, gate_exp, gate_u, gate_ln, g_ready, beta_ready = (
            sem("gate_arg"), sem("gate_exp"), sem("gate_u"), sem("gate_ln"), sem("g_ready"), sem("beta_ready"))
        gc_ps, gc_done, gdl, eg_done, ekd_done = (
            sem("gcum_psum"), sem("gcum_done"), sem("decay_left"), sem("exp_g"), sem("exp_left"))
        ch_ready, ch_evac, fT_ready = sem("chunk_ready"), sem("chunk_rows"), sem("chunkT_ready")
        tap_done, conv_step, conv_done, chan_done = (
            sem("tap_done"), sem("conv_step"), sem("conv_done"), sem("channels_done"))
        qsq_done, bT_ready, ksq, kss_done, rk_done, kh_done, kb_done = (
            sem("q_squared"), sem("rows_psum"), sem("k_squared"), sem("k_sumsq"), sem("k_scale"), sem("k_hat"),
            sem("k_beta"))
        qss_done, rq_done, v_done, z_done, zn_done, kd_done = (
            sem("q_sumsq"), sem("q_scale"), sem("v_beta"), sem("z_silu"), sem("z_normed"), sem("k_decayed"))
        kT_ps, kT_done = sem("kT_psum"), sem("kT_done")
        d_ps, d_exp, n_ps, np_done = sem("decay_psum"), sem("decay_exp"), sem("kk_kq_psum"), sem("n_p_done")
        nm_ready, w0_done, t0_ps, t0_done = sem("masked_n"), sem("w_init"), sem("t_init_psum"), sem("t_init")
        y_ps, y_cp, wt_ps, wt_done = sem("y_psum"), sem("y_copied"), sem("wt_psum"), sem("wt_updated")
        c3 = {k: sem("c3_" + k) for k in ("vn0p", "vn0", "o0p", "o0", "s1p", "s1", "zp", "r1", "ap", "a1",
                                         "vn1p", "vn1", "bp", "o1")}
        osq, oss_done, ro_done = sem("o_squared"), sem("o_sumsq"), sem("o_scale")

        def own(eng, s):
            n = [0]

            def link(ins, wait=True):
                n[0] += 1
                ins.then_inc(s, 1)
                if wait:
                    eng.wait_ge(s, n[0])
                return n[0]
            return link

        def tile_done(eng, t, first, n, used):
            if t == 0:
                eng.wait_ge(first, n)
            else:
                eng.wait_ge(w_used, used)

        def bc(ap, n):
            return ap.unsqueeze(2).to_broadcast([P, ap.shape[1], n])

        def rows(ap, n):
            return ap.unsqueeze(1).to_broadcast([P, n, ap.shape[1]])

        def heads(ap, n=HG):
            return ap.rearrange("p (h d) -> p h d", h=n)

        block = ctx.enter_context(nc.Block())

        @block.sync
        def _(sp):
            def slot(u, c, halves):
                if not (isinstance(u, int) and u < SLOTS):
                    sp.wait_ge(w_lo, u - SLOTS + 1)
                for dst, src in halves(raw[:, c % SLOTS, :]):
                    sp.dma_start(dst, src).then_inc(raw_in[c % SLOTS], 16)

            def up(w, j, k0):
                v = w.rearrange("(k p) (s n) -> p k s n", p=P, s=2)
                at = bass.ds(j * FC, FC)
                return lambda r: [(r.rearrange("p (k s n) -> p k s n", k=4, s=2)[:, :, s, :], v[:, k0:k0 + 4, s, at])
                                  for s in range(2)]

            def down(w, r0):
                return lambda r: [(r[:, k * D:(k + 1) * D], w[bass.ds(r0 + k * P, P), :]) for k in range(2)]

            def block(w, k0, nk, c0, nc_):
                v = w.rearrange("(k p) n -> p k n", p=P)
                h = nk // 2
                return lambda r: [(r[:, q * h * nc_:(q + 1) * h * nc_].rearrange("p (k n) -> p k n", k=h),
                                   v[:, k0 + q * h:k0 + (q + 1) * h, c0:c0 + nc_]) for q in range(2)]

            def ffn(base, wi, wo):
                slot(base, 0, up(wi, 0, 0))
                slot(base + 1, 1, up(wi, 0, 4))
                with sp.Fori(1, STEPS) as j:
                    slot(base + j * 3 - 1, 2, up(wi, j, 0))
                    slot(base + j * 3, 0, up(wi, j, 4))
                    slot(base + j * 3 + 1, 1, down(wo, j * FC - FC))
                slot(base + 3 * STEPS - 1, 2, down(wo, (STEPS - 1) * FC))

            for n, kind in enumerate(stages):
                base = UBASE[n]
                if kind == "ffn":
                    wi, wo = (l0_ffn_w_in, l0_ffn_w_out) if n < 3 else (l1_ffn_w_in, l1_ffn_w_out)
                    ffn(base, wi[0 if n % 3 == 0 else 1], wo[0 if n % 3 == 0 else 1])
                elif kind == "swa":
                    units = [block(a_w_in, 0, KT, QC, QKVC - QC)]
                    units += [block(a_w_in, 4 * h, 4, c * 512, 512) for c in range(2) for h in range(2)]
                    units += [down(a_w_out, 256 * i) for i in range(4)]
                    for c, u in enumerate(units):
                        slot(base + c, c, u)
                else:
                    units = [block(b_w_in, 0, KT, 4 * D, 2 * GH)]
                    units += [block(b_w_in, 4 * h, 4, CHUNKS[c][0], 512) for c in CHUNKS for h in range(2)]
                    units += [down(b_w_out, 256 * i) for i in range(4)]
                    for c, u in enumerate(units):
                        slot(base + c, c, u)
            for m in range(2 * TT):
                t, cols = m // 2, slice(m % 2 * 512, m % 2 * 512 + 512)
                sp.wait_ge(x_out, m + 1)
                sp.dma_start(out[0, t * P:(t + 1) * P, cols], xs[:, t, cols]).then_inc(out_done, 16)
            sp.wait_ge(out_done, 16 * 2 * TT)

        @block.gpsimd
        def _(pool):
            link = own(pool, pool_own)

            def gain_load(g):
                src = (l0_norms if g < 6 else l1_norms)[g % 6]
                pool.dma_start(gain[:, g % 2, :], src.partition_broadcast(P)).then_inc(gain_in[g % 2], 16)

            def select(v, op, fill, base, pattern, mult):
                link(pool.affine_select(out=v, in_=v, compare_op=op, fill=fill, base=base, pattern=pattern,
                                        channel_multiplier=mult))

            gain_load(0)
            gain_load(1)
            pool.memset(mhalf[:], -0.5)
            pool.memset(ones[:], 1.0)
            link(pool.memset(ident[:], 0.0))
            pool.affine_select(out=ident[:], in_=ident[:], compare_op=ALU.not_equal, fill=1.0, base=0,
                               pattern=[[-1, P]], channel_multiplier=1).then_inc(ident_built, 1)
            link(pool.memset(smask[:], 0.0))
            for c0 in (0, 256):
                select(smask[:, c0:c0 + P], ALU.is_ge, NEG, 0, [[-1, P]], 1)
            select(smask[:, P:2 * P], ALU.is_gt, NEG, 0, [[1, P]], -1)
            link(pool.memset(cumU[:], 1.0))
            select(cumU[:], ALU.is_ge, 0.0, 0, [[1, P]], -1)
            link(pool.memset(negL[:], 0.0))
            select(negL[:], ALU.is_ge, NEG, 0, [[1, P]], -1)
            link(pool.memset(lvl[:], 0.0))
            for i in range(LEVELS):
                b = 1 << i
                nb = P // (2 * b)
                v = lvl[:, i, :].rearrange("p (B h r) -> p B h r", h=2, r=b)[:, :, 1, :]
                link(pool.memset(v, 1.0))
                select(v, ALU.is_ge, 0.0, 0, [[-2 * b, nb], [0, b]], 1)
                select(v, ALU.is_ge, 0.0, b - 1, [[2 * b, nb], [0, b]], -1)
            freq = (500000.0 ** (-np.arange(0, ROT, 2, dtype=np.float32) / ROT)).astype(np.float32)
            for i in range(HALF):
                last = pool.memset(es[:, 0, i:i + 1], float(freq[i]))
            last.then_inc(tables, 1)

            def power(out, src, scale, shift, n, final=None):
                v = pwv[:, 0:n]
                link(pool.tensor_scalar(v, src, scale, shift, ALU.mult, ALU.add))
                ins = pool.tensor_tensor(out if final is None else v, v, mhalf[:, 0:n], ALU.pow)
                if final is not None:
                    link(ins)
                    ins = pool.tensor_scalar(out, v, final, None, ALU.mult)
                return ins

            def rope_group(t, c0, nh):
                v = qkv[:, t, c0:c0 + nh * DH].rearrange("p (h d) -> p h d", h=nh)
                x1, x2 = v[:, :, 0:HALF], v[:, :, HALF:ROT]
                tm = [rope[:, i, 0:nh * HALF].rearrange("p (h d) -> p h d", h=nh) for i in range(4)]
                c, s = rows(cs[:, t, :], nh), rows(sn[:, t, :], nh)
                pool.tensor_tensor(tm[0], x1, c, ALU.mult)
                pool.tensor_tensor(tm[1], x2, s, ALU.mult)
                pool.tensor_tensor(tm[2], x2, c, ALU.mult)
                link(pool.tensor_tensor(tm[3], x1, s, ALU.mult))
                pool.tensor_tensor(x1, tm[0], tm[1], ALU.subtract)
                return pool.tensor_tensor(x2, tm[2], tm[3], ALU.add)

            def swa():
                pool.wait_ge(trig, 1)
                for g, (c0, nh) in enumerate([(QC, KVH), (0, GQ), (512, GQ)]):
                    for t in range(TT):
                        pool.wait_ge(qkv_ready, 2 * g + t + 1)
                        ins = rope_group(t, c0, nh)
                        if g == 0:
                            link(ins)
                            src = qkv[:, t, QC:QC + P].rearrange("p (k d) -> p k d", k=KVH)
                            for dup in range(2):
                                dst = kdup[:, t, :].rearrange("p (k u d) -> p k u d", k=KVH, u=2)[:, :, dup, :]
                                ins = pool.tensor_copy(dst, src)
                                if dup == 0:
                                    link(ins)
                        ins.then_inc(rope_ready, 1)
                        pool.wait_ge(rope_ready, 2 * g + t + 1)
                pool.wait_ge(s_masked, 2 * NH)
                pool.tensor_tensor(es[:, :, :], nm[:, :, :], rows(sink[:], TT), ALU.add).then_inc(snk_in, 1)
                pool.wait_ge(es_done, 1)
                pool.tensor_tensor(rl[:, :, :], rl[:, :, :], es[:, :, :], ALU.add).then_inc(den_done, 1)

            sm = [small[:, i, :, :] for i in range(20)]

            def fl(i):
                return small[:, i, :, :].rearrange("p t h -> p (t h)")

            def gdn():
                b_, a_ = sm[0], sm[1]
                pool.wait_ge(ba_rows, 2)
                link(pool.tensor_tensor(a_, a_, rows(dtb[:], TT), ALU.add))
                link(pool.tensor_scalar(sm[2], a_, 0.0, -2.0, ALU.max, ALU.mult))
                pool.tensor_tensor(sm[2], a_, sm[2], ALU.add).then_inc(gate_arg, 1)
                pool.wait_ge(gate_exp, 3)
                link(pool.tensor_scalar(sm[4], sm[4], 1.0, None, ALU.add))
                pool.tensor_scalar(sm[5], sm[3], 1.0, None, ALU.add).then_inc(gate_u, 1)
                pool.wait_ge(gate_u, 1)
                link(pool.tensor_scalar(sm[6], sm[5], -1.0, None, ALU.add))
                link(pool.tensor_tensor(sm[6], sm[3], sm[6], ALU.subtract))
                link(pool.tensor_scalar(a_, a_, 0.0, None, ALU.max))
                link(pool.tensor_tensor(a_, a_, sm[6], ALU.add))
                pool.wait_ge(gate_ln, 1)
                link(pool.tensor_tensor(a_, a_, sm[7], ALU.add))
                link(pool.tensor_tensor(a_, a_, rows(alog[:], TT), ALU.mult))
                pool.tensor_scalar(sm[8], a_, -1.0, None, ALU.mult).then_inc(g_ready, 1)
                def decays():
                    pool.wait_ge(gc_done, 2)
                    pool.tensor_tensor(sm[10], sm[10], sm[9], ALU.subtract).then_inc(gdl, 1)
                    pool.wait_ge(gdl, 1)
                    pool.tensor_scalar(sm[13], sm[9], -1.0, None, ALU.mult).then_inc(gdl, 1)

                for c in range(1, 7):
                    hg = (CHUNKS[c][0] % D) // 512
                    hs = slice(hg * HG, hg * HG + HG)
                    if CHUNKS[c][1] == "k":
                        pool.wait_ge(kss_done, 2 * c)
                        for t in range(TT):
                            power(small[:, 15, t, hs], small[:, 14, t, hs], 1.0, EPS, HG).then_inc(rk_done, 1)
                            pool.wait_ge(rk_done, 2 * (c - 1) + t + 1)
                        for t in range(TT):
                            pool.wait_ge(kh_done, 2 * (c - 1) + t + 1)
                            pool.wait_ge(beta_ready, 1)
                            cols = slice(hg * 512, hg * 512 + 512)
                            pool.tensor_tensor(heads(kb[:, t, cols]), heads(khat[:, t, cols]),
                                               bc(small[:, 12, t, hs], GD), ALU.mult).then_inc(kb_done, 1)
                        if c == 1:
                            decays()
                    elif CHUNKS[c][1] == "q":
                        for i in range(4):
                            pool.wait_ge(chan_done, 4 * (c - 1) + i + 1)
                            pool.tensor_tensor(rT[:, i, :], gqT[:, hg * HG + i, :], gqT[:, hg * HG + i, :],
                                               ALU.mult).then_inc(qsq_done, 1)
                        pool.wait_ge(qss_done, c - 2)
                        for t in range(TT):
                            power(small[:, 17, t, hs], small[:, 16, t, hs], 1.0, EPS, HG,
                                  GD ** -0.5).then_inc(rq_done, 1)
                            pool.wait_ge(rq_done, 2 * (c - 3) + t + 1)
                pool.wait_ge(z_done, 4)
                for t in range(TT):
                    pool.tensor_tensor(heads(zs[:, t, :], GH), heads(zs[:, t, :], GH), rows(nrm[:], GH),
                                       ALU.mult).then_inc(zn_done, 1)
                pool.wait_ge(kT_ps, 8)
                pool.wait_ge(ekd_done, 1)
                pool.tensor_tensor(heads(khat[:, 1, :], GH), heads(khat[:, 0, :], GH),
                                   bc(small[:, 10, 0, :], GD), ALU.mult).then_inc(kd_done, 1)
                for q in range(4 * LEVELS):
                    level, b = divmod(q, 4)
                    if level == 0:
                        pool.wait_ge(np_done, 2 * (b + 1))
                    if q == 0:
                        pool.wait_ge(chan_done, 24)
                    elif 2 <= q < 6:
                        pool.wait_ge(w0_done, q - 1)
                    elif q >= 6:
                        pool.wait_ge(y_ps, q - 5)
                    pool.tensor_tensor(heads(NM[:, q % 2, :]), heads(Nm[:, b, :]), rows(lvl[:, level, :], HG),
                                       ALU.mult).then_inc(nm_ready, 1)
                for t in range(TT):
                    pool.wait_ge(oss_done, t + 1)
                    power(small[:, 19, t, :], small[:, 18, t, :], 1.0 / GD, EPS, GH).then_inc(ro_done, 1)
                    pool.wait_ge(ro_done, t + 1)

            def base_of_next(n, kind):
                if kind == "gdn":
                    pool.wait_ge(c3["r1"], NG)
                pool.wait_ge(gain_in[0], 16 * (n + 2))
                pool.wait_ge(gain_in[1], 16 * (n + 1))
                pool.tensor_tensor(gpair[kind], gain[:, 0, :], gain[:, 1, :], ALU.mult).then_inc(base_ready, 1)
                pool.wait_ge(xT_ps, 4 * TBASE[n + 1])
                for t in range(TT):
                    pool.tensor_tensor(xg[:, t, :], xs[:, t, :], gain[:, 0, :], ALU.mult).then_inc(base_ready, 1)

            for n, kind in enumerate(stages):
                pool.wait_ge(xsq, TT * (n + 1))
                power(rstd[:], xss[:], 1.0 / D, EPS, TT).then_inc(rstd_ready, 1)
                pool.wait_ge(rstd_ready, n + 1)
                if n:
                    for t in range(TT):
                        pool.wait_ge(x_new[t], n)
                    gain_load(2 * n + 1)
                if n + 1 < len(stages):
                    if n:
                        pool.wait_ge(base_ready, 3 * n)
                    else:
                        pool.wait_ge(xg_ready, 4)
                    gain_load(2 * n + 2)
                if kind == "swa":
                    swa()
                if kind == "gdn":
                    gdn()
                if n + 1 < len(stages):
                    base_of_next(n, kind)
                for t in range(TT):
                    pool.wait_ge(ysq, TT * n + t + 1)
                    power(yrs[:, t:t + 1], yss[:, t:t + 1], 1.0 / D, EPS, 1, COEF[n]).then_inc(yrs_ready, 1)
                    pool.wait_ge(yrs_ready, TT * n + t + 1)
                if n + 1 < len(stages):
                    pool.wait_ge(ys_done, n + 1)
                    link(pool.tensor_tensor(junk[:, 0, :], junk[:, 0, :], gain[:, 1, :], ALU.mult))
                    pool.tensor_tensor(xs[:, 0, :], xs[:, 0, :], junk[:, 0, :], ALU.add).then_inc(x_new[0], 1)

        @block.scalar
        def _(act):
            for t in range(TT):
                act.dma_start(xs[:, t, :], x[0, t * P:(t + 1) * P, :]).then_inc(x_in[t], 16)
            act.dma_start(posi[:], positions.rearrange("a (t p) -> p (a t)", p=P),
                          allow_slow_non_contiguous=True).then_inc(const_in, 16)
            act.dma_start(bias, a_b_in.partition_broadcast(P)).then_inc(const_in, 16)
            act.dma_start(sink[:], a_sinks.partition_broadcast(P)).then_inc(const_in, 16)
            act.dma_start(alog[:], b_A_log.partition_broadcast(P)).then_inc(const_in, 16)
            act.dma_start(dtb[:], b_dt_bias.partition_broadcast(P)).then_inc(const_in, 16)
            act.dma_start(nrm[:], b_norm.partition_broadcast(P)).then_inc(const_in, 16)
            act.dma_start(cwr[0:TAPS * CT, :], b_conv_w.rearrange("t (c p) -> (t c) p", p=P)).then_inc(const_in, 16)

            def hi(u, c, n=UNIT):
                if isinstance(u, int) and u >= total:
                    return
                third = (u - c % 3) // 3 if isinstance(u, int) else None
                act.wait_ge(raw_in[c % 3], 32 * (third + 1))
                if u >= SLOTS:
                    act.wait_ge(w_used, u - SLOTS + 1)
                act.activation(whi[:, c % 3, 0:n], raw[:, c % 3, 0:n], ACT.Copy).then_inc(w_hi, 1)

            def hi_loop(base, j, c):
                act.wait_ge(raw_in[c % 3], j * 32 + 32 * (base // 3 + c // 3 + 1))
                act.wait_ge(w_used, j * 3 + (base + c - SLOTS + 1))
                act.activation(whi[:, c % 3, :], raw[:, c % 3, :], ACT.Copy).then_inc(w_hi, 1)

            def turned(ti, m):
                t, h = divmod(m, 2)
                act.wait_ge(xT_ps, 4 * ti + m + 1)
                act.activation(xh[:, 4 * h:4 * h + 4, t * P:(t + 1) * P], heads(PS[:, 6 + h, :]),
                               ACT.Copy).then_inc(xT_hi, 1)

            def square_y(n, t):
                tile_done(act, t, y_ready, n + 1, UBASE[n + 1])
                act.wait_ge(xsq, TT * n + t + 1)
                act.activation(junk[:, t, :].rearrange("p (a b) -> p a b", a=2), PS[:, 2 * t:2 * t + 2, :],
                               ACT.Square, accum_out=yss[:, t:t + 1]).then_inc(ysq, 1)

            def enter(n):
                ti = TBASE[n]
                if n:
                    square_y(n - 1, 0)
                    hi(UBASE[n] + 1, 1)
                    turned(ti, 0)
                    square_y(n - 1, 1)
                    turned(ti, 1)
                    act.wait_ge(yrs_ready, TT * (n - 1) + 1)
                    act.activation(junk[:, 0, :].rearrange("p (a b) -> p a b", a=2), PS[:, 0:2, :], ACT.Copy,
                                   scale=yrs[:, 0:1]).then_inc(ys_done, 1)
                else:
                    hi(0, 0)
                    turned(ti, 0)
                    turned(ti, 1)
                    hi(1, 1)
                turned(ti, 2)
                turned(ti, 3)
                hi(UBASE[n] + 2, 2)
                for t in range(TT):
                    if n:
                        act.wait_ge(x_new[t], n)
                    else:
                        act.wait_ge(x_in[t], 16)
                    act.activation(junk[:, t, :], xs[:, t, :], ACT.Square,
                                   accum_out=xss[:, t:t + 1]).then_inc(xsq, 1)

            def ffn(n):
                f, base = FFN_OF[n], UBASE[n]

                def silu(j):
                    for t in range(TT):
                        if t == 0:
                            act.wait_ge(h_ready, j + (STEPS * f + 1))
                        elif isinstance(j, int):
                            act.wait_ge(w_used, base + (3 * j + 1 if j else 2))
                        else:
                            act.wait_ge(w_used, j * 3 + (base + 1))
                        act.activation(sg[:, t, :], PS[:, 4 + t, 0:FC], ACT.Silu,
                                       scale=rstd[:, t:t + 1]).then_inc(silu_done, 1)

                def turn(j, high=hTh[:, :, :]):
                    act.wait_ge(hT_ps, j + (STEPS * f + 1))
                    act.activation(high.rearrange("p k s -> p (k s)"), PS[:, 6, :], ACT.Copy).then_inc(hT_hi, 1)

                hi(base + 3, 3)
                act.wait_ge(rstd_ready, n + 1)
                silu(0)
                hi(base + 4, 4)
                if n == 0:
                    act.wait_ge(dve_trig, 1)
                    act.activation(sn[:, :, :].rearrange("p t f -> p (t f)"), ang[:, 0, :], ACT.Sin)
                    act.activation(cs[:, :, :].rearrange("p t f -> p (t f)"), ang[:, 1, :], ACT.Sin
                                   ).then_inc(trig, 1)
                with act.Fori(1, STEPS - 1) as j:
                    turn(j - 1)
                    hi_loop(base, j, 2)
                    silu(j)
                    hi_loop(base, j, 3)
                    hi_loop(base, j, 4)
                j = STEPS - 1
                turn(j - 1)
                hi(base + 3 * j + 2, 2)
                silu(j)
                turn(j, lasth)
                hi(base + 3 * j + 3, 3)

            def swa(n):
                base = UBASE[n]
                hi(base + 3, 3)
                hi(base + 4, 4)
                hi(base + 5, 5)
                hi(base + 6, 6)

                def turn(e):
                    act.wait_ge(sT_ps, e + 1)
                    if e == 0:
                        act.activation(kT.rearrange("p k s -> p (k s)"), PS[:, 6, :], ACT.Copy).then_inc(sT_done, 1)
                    else:
                        act.activation(qT[:, 2 * e - 2:2 * e, :].rearrange("p k s -> p (k s)"),
                                       PS[:, 6 + e % 2, :], ACT.Copy).then_inc(sT_done, 1)
                turn(0)
                hi(base + 7, 7)
                turn(1)
                turn(2)
                for h in range(NH):
                    if h == 2:
                        turn(3)
                        turn(4)
                    act.wait_ge(s_masked, 2 * h + 2)
                    if h >= 3:
                        act.wait_ge(pT_ps, h - 2)
                    act.activation(pr[:, h % 3, 0:P], sc[:, h % 2, 0:P], ACT.Exp, scale=-1.0,
                                   bias=nm[:, 0, h:h + 1], accum_out=rl[:, 0, h:h + 1])
                    act.activation(pr[:, h % 3, P:384], sc[:, h % 2, P:384], ACT.Exp, scale=-1.0,
                                   bias=nm[:, 1, h:h + 1], accum_out=rl[:, 1, h:h + 1]).then_inc(p_ready, 1)
                act.wait_ge(snk_in, 1)
                act.activation(es[:, :, :], es[:, :, :], ACT.Exp).then_inc(es_done, 1)
                for m in range(4):
                    turned(TBASE[n] + 1, m)
                for c in range(8, 10):
                    hi(base + c, c)

            def gdn(n):
                base = UBASE[n]

                def f(i):
                    return small[:, i, :, :]
                hi(base + 3, 3)
                act.wait_ge(rstd_ready, n + 1)
                for s in range(1, PROJ_UNITS):
                    c = s // 2
                    if s % 2 == 0 and c <= 6:
                        for t in range(TT):
                            tile_done(act, t, ch_ready, c, base + s + 1)
                            if c > 1:
                                act.wait_ge(fT_ready, 2 * (c - 1))
                            act.activation(stage[:, t, :], PS[:, (0 if c % 2 else 2) + t, :], ACT.Copy,
                                           scale=rstd[:, t:t + 1]).then_inc(ch_evac, 1)
                    elif s % 2 == 0:
                        for t in range(TT):
                            tile_done(act, t, ch_ready, c, base + s + 1)
                            act.activation(zs[:, t, (c - 7) * 512:(c - 6) * 512], PS[:, (0 if c % 2 else 2) + t, :],
                                           ACT.Silu, scale=rstd[:, t:t + 1]).then_inc(z_done, 1)
                    c = (s - 1) // 2
                    if s % 2 == 1 and 1 <= c <= 6:
                        for i in range(4):
                            act.wait_ge(fT_ready, 2 * (c - 1) + i // 2 + 1)
                            if c > 1:
                                act.wait_ge(chan_done, 4 * (c - 2) + i + 1)
                            tile = CHUNKS[c][0] // P + i
                            act.activation(cacc[:, i, :], PS[:, 6 + i // 2, (i % 2) * S:(i % 2 + 1) * S], ACT.Copy,
                                           scale=cw[:, 3 * CT + tile:3 * CT + tile + 1]).then_inc(tap_done, 1)
                    c = (s - 3) // 2
                    if s % 2 == 1 and c in (1, 2):
                        for t in range(TT):
                            act.wait_ge(bT_ready, 2 * (c - 1) + t + 1)
                            if c == 2:
                                act.wait_ge(kss_done, t + 1)
                            act.activation(junk[:, t, 0:512], PS[:, 4 + t, :], ACT.Square).then_inc(ksq, 1)
                    hi(base + s + 3, s + 3)
                    if s == 3:
                        act.wait_ge(gate_arg, 1)
                        act.activation(f(3), f(2), ACT.Exp).then_inc(gate_exp, 1)
                        act.activation(f(4), f(0), ACT.Exp, scale=-1.0).then_inc(gate_exp, 1)
                        act.wait_ge(const_in, 16 * 7)
                        act.activation(alog[:], alog[:], ACT.Exp).then_inc(gate_exp, 1)
                    if s == 4:
                        act.wait_ge(gate_u, 1)
                        act.activation(f(7), f(5), ACT.Ln).then_inc(gate_ln, 1)
                    c = (s - 2) // 2
                    if s % 2 == 0 and 1 <= c <= 6:
                        kind, hg = CHUNKS[c][1], (CHUNKS[c][0] % D) // 512
                        for i in range(4):
                            act.wait_ge(conv_done, 4 * (c - 1) + i + 1)
                            if c > 1:
                                act.wait_ge(bT_ready, 2 * (c - 1))
                            dst = gqT[:, hg * HG + i, :] if kind == "q" else rT[:, i, :]
                            act.activation(dst, cacc[:, i, :], ACT.Silu).then_inc(chan_done, 1)
                    if s == 7:
                        act.wait_ge(gdl, 2)
                        act.activation(f(11), f(9), ACT.Exp).then_inc(eg_done, 1)
                        act.activation(f(10), f(10), ACT.Exp).then_inc(ekd_done, 1)
                for e in range(8):
                    hg, rest = divmod(e, 4)
                    what, t = divmod(rest, 2)
                    act.wait_ge(kT_ps, e + 1)
                    dst = (kbT if what else khT)[:, hg * HG:hg * HG + HG, t * P:(t + 1) * P]
                    act.activation(dst, heads(PS[:, 6 + e % 2, :]), ACT.Copy).then_inc(kT_done, 1)
                for b in range(4):
                    hg, t = divmod(b, 2)
                    act.wait_ge(d_ps, b + 1)
                    if b >= 2:
                        act.wait_ge(np_done, 2 * (b - 1))
                    for i in range(HG):
                        h = hg * HG + i
                        last = act.activation(Dm[:, b % 2, i * P:(i + 1) * P], PS[:, b % 2, i * P:(i + 1) * P],
                                              ACT.Exp, bias=small[:, 13, t, h:h + 1])
                    last.then_inc(d_exp, 1)
                for b in range(4):
                    act.wait_ge(t0_ps, b + 1)
                    act.activation(Tm[:, 4 * b:4 * b + 4, :], heads(PS[:, 6 + b % 2, :]), ACT.Copy).then_inc(t0_done, 1)
                for q in range(4 * (LEVELS - 1)):
                    act.wait_ge(y_ps, q + 1)
                    if q >= 2:
                        act.wait_ge(wt_ps, q - 1)
                    act.activation(Dm[:, q % 2, :], PS[:, q % 2, :], ACT.Copy).then_inc(y_cp, 1)
                for hg in range(NG):
                    act.wait_ge(c3["vn0p"], hg + 1)
                    act.activation(Dm[:, hg, :], PS[:, hg, :], ACT.Copy).then_inc(c3["vn0"], 1)
                for hg in range(NG):
                    act.wait_ge(c3["s1p"], hg + 1)
                    act.activation(NM[:, hg, :], PS[:, 4 + hg, :], ACT.Copy).then_inc(c3["s1"], 1)
                for hg in range(NG):
                    act.wait_ge(c3["vn1p"], hg + 1)
                    act.activation(vn1v[hg], PS[:, 2 + hg, :], ACT.Copy).then_inc(c3["vn1"], 1)
                for t in range(TT):
                    act.wait_ge(c3["o0"] if t == 0 else c3["o1"], NG)
                    act.activation(kbTv[:, t, :], ov[t], ACT.Square).then_inc(osq, 1)
                for m in range(4):
                    turned(TBASE[n] + 1, m)
                for c in range(20, 22):
                    hi(base + c, c)

            for n, kind in enumerate(stages):
                enter(n)
                (ffn if kind == "ffn" else swa if kind == "swa" else gdn)(n)
            for t in range(TT):
                square_y(len(stages) - 1, t)

        @block.tensor
        def _(pe):
            def mm3(dst, sh, sl, wh, wl, start, stop):
                pe.matmul(dst, sh, wh, start=start, stop=False)
                pe.matmul(dst, sh, wl, start=False, stop=False)
                return pe.matmul(dst, sl, wh, start=False, stop=stop)

            def turn_x(ti, m):
                t, h = divmod(m, 2)
                pe.wait_ge(xg_ready, 4 * ti + m + 1)
                if m >= 2:
                    pe.wait_ge(xT_lo, 4 * ti + m - 1)
                for k in range(4):
                    last = pe.transpose(PS[:, 6 + h, k * P:(k + 1) * P],
                                        xg[:, t, (4 * h + k) * P:(4 * h + k + 1) * P], ident[:])
                last.then_inc(xT_ps, 1)

            def wide(c, t, bank, ncol, nk, k0, start, stop, ks=None):
                wh = whi[:, c % 3, 0:nk * ncol].rearrange("p (k n) -> p k n", k=nk)
                wl = wlo[:, c % 3, 0:nk * ncol].rearrange("p (k n) -> p k n", k=nk)
                for k in ks or range(nk):
                    tok = slice(t * P, (t + 1) * P)
                    last = mm3(bank, xh[:, k0 + k, tok], xl[:, k0 + k, tok], wh[:, k, :], wl[:, k, :],
                               start and k == 0, stop and k == nk - 1)
                return last

            def down(c, t, sh, sl, start, stop, ks=(0, 1)):
                for k in ks:
                    tok = slice(t * P, (t + 1) * P)
                    for h in range(2):
                        cols = slice(k * D + h * 512, k * D + h * 512 + 512)
                        pe.matmul(PS[:, 2 * t + h, :], sh[:, k, tok], whi[:, c % 3, cols],
                                  start=start and k == 0, stop=False)
                        pe.matmul(PS[:, 2 * t + h, :], sh[:, k, tok], wlo[:, c % 3, cols], start=False, stop=False)
                    for h in range(2):
                        cols = slice(k * D + h * 512, k * D + h * 512 + 512)
                        last = pe.matmul(PS[:, 2 * t + h, :], sl[:, k, tok], whi[:, c % 3, cols],
                                         start=False, stop=stop and k == 1)
                return last

            def begin(n):
                ti = TBASE[n]
                if n == 0:
                    turn_x(ti, 0)
                turn_x(ti, 1)
                pe.wait_ge(w_lo, UBASE[n] + 1)
                pe.wait_ge(xT_lo, 4 * ti + 1)

            def turn_next(n):
                if n + 1 < len(stages):
                    turn_x(TBASE[n + 1], 0)

            def ffn(n):
                f, base, ti = FFN_OF[n], UBASE[n], TBASE[n]

                def up(c, t, k0):
                    return wide(c, t, PS[:, 4 + t, :], 512, 4, k0, k0 == 0, k0 == 4)

                def turn(j):
                    pe.wait_ge(g_done, j * 2 + (2 * STEPS * f + 2))
                    for k in range(2):
                        for t in range(TT):
                            last = pe.transpose(PS[:, 6, k * S + t * P:k * S + (t + 1) * P],
                                                gated[:, t, k * P:(k + 1) * P], ident[:])
                    last.then_inc(hT_ps, 1)

                def up_step(j):
                    pe.wait_ge(w_lo, j * 3 + base)
                    pe.wait_ge(g_done, j * 2 + 2 * STEPS * f)
                    for t in range(TT):
                        last = up(2, t, 0)
                    last.then_inc(w_used, 1)
                    turn(j - 1)
                    pe.wait_ge(w_lo, j * 3 + (base + 1))
                    up(0, 0, 4).then_inc(h_ready, 1)
                    up(0, 1, 4).then_inc(w_used, 1)

                def step(j, first):
                    up_step(j)
                    pe.wait_ge(w_lo, j * 3 + (base + 2))
                    pe.wait_ge(hT_lo, j + STEPS * f)
                    for t in range(TT):
                        last = down(1, t, hTh, hTl, first, False)
                    last.then_inc(w_used, 1)

                def first_tile():
                    up(0, 0, 0)
                    pe.wait_ge(w_lo, base + 2)
                    pe.wait_ge(xT_lo, 4 * ti + 2)
                    wide(1, 0, PS[:, 4, :], 512, 4, 4, False, False, (0, 1))
                    turn_x(ti, 2)
                    wide(1, 0, PS[:, 4, :], 512, 4, 4, False, True, (2, 3)).then_inc(h_ready, 1)
                    turn_x(ti, 3)

                begin(n)
                first_tile()
                pe.wait_ge(xT_lo, 4 * ti + 3)
                up(0, 1, 0).then_inc(w_used, 1)
                pe.wait_ge(xT_lo, 4 * ti + 4)
                up(1, 1, 4).then_inc(w_used, 1)
                step(1, True)
                with pe.Fori(2, STEPS - 1) as j:
                    step(j, False)
                j = STEPS - 1
                up_step(j)
                pe.wait_ge(w_lo, base + 3 * j + 2)
                pe.wait_ge(hT_lo, STEPS * f + j)
                down(1, 0, hTh, hTl, False, False, (0,))
                turn(j)
                down(1, 0, hTh, hTl, False, False, (1,))
                pe.wait_ge(w_lo, base + 3 * j + 3)
                pe.wait_ge(hT_lo, STEPS * f + j + 1)
                down(2, 0, lasth, lastl, False, True).then_inc(y_ready, 1)
                down(1, 1, hTh, hTl, False, False).then_inc(w_used, 1)
                down(2, 1, lasth, lastl, False, True, (0,))
                turn_next(n)
                down(2, 1, lasth, lastl, False, True, (1,)).then_inc(w_used, 1)

            def out_proj(n, c0):
                base, ti = UBASE[n], TBASE[n] + 1

                def part(i, t, ks=(0, 1)):
                    pe.wait_ge(xT_lo, 4 * ti + 2 * t + (1 if i < 2 else 2))
                    return down(c0 + i, t, xh[:, 2 * i:2 * i + 2, :], xl[:, 2 * i:2 * i + 2, :], i == 0, i == 3,
                                ks)

                pe.wait_ge(xg_ready, 4 * ti + 4)
                turn_x(ti, 0)
                turn_x(ti, 1)
                for i in range(2):
                    pe.wait_ge(w_lo, base + c0 + i + 1)
                    part(i, 0)
                    if i == 0:
                        turn_x(ti, 2)
                        turn_x(ti, 3)
                    part(i, 1).then_inc(w_used, 1)
                pe.wait_ge(w_lo, base + c0 + 3)
                part(2, 0)
                pe.wait_ge(w_lo, base + c0 + 4)
                part(3, 0).then_inc(y_ready, 1)
                part(2, 1).then_inc(w_used, 1)
                part(3, 1, (0,))
                turn_next(n)
                part(3, 1, (1,)).then_inc(w_used, 1)

            def swa(n):
                base, ti = UBASE[n], TBASE[n]
                vcol = QC + P

                def turn_q(e):
                    for i in range(2):
                        for t in range(TT):
                            pair = 2 * e - 2 + i
                            last = pe.transpose(PS[:, 6 + e % 2, i * S + t * P:i * S + (t + 1) * P],
                                                qkv[:, t, pair * P:(pair + 1) * P], ident[:])
                    last.then_inc(sT_ps, 1)

                kvbank = [PS[:, 4 + t, 0:2 * P] for t in range(TT)]
                begin(n)
                wide(0, 0, kvbank[0], 2 * P, KT, 0, True, False, range(4))
                pe.wait_ge(xT_lo, 4 * ti + 2)
                wide(0, 0, kvbank[0], 2 * P, KT, 0, False, True, range(4, KT)).then_inc(sp_ready, 1)
                pe.wait_ge(w_lo, base + 2)
                pe.wait_ge(ys_done, n)
                wide(1, 0, PS[:, 0, :], 512, 4, 0, True, False, (0, 1))
                turn_x(ti, 2)
                wide(1, 0, PS[:, 0, :], 512, 4, 0, False, False, (2, 3))
                turn_x(ti, 3)
                pe.wait_ge(xT_lo, 4 * ti + 3)
                wide(0, 1, kvbank[1], 2 * P, KT, 0, True, False, range(4))
                pe.wait_ge(xT_lo, 4 * ti + 4)
                wide(0, 1, kvbank[1], 2 * P, KT, 0, False, True, range(4, KT)).then_inc(w_used, 1)
                wide(1, 1, PS[:, 1, :], 512, 4, 0, True, False).then_inc(w_used, 1)
                for c in range(2, 5):
                    chunk, h = divmod(c - 1, 2)
                    pe.wait_ge(w_lo, base + c + 1)
                    if c == 3:
                        pe.wait_ge(x_new[1], n)
                    last = wide(c, 0, PS[:, 2 * chunk, :], 512, 4, 4 * h, h == 0, h == 1)
                    if h:
                        last.then_inc(sp_ready, 1)
                    wide(c, 1, PS[:, 2 * chunk + 1, :], 512, 4, 4 * h, h == 0, h == 1).then_inc(w_used, 1)
                    if c == 3:
                        pe.wait_ge(rope_ready, 2)
                        for kv in range(KVH):
                            for t in range(TT):
                                last = pe.transpose(PS[:, 6, kv * S + t * P:kv * S + (t + 1) * P],
                                                    kdup[:, t, kv * P:(kv + 1) * P], ident[:])
                        last.then_inc(sT_ps, 1)
                        pe.wait_ge(const_in, 16 * 7)
                        pe.transpose(PS[:, 7, 0:TAPS * CT], cwr[0:TAPS * CT, :],
                                     ident[0:TAPS * CT, 0:TAPS * CT]).then_inc(cw_ps, 1)
                pe.wait_ge(rope_ready, 4)
                pe.wait_ge(cw_done, 1)
                turn_q(1)
                pe.wait_ge(sT_done, 1)
                turn_q(2)
                for step in range(NH + 3):
                    if step == 2:
                        pe.wait_ge(rope_ready, 6)
                        pe.wait_ge(sT_done, 2)
                        turn_q(3)
                        pe.wait_ge(sT_done, 3)
                        turn_q(4)
                    h = step
                    if h < NH:
                        pair, po, kv = h // 2, (h % 2) * DH, h // GQ
                        pe.wait_ge(sT_done, 3 if h < GQ else 5)
                        if h < 2:
                            pe.wait_ge(qkv_ready, 6)
                        else:
                            pe.wait_ge(s_masked, 2 * (h - 1))
                        q, k = qT[po:po + DH, pair, :], kT[po:po + DH, kv, :]
                        pe.matmul(PS[:, h % 2, 0:P], q[:, 0:P], k[:, 0:P], start=True, stop=True)
                        pe.matmul(PS[:, h % 2, P:384], q[:, P:S], k, start=True, stop=True).then_inc(s_ready, 1)
                    g = step - 2
                    if 0 <= g < NH:
                        pe.wait_ge(p_ready, g + 1)
                        if g >= 2:
                            pe.wait_ge(pT_done, g - 1)
                        for i in range(3):
                            last = pe.transpose(PS[:, 2 + g % 2, i * P:(i + 1) * P], pr[:, g % 3, i * P:(i + 1) * P],
                                                ident[:])
                        last.then_inc(pT_ps, 1)
                    g = step - 3
                    if g >= 0:
                        pe.wait_ge(pT_done, g + 1)
                        if g == 0:
                            pe.wait_ge(sT_done, 5)
                        kv = g // GQ
                        v = slice(vcol + kv * DH, vcol + (kv + 1) * DH)
                        at = slice((g % GQ) * DH, (g % GQ + 1) * DH)
                        pe.matmul(PS[:, 4 + kv, at], pT[:, g % 2, 0:P], qkv[:, 0, v], start=True, stop=True)
                        pe.matmul(PS[:, 6 + kv, at], pT[:, g % 2, P:2 * P], qkv[:, 0, v], start=True, stop=False)
                        pe.matmul(PS[:, 6 + kv, at], pT[:, g % 2, 2 * P:384], qkv[:, 1, v],
                                  start=False, stop=True).then_inc(pv_done, 1)
                out_proj(n, 5)

            def gdn(n):
                base, ti = UBASE[n], TBASE[n]
                g_flat = small[:, 8, :, :].rearrange("p t h -> p (t h)")

                def col(i):
                    return slice(i * P, (i + 1) * P)

                def four(bank, lhs, rhs, start=True):
                    for i in range(HG):
                        last = pe.matmul(PS[:, bank, col(i)], lhs(i), rhs(i), start=start, stop=True)
                    return last

                def turn_chunk(c):
                    pe.wait_ge(ch_evac, 2 * c)
                    if c > 1:
                        pe.wait_ge(conv_done, 4 * (c - 1))
                    for i in range(4):
                        for t in range(TT):
                            at = (i % 2) * S + t * P
                            last = pe.transpose(PS[:, 6 + i // 2, at:at + P], stage[:, t, col(i)], ident[:])
                        if i % 2:
                            last.then_inc(fT_ready, 1)

                def turn_back(c):
                    pe.wait_ge(chan_done, 4 * c)
                    if c == 2:
                        pe.wait_ge(gc_done, 2)
                    free = {1: (ba_rows, 2), 2: (kh_done, 2), 3: (kh_done, 4), 4: (qss_done, 1), 5: (qss_done, 2),
                            6: (v_done, 2)}[c]
                    pe.wait_ge(*free)
                    if CHUNKS[c][1] == "q":
                        pe.wait_ge(qsq_done, 4 * (c - 2))
                        for t in range(TT):
                            for i in range(4):
                                last = pe.matmul(PS[:, 4, 4 * t + i:4 * t + i + 1], rT[:, i, t * P:(t + 1) * P],
                                                 ones[:, 0:1], start=True, stop=True)
                            last.then_inc(bT_ready, 1)
                    else:
                        for t in range(TT):
                            for i in range(4):
                                last = pe.transpose(PS[:, 4 + t, col(i)], rT[:, i, t * P:(t + 1) * P], ident[:])
                            last.then_inc(bT_ready, 1)

                def turn_k(e):
                    hg, rest = divmod(e, 4)
                    what, t = divmod(rest, 2)
                    pe.wait_ge(kb_done if what else kh_done, 2 * hg + t + 1)
                    if e < 2:
                        pe.wait_ge(conv_done, 24)
                    else:
                        pe.wait_ge(kT_done, e - 1)
                    src = kb if what else khat
                    for i in range(HG):
                        at = (hg * HG + i) * P
                        last = pe.transpose(PS[:, 6 + e % 2, col(i)], src[:, t, at:at + P], ident[:])
                    last.then_inc(kT_ps, 1)

                n2 = 2 * GH
                begin(n)
                pe.wait_ge(w_lo, base + 2)
                pe.wait_ge(ys_done, n)
                wide(1, 0, PS[:, 0, :], 512, 4, 0, True, False, (0, 1))
                turn_x(ti, 2)
                wide(1, 0, PS[:, 0, :], 512, 4, 0, False, False, (2, 3))
                turn_x(ti, 3)
                pe.wait_ge(xT_lo, 4 * ti + 3)
                wide(1, 1, PS[:, 1, :], 512, 4, 0, True, False)
                pe.wait_ge(xT_lo, 4 * ti + 4)
                for k in range(KT):
                    w = slice(k * n2, (k + 1) * n2)
                    last = mm3(PS[0:n2, 4, 0:S], whi[:, 0, w], wlo[:, 0, w], xh[:, k, :], xl[:, k, :],
                               k == 0, k == KT - 1)
                last.then_inc(w_used, 2)
                for s in range(2, PROJ_UNITS):
                    c, h = (s + 1) // 2, (s + 1) % 2
                    pe.wait_ge(w_lo, base + s + 1)
                    if h == 0 and c == 2:
                        pe.wait_ge(x_new[1], n)
                    if h == 0 and c > 2:
                        pe.wait_ge(ch_evac, 2 * (c - 2))
                    bank = 0 if c % 2 else 2
                    last = wide(s, 0, PS[:, bank, :], 512, 4, 4 * h, h == 0, h == 1)
                    if h:
                        last.then_inc(ch_ready, 1)
                    wide(s, 1, PS[:, bank + 1, :], 512, 4, 4 * h, h == 0, h == 1).then_inc(w_used, 1)
                    if s == 2:
                        pe.wait_ge(ba_cols, 1)
                        for t in range(TT):
                            last = pe.transpose(PS[:, 5, t * n2:(t + 1) * n2], baT[:, t * P:(t + 1) * P],
                                                ident[0:n2, 0:n2])
                        last.then_inc(ba_ps, 1)
                    if s == 6:
                        pe.wait_ge(g_ready, 1)
                        pe.wait_ge(kh_done, 2)
                        pe.matmul(PS[:, 4, 0:n2], cumU[:], g_flat, start=True, stop=True)
                        pe.matmul(PS[:, 4, n2:2 * n2], ones[:], g_flat, start=True, stop=True).then_inc(gc_ps, 1)
                    if s % 2 and 1 <= (s - 1) // 2 <= 6:
                        turn_chunk((s - 1) // 2)
                    if s % 2 and 1 <= (s - 3) // 2 <= 6:
                        turn_back((s - 3) // 2)
                    if s >= 15:
                        turn_k(2 * (s - 15))
                        turn_k(2 * (s - 15) + 1)
                for e in range(4, 8):
                    turn_k(e)
                pe.wait_ge(z_done, 4)
                pe.wait_ge(v_done, 4)
                for b in range(4):
                    hg, t = divmod(b, 2)
                    tok = slice(t * P, (t + 1) * P)
                    pe.wait_ge(kT_done, 4 * hg + 4)
                    if b >= 2:
                        pe.wait_ge(d_exp, b - 1)
                    pe.matmul(PS[:, b % 2, :], ident[:], rows(negL[:], HG), start=True, stop=False)
                    for i in range(HG):
                        h = hg * HG + i
                        last = pe.matmul(PS[:, b % 2, col(i)], small[:, 8, t, h:h + 1].to_broadcast([P, P]), cumU[:],
                                         start=False, stop=i == HG - 1)
                    last.then_inc(d_ps, 1)
                    if b >= 2:
                        pe.wait_ge(np_done, 2 * (b - 1))
                    four(2 + b % 2, lambda i: khT[:, hg * HG + i, tok], lambda i: kbT[:, hg * HG + i, tok]
                         ).then_inc(n_ps, 1)
                    four(4 + b % 2, lambda i: khT[:, hg * HG + i, tok], lambda i: gqT[:, hg * HG + i, tok]
                         ).then_inc(n_ps, 1)
                for b in range(4):
                    pe.wait_ge(w0_done, b + 1)
                    if b >= 2:
                        pe.wait_ge(t0_done, b - 1)
                    for i in range(HG):
                        last = pe.transpose(PS[:, 6 + b % 2, col(i)], Wm[:, 4 * b + i, :], ident[:])
                    last.then_inc(t0_ps, 1)
                nq = 4 * (LEVELS - 1)
                for q in range(nq + 1):
                    if q < nq:
                        b = q % 4
                        pe.wait_ge(nm_ready, q + 5)
                        if q < 4:
                            pe.wait_ge(t0_done, b + 1)
                        else:
                            pe.wait_ge(wt_done, q - 3)
                        if q < 2:
                            pe.wait_ge(d_exp, 4)
                        else:
                            pe.wait_ge(y_cp, q - 1)
                        four(q % 2, lambda i: NM[:, q % 2, col(i)], lambda i: Tm[:, 4 * b + i, :]).then_inc(y_ps, 1)
                    if q >= 1:
                        r = q - 1
                        b = r % 4
                        pe.wait_ge(y_cp, r + 1)
                        if r < 2:
                            pe.wait_ge(np_done, 8)
                        else:
                            pe.wait_ge(wt_done, r - 1)
                        last = four(2 + r % 2, lambda i: Dm[:, r % 2, col(i)], lambda i: Wm[:, 4 * b + i, :])
                        if r < nq - 4:
                            last = four(4 + r % 2, lambda i: Wm[:, 4 * b + i, :], lambda i: Dm[:, r % 2, col(i)])
                        last.then_inc(wt_ps, 1)
                pe.wait_ge(wt_done, nq)
                for hg in range(NG):
                    four(hg, lambda i: Wm[:, 8 * hg + i, :], lambda i: vb[:, 0, (hg * HG + i) * P:(hg * HG + i + 1) * P]
                         ).then_inc(c3["vn0p"], 1)
                pe.wait_ge(kd_done, 1)
                for hg in range(NG):
                    pe.wait_ge(c3["vn0"], hg + 1)
                    four(4 + hg, lambda i: khat[:, 1, (hg * HG + i) * P:(hg * HG + i + 1) * P],
                         lambda i: Dm[:, hg, col(i)]).then_inc(c3["s1p"], 1)
                for hg in range(NG):
                    four(2 + hg, lambda i: PTm[:, 2 * hg, col(i)], lambda i: Dm[:, hg, col(i)]).then_inc(c3["o0p"], 1)
                for hg in range(NG):
                    pe.wait_ge(c3["s1"], hg + 1)
                    four(6 + hg, lambda i: kbT[:, hg * HG + i, P:S], lambda i: NM[:, hg, col(i)]).then_inc(c3["zp"], 1)
                for hg in range(NG):
                    four(hg, lambda i: gqT[:, hg * HG + i, P:S], lambda i: NM[:, hg, col(i)]).then_inc(c3["ap"], 1)
                for hg in range(NG):
                    pe.wait_ge(c3["r1"], hg + 1)
                    pe.wait_ge(c3["o0"], hg + 1)
                    four(2 + hg, lambda i: Wm[:, 8 * hg + 4 + i, :], lambda i: R1[:, hg, col(i)]
                         ).then_inc(c3["vn1p"], 1)
                for hg in range(NG):
                    pe.wait_ge(c3["vn1"], hg + 1)
                    four(4 + hg, lambda i: PTm[:, 2 * hg + 1, col(i)], lambda i: vn1v[hg][:, col(i)]
                         ).then_inc(c3["bp"], 1)
                out_proj(n, PROJ_UNITS)

            pe.wait_ge(ident_built, 1)
            for n, kind in enumerate(stages):
                (ffn if kind == "ffn" else swa if kind == "swa" else gdn)(n)

        @block.vector
        def _(dve):
            link = own(dve, dve_own)

            def lo(u, c):
                if isinstance(u, int) and u >= total:
                    return
                dve.wait_ge(w_hi, u + 1)
                dve.tensor_tensor(wlo[:, c % 3, :], raw[:, c % 3, :], whi[:, c % 3, :], ALU.subtract).then_inc(w_lo, 1)

            def turned(ti, m):
                t, h = divmod(m, 2)
                dve.wait_ge(xT_hi, 4 * ti + m + 1)
                at = (slice(None), slice(4 * h, 4 * h + 4), slice(t * P, (t + 1) * P))
                dve.tensor_tensor(xl[at], heads(PS[:, 6 + h, :]), xh[at], ALU.subtract).then_inc(xT_lo, 1)

            def scaled(n, t, g, out, h):
                dve.wait_ge(yrs_ready, TT * n + t + 1)
                return link(dve.scalar_tensor_tensor(out=out, in0=PS[:, 2 * t + h, :], scalar=yrs[:, t:t + 1],
                                                     in1=g[:, h * 512:h * 512 + 512], op0=ALU.mult, op1=ALU.mult),
                            wait=False)

            def angles():
                dve.wait_ge(const_in, 16 * 7)
                dve.wait_ge(tables, 1)
                dve.tensor_scalar(nsink[:], sink[:], -1.0, None, ALU.mult)
                link(dve.tensor_copy(ang[:, 2, 0:TT], posi[:]))
                for t in range(TT):
                    last = dve.tensor_scalar(ang[:, 3, t * HALF:(t + 1) * HALF], es[:, 0, 0:HALF], ang[:, 2, t:t + 1], None,
                                             ALU.mult)
                link(last)
                magic = 1.5 * 2.0 ** 23
                c1 = 6.28125
                c2 = float(np.float32(TWO_PI - c1).view(np.uint32).__and__(np.uint32(0xfffff000)).view(np.float32))
                c3_ = TWO_PI - c1 - c2
                turns = ang[:, 2, :]
                for i, quarter in enumerate((0.0, 0.25)):
                    r = ang[:, i, :]
                    link(dve.tensor_scalar(turns, ang[:, 3, :], 1.0 / TWO_PI, quarter, ALU.mult, ALU.add))
                    link(dve.tensor_scalar(turns, turns, magic, None, ALU.add))
                    link(dve.tensor_scalar(turns, turns, magic, None, ALU.subtract))
                    src = ang[:, 3, :]
                    for part in (c1, c2, c3_):
                        link(dve.scalar_tensor_tensor(out=r, in0=turns, scalar=-part, in1=src, op0=ALU.mult, op1=ALU.add))
                        src = r
                    if quarter:
                        link(dve.tensor_scalar(r, r, TWO_PI / 4, None, ALU.add))
                    ins = dve.tensor_scalar(r, r, PI_BELOW, -PI_BELOW, ALU.min, ALU.max)
                    if i == 0:
                        link(ins)
                ins.then_inc(dve_trig, 1)

            def next_input(n, t):
                dve.wait_ge(base_ready, 3 * (n + 1))
                if t:
                    dve.wait_ge(xg_ready, 4 * TBASE[n + 1] + 2)
                made = [scaled(n, t, gpair[stages[n]], tmp[:, h, :], h) for h in range(2)]
                for h in range(2):
                    cols = slice(h * 512, h * 512 + 512)
                    dve.wait_ge(dve_own, made[h])
                    dve.tensor_tensor(xg[:, t, cols], tmp[:, h, :], xg[:, t, cols], ALU.add).then_inc(xg_ready, 1)

            def enter(n):
                ti = TBASE[n]
                if n:
                    next_input(n - 1, 0)
                    turned(ti, 0)
                    lo(UBASE[n] + 1, 1)
                    turned(ti, 1)
                    next_input(n - 1, 1)
                else:
                    dve.wait_ge(gain_in[0], 16)
                    for t in range(TT):
                        dve.wait_ge(x_in[t], 16)
                        for h in range(2):
                            cols = slice(h * 512, h * 512 + 512)
                            dve.tensor_tensor(xg[:, t, cols], xs[:, t, cols], gain[:, 0, cols], ALU.mult
                                              ).then_inc(xg_ready, 1)
                        if t == 0:
                            turned(ti, 0)
                            lo(0, 0)
                            turned(ti, 1)
                    lo(1, 1)
                turned(ti, 2)
                turned(ti, 3)
                if n:
                    made = [scaled(n - 1, 1, gain[:, 1, :], junk[:, 1, h * 512:h * 512 + 512], h) for h in range(2)]
                    for h in range(2):
                        cols = slice(h * 512, h * 512 + 512)
                        dve.wait_ge(dve_own, made[h])
                        ins = dve.tensor_tensor(xs[:, 1, cols], xs[:, 1, cols], junk[:, 1, cols], ALU.add)
                    ins.then_inc(x_new[1], 1)
                lo(UBASE[n] + 2, 2)

            def ffn(n):
                f, base = FFN_OF[n], UBASE[n]

                def mul(j):
                    for t in range(TT):
                        dve.wait_ge(silu_done, j * 2 + (2 * STEPS * f + t + 1))
                        dve.scalar_tensor_tensor(out=gated[:, t, :], in0=PS[:, 4 + t, FC:2 * FC],
                                                 scalar=rstd[:, t:t + 1], in1=sg[:, t, :],
                                                 op0=ALU.mult, op1=ALU.mult).then_inc(g_done, 1)

                def turn(j, high=hTh[:, :, :], low=hTl[:, :, :]):
                    dve.wait_ge(hT_hi, j + (STEPS * f + 1))
                    flat = "p k s -> p (k s)"
                    dve.tensor_tensor(low.rearrange(flat), PS[:, 6, :], high.rearrange(flat),
                                      ALU.subtract).then_inc(hT_lo, 1)

                lo(base + 3, 3)
                mul(0)
                lo(base + 4, 4)
                if n == 0:
                    angles()
                with dve.Fori(1, STEPS - 1) as j:
                    turn(j - 1)
                    lo(j * 3 + (base + 2), 2)
                    mul(j)
                    lo(j * 3 + (base + 3), 3)
                    lo(j * 3 + (base + 4), 4)
                j = STEPS - 1
                turn(j - 1)
                lo(base + 3 * j + 2, 2)
                mul(j)
                turn(j, lasth, lastl)
                lo(base + 3 * j + 3, 3)

            def swa(n):
                base = UBASE[n]
                scale = -DH ** -0.5

                def rows_out(g, bank, c0, nc_, used):
                    for t in range(TT):
                        tile_done(dve, t, sp_ready, g + 1, used)
                        dve.scalar_tensor_tensor(out=qkv[:, t, c0:c0 + nc_], in0=PS[:, bank(t), 0:nc_],
                                                 scalar=rstd[:, t:t + 1], in1=bias[:, c0:c0 + nc_],
                                                 op0=ALU.mult, op1=ALU.add).then_inc(qkv_ready, 1)

                dve.wait_ge(rstd_ready, n + 1)
                rows_out(0, lambda t: 4 + t, QC, QKVC - QC, base + 1)
                lo(base + 3, 3)
                lo(base + 4, 4)
                rows_out(1, lambda t: t, 0, 512, base + 3)
                lo(base + 5, 5)
                lo(base + 6, 6)
                dve.wait_ge(cw_ps, 1)
                dve.tensor_copy(cw[:], PS[:, 7, 0:TAPS * CT]).then_inc(cw_done, 1)
                rows_out(2, lambda t: 2 + t, 512, 512, base + 5)
                lo(base + 7, 7)
                for step in range(NH + 2):
                    h = step
                    if h < NH:
                        dve.wait_ge(s_ready, h + 1)
                        if h >= 2:
                            dve.wait_ge(p_ready, h - 1)
                        for t, cols in enumerate((slice(0, P), slice(P, 384))):
                            dve.tensor_tensor_reduce(out=sc[:, h % 2, cols], in0=PS[:, h % 2, cols],
                                                     in1=smask[:, cols], scale=scale, scalar=nsink[:, h:h + 1],
                                                     op0=ALU.add, op1=ALU.min,
                                                     accum_out=nm[:, t, h:h + 1]).then_inc(s_masked, 1)
                    g = step - 2
                    if g >= 0:
                        dve.wait_ge(pT_ps, g + 1)
                        dve.tensor_copy(pT[:, g % 2, :], PS[:, 2 + g % 2, 0:384]).then_inc(pT_done, 1)
                dve.wait_ge(den_done, 1)
                link(dve.reciprocal(es[:, :, :], rl[:, :, :]))
                dve.wait_ge(pv_done, NH)
                for t in range(TT):
                    for h in range(2):
                        cols = slice(h * 512, h * 512 + 512)
                        dve.tensor_tensor(heads(xg[:, t, cols], GQ), heads(PS[:, 4 + 2 * t + h, :], GQ),
                                          bc(es[:, t, h * GQ:(h + 1) * GQ], DH), ALU.mult).then_inc(xg_ready, 1)
                for m in range(4):
                    turned(TBASE[n] + 1, m)
                for c in range(8, 10):
                    lo(base + c, c)

            def gdn(n):
                base = UBASE[n]

                def f(i):
                    return small[:, i, :, :]

                dve.wait_ge(rstd_ready, n + 1)
                dve.wait_ge(w_used, base + 2)
                dve.tensor_copy(baT, PS[0:2 * GH, 4, 0:S]).then_inc(ba_cols, 1)
                lo(base + 3, 3)
                for s in range(1, PROJ_UNITS):
                    if s == 3:
                        dve.wait_ge(ba_ps, 1)
                        for t in range(TT):
                            at = t * 2 * GH
                            dve.tensor_scalar(small[:, 0, t, :], PS[:, 5, at:at + GH], rstd[:, t:t + 1], None,
                                              ALU.mult)
                            dve.tensor_scalar(small[:, 1, t, :], PS[:, 5, at + GH:at + 2 * GH], rstd[:, t:t + 1],
                                              None, ALU.mult).then_inc(ba_rows, 1)
                    if s == 5:
                        dve.wait_ge(gate_u, 1)
                        dve.reciprocal(f(12), f(4)).then_inc(beta_ready, 1)
                    if s == 7:
                        dve.wait_ge(gc_ps, 1)
                        for i in range(2):
                            dve.tensor_copy(f(9 + i), PS[:, 4, i * 2 * GH:(i + 1) * 2 * GH].rearrange(
                                "p (t h) -> p t h", t=TT)).then_inc(gc_done, 1)
                    c = (s - 3) // 2 if s % 2 else 0
                    kind = CHUNKS[c][1] if 1 <= c <= 6 else None
                    hg = (CHUNKS[c][0] % D) // 512 if kind else 0
                    hs = slice(hg * HG, hg * HG + HG)
                    cols = slice(hg * 512, hg * 512 + 512)
                    if kind == "k":
                        for t in range(TT):
                            dve.wait_ge(ksq, 2 * (c - 1) + t + 1)
                            dve.tensor_reduce(small[:, 14, t, hs], heads(junk[:, t, 0:512]), AX.X,
                                              ALU.add).then_inc(kss_done, 1)
                    if kind == "q":
                        dve.wait_ge(bT_ready, 2 * c)
                        dve.tensor_copy(small[:, 16, :, hs], PS[:, 4, 0:2 * HG].rearrange("p (t h) -> p t h", t=TT)
                                        ).then_inc(qss_done, 1)
                    if kind == "v":
                        for t in range(TT):
                            dve.wait_ge(bT_ready, 2 * (c - 1) + t + 1)
                            dve.tensor_tensor(heads(vb[:, t, cols]), heads(PS[:, 4 + t, :]),
                                              bc(small[:, 12, t, hs], GD), ALU.mult).then_inc(v_done, 1)
                    lo(base + s + 3, s + 3)
                    if kind == "k":
                        for t in range(TT):
                            dve.wait_ge(rk_done, 2 * (c - 1) + t + 1)
                            dve.tensor_tensor(heads(khat[:, t, cols]), heads(PS[:, 4 + t, :]),
                                              bc(small[:, 15, t, hs], GD), ALU.mult).then_inc(kh_done, 1)
                    c = (s - 1) // 2
                    if s % 2 and 1 <= c <= 6:
                        for pair in range(2):
                            at = {}
                            for k in range(1, TAPS):
                                for i in (2 * pair, 2 * pair + 1):
                                    if k == 1:
                                        dve.wait_ge(tap_done, 4 * (c - 1) + i + 1)
                                    else:
                                        dve.wait_ge(dve_own, at[i])
                                    col = (TAPS - 1 - k) * CT + CHUNKS[c][0] // P + i
                                    x0 = (i % 2) * S
                                    ins = dve.scalar_tensor_tensor(
                                        out=cacc[:, i, k:], in0=PS[:, 6 + i // 2, x0:x0 + S - k],
                                        scalar=cw[:, col:col + 1], in1=cacc[:, i, k:], op0=ALU.mult, op1=ALU.add)
                                    if k == TAPS - 1:
                                        ins.then_inc(conv_done, 1)
                                    else:
                                        at[i] = link(ins, wait=False)
                for b in range(4):
                    for i, dst in enumerate((Nm, PTm)):
                        if i == 0:
                            dve.wait_ge(d_exp, b + 1)
                        dve.wait_ge(n_ps, 2 * b + i + 1)
                        dve.tensor_tensor(dst[:, b, :], PS[:, 2 + 2 * i + b % 2, :], Dm[:, b % 2, :],
                                          ALU.mult).then_inc(np_done, 1)
                for b in range(4):
                    dve.wait_ge(nm_ready, b + 1)
                    dve.tensor_tensor(Wm[:, 4 * b:4 * b + 4, :], rows(ident[:], HG), heads(NM[:, b % 2, :]),
                                      ALU.subtract).then_inc(w0_done, 1)
                nq = 4 * (LEVELS - 1)
                for r in range(nq):
                    b = r % 4
                    dve.wait_ge(wt_ps, r + 1)
                    if r < nq - 4:
                        v = Tm[:, 4 * b:4 * b + 4, :]
                        dve.tensor_tensor(v, v, heads(PS[:, 4 + r % 2, :]), ALU.subtract)
                    v = Wm[:, 4 * b:4 * b + 4, :]
                    dve.tensor_tensor(v, v, heads(PS[:, 2 + r % 2, :]), ALU.subtract).then_inc(wt_done, 1)
                dve.wait_ge(rq_done, 4)
                dve.wait_ge(eg_done, 1)
                for hg in range(NG):
                    hs, cols = slice(hg * HG, hg * HG + HG), slice(hg * 512, hg * 512 + 512)
                    dve.wait_ge(c3["o0p"], hg + 1)
                    dve.tensor_tensor(heads(khat[:, 0, cols]), heads(PS[:, 2 + hg, :]), bc(small[:, 17, 0, hs], GD),
                                      ALU.mult).then_inc(c3["o0"], 1)
                for hg in range(NG):
                    hs, cols = slice(hg * HG, hg * HG + HG), slice(hg * 512, hg * 512 + 512)
                    dve.wait_ge(c3["zp"], hg + 1)
                    link(dve.tensor_tensor(heads(R1[:, hg, :]), heads(PS[:, 6 + hg, :]), bc(small[:, 11, 1, hs], GD),
                                           ALU.mult))
                    dve.tensor_tensor(R1[:, hg, :], vb[:, 1, cols], R1[:, hg, :], ALU.subtract
                                      ).then_inc(c3["r1"], 1)
                for hg in range(NG):
                    hs = slice(hg * HG, hg * HG + HG)
                    dve.wait_ge(c3["ap"], hg + 1)
                    dve.tensor_tensor(heads(a1v[hg]), heads(PS[:, hg, :]), bc(small[:, 11, 1, hs], GD),
                                      ALU.mult).then_inc(c3["a1"], 1)
                for hg in range(NG):
                    hs, cols = slice(hg * HG, hg * HG + HG), slice(hg * 512, hg * 512 + 512)
                    dve.wait_ge(c3["bp"], hg + 1)
                    dve.wait_ge(c3["a1"], hg + 1)
                    link(dve.tensor_tensor(a1v[hg], PS[:, 4 + hg, :], a1v[hg], ALU.add))
                    dve.tensor_tensor(heads(vb[:, 0, cols]), heads(a1v[hg]), bc(small[:, 17, 1, hs], GD),
                                      ALU.mult).then_inc(c3["o1"], 1)
                for t in range(TT):
                    dve.wait_ge(osq, t + 1)
                    dve.tensor_reduce(small[:, 18, t, :], heads(kbTv[:, t, :], GH), AX.X, ALU.add
                                      ).then_inc(oss_done, 1)
                dve.wait_ge(zn_done, TT)
                for t in range(TT):
                    dve.wait_ge(ro_done, t + 1)
                    link(dve.tensor_tensor(heads(ov[t], GH), heads(ov[t], GH), bc(small[:, 19, t, :], GD), ALU.mult))
                    for h in range(2):
                        cols = slice(h * 512, h * 512 + 512)
                        dve.tensor_tensor(xg[:, t, cols], ov[t][:, cols], zs[:, t, cols], ALU.mult
                                          ).then_inc(xg_ready, 1)
                for m in range(4):
                    turned(TBASE[n] + 1, m)
                for c in range(20, 22):
                    lo(base + c, c)

            for n, kind in enumerate(stages):
                enter(n)
                (ffn if kind == "ffn" else swa if kind == "swa" else gdn)(n)
            n = len(stages) - 1
            dve.wait_ge(gain_in[1], 16 * (n + 1))
            for t in range(TT):
                if t:
                    dve.wait_ge(x_out, 2)
                made = [scaled(n, t, gain[:, 1, :], tmp[:, h, :], h) for h in range(2)]
                for h in range(2):
                    cols = slice(h * 512, h * 512 + 512)
                    dve.wait_ge(dve_own, made[h])
                    dve.tensor_tensor(xs[:, t, cols], xs[:, t, cols], tmp[:, h, :], ALU.add).then_inc(x_out, 1)


_INS = ["x", "positions", "l0_norms", "l0_ffn_w_in", "l0_ffn_w_out", "a_w_in", "a_b_in", "a_sinks", "a_w_out",
        "l1_norms", "l1_ffn_w_in", "l1_ffn_w_out", "b_w_in", "b_conv_w", "b_A_log", "b_dt_bias", "b_norm", "b_w_out"]


def kernel(**inputs):
    import numpy as _np
    import concourse.bacc as _bacc
    from concourse import mybir as _mybir
    from concourse.bass_utils import run_bass_kernel_spmd as _run

    nc = _bacc.Bacc("TRN2", target_bir_lowering=False, num_devices=1)
    arrays, args = {}, []
    for name in _INS:
        a = _np.ascontiguousarray(inputs[name])
        arrays[f"in_{name}"] = a
        args.append(nc.dram_tensor(f"in_{name}", a.shape, _mybir.dt.from_np(a.dtype), kind="ExternalInput").ap())
    o = nc.dram_tensor("out_0", (1, S, D), F32, kind="ExternalOutput").ap()
    build(nc, *args, o)
    r = _run(nc, [arrays], core_ids=[0])
    return _np.asarray(r.results[0]["out_0"])
```

```python
from contextlib import ExitStack

import numpy as np

import concourse.bass as bass
from concourse import mybir

F32 = mybir.dt.float32
F32R = mybir.dt.float32r
I32 = mybir.dt.int32
ALU = mybir.AluOpType
ACT = mybir.ActivationFunctionType
AX = mybir.AxisListType

P = 128
D = 1024
KT = D // P
TT = 2
S = TT * P
DFF = 2816
EPS = 1e-6
FC = 256
STEPS = DFF // FC
SLOTS = 3
HBANK = [4, 5]
HBANK0 = [4, 0]
UNIT = 2048

NH, KVH, DH = 16, 2, 64
GQ = NH // KVH
QC, QKVC = NH * DH, (NH + 2 * KVH) * DH
ROT = DH // 4
HALF = ROT // 2
NEG = -1e30
QBANK = [6, 4, 7, 5, 6]

GH, GD = 8, 128
HG = 4
NG = GH // HG
TAPS = 4
KBANK = [6, 7, 4, 5]
CT = 3 * GH
LEVELS = 7

STAGES = ["ffn", "swa", "ffn", "ffn", "gdn", "ffn"]
UNITS = {"ffn": 3 * STEPS, "swa": 9, "gdn": 21}
INPUTS = {"ffn": 1, "swa": 2, "gdn": 2}
UBASE = [sum(UNITS[s] for s in STAGES[:n]) for n in range(len(STAGES) + 1)]
TBASE = [sum(INPUTS[s] for s in STAGES[:n]) for n in range(len(STAGES) + 1)]
OUT_INPUTS = [TBASE[n] + 1 for n, s in enumerate(STAGES) if s != "ffn"]
FFN_OF = {n: i for i, n in enumerate(n for n, s in enumerate(STAGES) if s == "ffn")}
COEF = [0.5, 1.0, 0.5, 0.5, 1.0, 0.5]

CHUNKS = {1: (1024, "k"), 2: (1536, "k"), 3: (0, "q"), 4: (512, "q"), 5: (2048, "v"), 6: (2560, "v"),
          7: (3072, "z"), 8: (3584, "z")}
PROJ_UNITS = 17
TWO_PI = 2 * np.pi
PI_BELOW = 3.1415925


def build(nc, x, positions, l0_norms, l0_ffn_w_in, l0_ffn_w_out, a_w_in, a_b_in, a_sinks, a_w_out,
          l1_norms, l1_ffn_w_in, l1_ffn_w_out, b_w_in, b_conv_w, b_A_log, b_dt_bias, b_norm, b_w_out,
          out, limit=len(STAGES)):
    stages = STAGES[:limit]
    total = UBASE[limit]
    with ExitStack() as ctx:
        def sb(name, shape, dt=F32):
            return ctx.enter_context(nc.sbuf_tensor(name, shape, dt))

        def sem(name):
            return ctx.enter_context(nc.semaphore(name))

        raw = sb("w_raw", [P, SLOTS, UNIT])
        whi = sb("w_high", [P, SLOTS, UNIT], F32R)
        wlo = sb("w_low", [P, SLOTS, UNIT], F32R)
        xh = sb("xT_high", [P, KT, S], F32R)
        xl = sb("xT_low", [P, KT, S], F32R)
        hTh = sb("hT_high", [P, 2, S], F32R)
        hTl = sb("hT_low", [P, 2, S], F32R)
        xs = sb("x_rows", [P, TT, D])
        xg = sb("x_gained", [P, TT, D])
        junk = sb("squares", [P, TT, D])
        gain = sb("gain_rows", [P, 2, D])
        arena = sb("mixer_arena", [P, 8 * 2048 + 1024])
        ident = sb("ident", [P, P])
        ones = sb("ones", [P, P])
        xss = sb("x_sumsq", [P, TT])
        yss = sb("y_sumsq", [P, TT])
        rstd = sb("rstd", [P, TT])
        yrs = sb("y_scale", [P, TT])
        pwv = sb("pow_base", [P, 2 * GH])
        mhalf = sb("minus_half", [P, 2 * GH])
        cs = sb("cos_rows", [P, TT, HALF])
        sn = sb("sin_rows", [P, TT, HALF])
        posi = sb("pos_int", [P, TT], I32)
        sink = sb("sinks", [P, NH])
        nsink = sb("minus_sinks", [P, NH])
        nm = sb("minus_rowmax", [P, TT, NH])
        rl = sb("row_sums", [P, TT, NH])
        es = sb("exp_sink", [P, TT, NH])
        cumU = sb("upper_ones", [P, P])
        negL = sb("mask_future", [P, P])
        lvl = sb("level_masks", [P, LEVELS, P])
        cw = sb("conv_w", [P, TAPS * CT])
        nrm = sb("gdn_norm", [P, GD])
        alog = sb("a_log", [P, GH])
        dtb = sb("dt_bias", [P, GH])
        small = sb("gdn_small", [P, 20, TT, GH])

        PS = ctx.enter_context(nc.psum_tensor("banks", [P, 8, 512], F32))

        def view(at, *shape):
            n = int(np.prod(shape))
            v = arena[:, at:at + n]
            if len(shape) == 2:
                v = v.rearrange("p (a b) -> p a b", a=shape[0])
            if len(shape) == 3:
                v = v.rearrange("p (a b c) -> p a b c", a=shape[0], b=shape[1])
            return v

        sg = view(14336, TT, FC)
        gated = view(14336 + 512, TT, FC)
        tmp = view(16384, 2, 512)
        qkv = view(0, TT, QKVC)
        kdup = view(2560, TT, 2 * P)
        kT = view(3072, KVH, S)
        qT = view(3584, NH // 2, S)
        sc = view(5632, 2, 384)
        pr = view(6400, 3, 384)
        pT = view(7552, 2, 384)
        bias = view(8320, QKVC)
        smask = view(9600, 384)
        rope = view(9984, 4, GQ * HALF)
        ang = view(10496, 4, TT * HALF)
        cwr = view(10752, P)
        gqT = view(0, GH, S)
        vb = view(2048, TT, D)
        khat = view(4096, TT, D)
        Wm = view(6144, 2 * GH, P)
        Tm = view(8192, 2 * GH, P)
        khT = view(10240, GH, S)
        zs = view(12288, TT, D)
        stage = view(14336, TT, 512)
        Dm = view(14336, 2, 512)
        cacc = view(15360, 4, S)
        NM = view(15360, 2, 512)
        rT = view(16384, 4, S)
        R1 = view(16384, 2, 512)
        vn1v = [view(8192 + 512 * hg, 512) for hg in range(NG)]
        a1v = [view(9216 + 512 * hg, 512) for hg in range(NG)]
        ov = [khat[:, 0, :], vb[:, 0, :]]
        osqv = [khat[:, 1, :], view(11264, D)]
        lasth, lastl = xh[:, KT - 2:KT, :], xl[:, KT - 2:KT, :]
        baT = cacc[0:2 * GH, 0, :]
        gpair = {kind: view(11264, D) for kind in ("ffn", "swa")}
        gpair["gdn"] = vb[:, 1, :]
        Nm = xg[:, :, :].rearrange("p t d -> p (t d)").rearrange("p (b n) -> p b n", b=4)
        PTm = junk[:, :, :].rearrange("p t d -> p (t d)").rearrange("p (b n) -> p b n", b=4)

        x_in = [sem(f"x_in{t}") for t in range(TT)]
        const_in, out_done, x_out = sem("const_in"), sem("out_done"), sem("x_out")
        raw_in = [sem(f"raw_in{s}") for s in range(SLOTS)]
        gain_in = [sem(f"gain_in{s}") for s in range(2)]
        w_hi, w_lo, w_used = sem("w_hi"), sem("w_lo"), sem("w_used")
        ident_built, tables = sem("ident_built"), sem("tables_built")
        xg_ready, xT_ps, xT_hi, xT_lo = sem("xg_ready"), sem("xT_psum"), sem("xT_hi"), sem("xT_lo")
        xsq, rstd_ready = [sem(f"x_squared{t}") for t in range(TT)], sem("rstd_ready")
        y_ready, ysq, yrs_ready = sem("y_ready"), sem("y_squared"), sem("y_scale_ready")
        base_ready, ys_done = sem("x_base_ready"), sem("y_scaled")
        x_new = [sem(f"x_new{t}") for t in range(TT)]
        h_ready, silu_done, g_done = sem("h_ready"), sem("silu_done"), sem("gated_done")
        hT_ps, hT_hi, hT_lo = sem("hT_psum"), sem("hT_hi"), sem("hT_lo")
        dve_own, pool_own = sem("dve_own"), sem("pool_own")
        trig, dve_trig, cw_ps, cw_done = sem("trig"), sem("angles"), sem("conv_w_psum"), sem("conv_w")
        sp_ready, qkv_ready, rope_ready = sem("swa_proj"), sem("qkv_ready"), sem("rope_ready")
        sT_ps, sT_done = sem("qkT_psum"), sem("qkT_done")
        s_ready, s_masked, p_ready = sem("scores_ready"), sem("scores_masked"), sem("probs_ready")
        pT_ps, pT_done, pv_done = sem("probsT_psum"), sem("probsT_done"), sem("pv_done")
        snk_in, es_done, den_done = sem("sink_arg"), sem("exp_sink_done"), sem("den_done")
        ba_cols, ba_ps, ba_rows = sem("ba_cols"), sem("ba_psum"), sem("ba_rows")
        gate_arg, gate_exp, gate_u, gate_ln, g_ready, beta_ready = (
            sem("gate_arg"), sem("gate_exp"), sem("gate_u"), sem("gate_ln"), sem("g_ready"), sem("beta_ready"))
        gc_ps, gc_done, gdl, eg_done, ekd_done = (
            sem("gcum_psum"), sem("gcum_done"), sem("decay_left"), sem("exp_g"), sem("exp_left"))
        ch_ready, ch_evac, fT_ready = sem("chunk_ready"), sem("chunk_rows"), sem("chunkT_ready")
        tap_done, conv_step, conv_done, chan_done = (
            sem("tap_done"), sem("conv_step"), sem("conv_done"), sem("channels_done"))
        qsq_done, bT_ready, ksq, kss_done, rk_done, kh_done = (
            sem("q_squared"), sem("rows_psum"), sem("k_squared"), sem("k_sumsq"), sem("k_scale"), sem("k_hat"))
        qss_done, rq_done, v_done, z_done, zn_done, kd_done = (
            sem("q_sumsq"), sem("q_scale"), sem("v_beta"), sem("z_silu"), sem("z_normed"), sem("k_decayed"))
        kT_ps, kT_done = sem("kT_psum"), sem("kT_done")
        d_ps, d_exp, n_ps, np_done = sem("decay_psum"), sem("decay_exp"), sem("kk_kq_psum"), sem("n_p_done")
        nm_ready, w0_done, t0_ps, t0_done = sem("masked_n"), sem("w_init"), sem("t_init_psum"), sem("t_init")
        y_ps, y_cp, wt_ps, wt_done = sem("y_psum"), sem("y_copied"), sem("wt_psum"), sem("wt_updated")
        c3 = {k: sem("c3_" + k) for k in ("vn0p", "vn0", "o0p", "o0", "s1p", "s1", "zp", "r1", "ap", "a1",
                                         "vn1p", "vn1", "bp", "o1")}
        gated1 = sem("o_gated1")
        oss_done, ro_done = sem("o_sumsq"), sem("o_scale")

        def own(eng, s):
            n = [0]

            def link(ins, wait=True):
                n[0] += 1
                ins.then_inc(s, 1)
                if wait:
                    eng.wait_ge(s, n[0])
                return n[0]
            return link

        def tile_done(eng, t, first, n, used):
            if t == 0:
                eng.wait_ge(first, n)
            else:
                eng.wait_ge(w_used, used)

        def order(ti, m):
            return (m % 2, m // 2) if ti in OUT_INPUTS else (m // 2, m % 2)

        def chunk_bank(c):
            return 4 if c == 1 else 0 if c % 2 else 2

        def bc(ap, n):
            return ap.unsqueeze(2).to_broadcast([P, ap.shape[1], n])

        def rows(ap, n):
            return ap.unsqueeze(1).to_broadcast([P, n, ap.shape[1]])

        def heads(ap, n=HG):
            return ap.rearrange("p (h d) -> p h d", h=n)

        block = ctx.enter_context(nc.Block())

        @block.sync
        def _(sp):
            def slot(u, c, halves):
                if not (isinstance(u, int) and u < SLOTS):
                    sp.wait_ge(w_lo, u - SLOTS + 1)
                for dst, src in halves(raw[:, c % SLOTS, :]):
                    sp.dma_start(dst, src).then_inc(raw_in[c % SLOTS], 16)

            def up(w, j, k0):
                v = w.rearrange("(k p) (s n) -> p k s n", p=P, s=2)
                at = bass.ds(j * FC, FC)
                return lambda r: [(r.rearrange("p (k s n) -> p k s n", k=4, s=2)[:, :, s, :], v[:, k0:k0 + 4, s, at])
                                  for s in range(2)]

            def down(w, r0):
                return lambda r: [(r[:, k * D:(k + 1) * D], w[bass.ds(r0 + k * P, P), :]) for k in range(2)]

            def block(w, k0, nk, c0, nc_):
                v = w.rearrange("(k p) n -> p k n", p=P)
                h = nk // 2
                return lambda r: [(r[:, q * h * nc_:(q + 1) * h * nc_].rearrange("p (k n) -> p k n", k=h),
                                   v[:, k0 + q * h:k0 + (q + 1) * h, c0:c0 + nc_]) for q in range(2)]

            def ffn(base, wi, wo):
                slot(base, 0, up(wi, 0, 0))
                if base == 0:
                    sp.dma_start(xs[:, 1, :], x[0, P:S, :]).then_inc(x_in[1], 16)
                slot(base + 1, 1, up(wi, 0, 4))
                with sp.Fori(1, STEPS) as j:
                    slot(base + j * 3 - 1, 2, up(wi, j, 0))
                    slot(base + j * 3, 0, up(wi, j, 4))
                    slot(base + j * 3 + 1, 1, down(wo, j * FC - FC))
                slot(base + 3 * STEPS - 1, 2, down(wo, (STEPS - 1) * FC))

            sp.dma_start(xs[:, 0, :], x[0, 0:P, :]).then_inc(x_in[0], 16)
            for n, kind in enumerate(stages):
                base = UBASE[n]
                if kind == "ffn":
                    wi, wo = (l0_ffn_w_in, l0_ffn_w_out) if n < 3 else (l1_ffn_w_in, l1_ffn_w_out)
                    ffn(base, wi[0 if n % 3 == 0 else 1], wo[0 if n % 3 == 0 else 1])
                elif kind == "swa":
                    units = [block(a_w_in, 0, KT, QC, QKVC - QC)]
                    units += [block(a_w_in, 4 * h, 4, c * 512, 512) for c in range(2) for h in range(2)]
                    units += [down(a_w_out, 256 * i) for i in range(4)]
                    for c, u in enumerate(units):
                        slot(base + c, c, u)
                else:
                    units = [block(b_w_in, 4 * h, 4, CHUNKS[c][0], 512) for c in CHUNKS for h in range(2)]
                    units.insert(2, block(b_w_in, 0, KT, 4 * D, 2 * GH))
                    units += [down(b_w_out, 256 * i) for i in range(4)]
                    for c, u in enumerate(units):
                        slot(base + c, c, u)
            for m in range(2 * TT):
                t, cols = m // 2, slice(m % 2 * 512, m % 2 * 512 + 512)
                sp.wait_ge(x_out, m + 1)
                sp.dma_start(out[0, t * P:(t + 1) * P, cols], xs[:, t, cols]).then_inc(out_done, 16)
            sp.wait_ge(out_done, 16 * 2 * TT)

        @block.gpsimd
        def _(pool):
            link = own(pool, pool_own)

            def gain_load(g):
                src = (l0_norms if g < 6 else l1_norms)[g % 6]
                pool.dma_start(gain[:, g % 2, :], src.partition_broadcast(P)).then_inc(gain_in[g % 2], 16)

            def select(v, op, fill, base, pattern, mult):
                link(pool.affine_select(out=v, in_=v, compare_op=op, fill=fill, base=base, pattern=pattern,
                                        channel_multiplier=mult))

            gain_load(0)
            pool.memset(mhalf[:], -0.5)
            pool.memset(ones[:], 1.0)
            link(pool.memset(ident[:], 0.0))
            pool.affine_select(out=ident[:], in_=ident[:], compare_op=ALU.not_equal, fill=1.0, base=0,
                               pattern=[[-1, P]], channel_multiplier=1).then_inc(ident_built, 1)
            link(pool.memset(smask[:], 0.0))
            for c0 in (0, 256):
                select(smask[:, c0:c0 + P], ALU.is_ge, NEG, 0, [[-1, P]], 1)
            select(smask[:, P:2 * P], ALU.is_gt, NEG, 0, [[1, P]], -1)
            link(pool.memset(cumU[:], 1.0))
            select(cumU[:], ALU.is_ge, 0.0, 0, [[1, P]], -1)
            link(pool.memset(negL[:], 0.0))
            select(negL[:], ALU.is_ge, NEG, 0, [[1, P]], -1)
            link(pool.memset(lvl[:], 0.0))
            for i in range(LEVELS):
                b = 1 << i
                nb = P // (2 * b)
                v = lvl[:, i, :].rearrange("p (B h r) -> p B h r", h=2, r=b)[:, :, 1, :]
                link(pool.memset(v, 1.0))
                select(v, ALU.is_ge, 0.0, 0, [[-2 * b, nb], [0, b]], 1)
                select(v, ALU.is_ge, 0.0, b - 1, [[2 * b, nb], [0, b]], -1)
            freq = (500000.0 ** (-np.arange(0, ROT, 2, dtype=np.float32) / ROT)).astype(np.float32)
            for i in range(HALF):
                last = pool.memset(es[:, 0, i:i + 1], float(freq[i]))
            last.then_inc(tables, 1)
            gain_load(1)

            def power(out, src, scale, shift, n, final=None):
                v = pwv[:, 0:n]
                link(pool.tensor_scalar(v, src, scale, shift, ALU.mult, ALU.add))
                ins = pool.tensor_tensor(out if final is None else v, v, mhalf[:, 0:n], ALU.pow)
                if final is not None:
                    link(ins)
                    ins = pool.tensor_scalar(out, v, final, None, ALU.mult)
                return ins

            def rope_group(t, c0, nh):
                v = qkv[:, t, c0:c0 + nh * DH].rearrange("p (h d) -> p h d", h=nh)
                x1, x2 = v[:, :, 0:HALF], v[:, :, HALF:ROT]
                tm = [rope[:, i, 0:nh * HALF].rearrange("p (h d) -> p h d", h=nh) for i in range(4)]
                c, s = rows(cs[:, t, :], nh), rows(sn[:, t, :], nh)
                pool.tensor_tensor(tm[0], x1, c, ALU.mult)
                pool.tensor_tensor(tm[1], x2, s, ALU.mult)
                pool.tensor_tensor(tm[2], x2, c, ALU.mult)
                link(pool.tensor_tensor(tm[3], x1, s, ALU.mult))
                pool.tensor_tensor(x1, tm[0], tm[1], ALU.subtract)
                return pool.tensor_tensor(x2, tm[2], tm[3], ALU.add)

            def swa():
                pool.wait_ge(trig, 1)
                for g, (c0, nh) in enumerate([(QC, KVH), (0, GQ), (512, GQ)]):
                    for t in range(TT):
                        pool.wait_ge(qkv_ready, 2 * g + t + 1)
                        ins = rope_group(t, c0, nh)
                        if g == 0:
                            link(ins)
                            src = qkv[:, t, QC:QC + P].rearrange("p (k d) -> p k d", k=KVH)
                            for dup in range(2):
                                dst = kdup[:, t, :].rearrange("p (k u d) -> p k u d", k=KVH, u=2)[:, :, dup, :]
                                ins = pool.tensor_copy(dst, src)
                                if dup == 0:
                                    link(ins)
                        ins.then_inc(rope_ready, 1)
                        pool.wait_ge(rope_ready, 2 * g + t + 1)
                for kv in range(KVH):
                    hs = slice(kv * GQ, (kv + 1) * GQ)
                    pool.wait_ge(s_masked, 2 * GQ * (kv + 1))
                    pool.tensor_tensor(es[:, :, hs], nm[:, :, hs], rows(sink[:, hs], TT), ALU.add
                                       ).then_inc(snk_in, 1)
                    pool.wait_ge(es_done, kv + 1)
                    pool.tensor_tensor(rl[:, :, hs], rl[:, :, hs], es[:, :, hs], ALU.add).then_inc(den_done, 1)

            sm = [small[:, i, :, :] for i in range(20)]

            def fl(i):
                return small[:, i, :, :].rearrange("p t h -> p (t h)")

            def gdn():
                b_, a_ = sm[0], sm[1]
                pool.wait_ge(ba_rows, 2)
                link(pool.tensor_tensor(a_, a_, rows(dtb[:], TT), ALU.add))
                link(pool.tensor_scalar(sm[2], a_, 0.0, -2.0, ALU.max, ALU.mult))
                pool.tensor_tensor(sm[2], a_, sm[2], ALU.add).then_inc(gate_arg, 1)
                pool.wait_ge(gate_exp, 3)
                link(pool.tensor_scalar(sm[4], sm[4], 1.0, None, ALU.add))
                pool.tensor_scalar(sm[5], sm[3], 1.0, None, ALU.add).then_inc(gate_u, 1)
                pool.wait_ge(gate_u, 1)
                link(pool.tensor_scalar(sm[6], sm[5], -1.0, None, ALU.add))
                link(pool.tensor_tensor(sm[6], sm[3], sm[6], ALU.subtract))
                link(pool.tensor_scalar(a_, a_, 0.0, None, ALU.max))
                link(pool.tensor_tensor(a_, a_, sm[6], ALU.add))
                pool.wait_ge(gate_ln, 1)
                link(pool.tensor_tensor(a_, a_, sm[7], ALU.add))
                link(pool.tensor_tensor(a_, a_, rows(alog[:], TT), ALU.mult))
                pool.tensor_scalar(sm[8], a_, -1.0, None, ALU.mult).then_inc(g_ready, 1)
                def decays():
                    pool.wait_ge(gc_done, 2)
                    pool.tensor_tensor(sm[10], sm[10], sm[9], ALU.subtract).then_inc(gdl, 1)
                    pool.wait_ge(gdl, 1)
                    pool.tensor_scalar(sm[13], sm[9], -1.0, None, ALU.mult).then_inc(gdl, 1)

                for c in range(1, 7):
                    hg = (CHUNKS[c][0] % D) // 512
                    hs = slice(hg * HG, hg * HG + HG)
                    if CHUNKS[c][1] == "k":
                        pool.wait_ge(kss_done, 2 * c)
                        for t in range(TT):
                            power(small[:, 15, t, hs], small[:, 14, t, hs], 1.0, EPS, HG).then_inc(rk_done, 1)
                            pool.wait_ge(rk_done, 2 * (c - 1) + t + 1)
                        if c == 1:
                            decays()
                    elif CHUNKS[c][1] == "q":
                        for i in range(4):
                            pool.wait_ge(chan_done, 4 * (c - 1) + i + 1)
                            pool.tensor_tensor(rT[:, i, :], gqT[:, hg * HG + i, :], gqT[:, hg * HG + i, :],
                                               ALU.mult).then_inc(qsq_done, 1)
                        pool.wait_ge(qss_done, c - 2)
                        for t in range(TT):
                            power(small[:, 17, t, hs], small[:, 16, t, hs], 1.0, EPS, HG,
                                  GD ** -0.5).then_inc(rq_done, 1)
                            pool.wait_ge(rq_done, 2 * (c - 3) + t + 1)
                pool.wait_ge(z_done, 4)
                for t in range(TT):
                    pool.tensor_tensor(heads(zs[:, t, :], GH), heads(zs[:, t, :], GH), rows(nrm[:], GH),
                                       ALU.mult).then_inc(zn_done, 1)
                pool.wait_ge(kT_ps, 4)
                pool.wait_ge(ekd_done, 1)
                pool.tensor_tensor(heads(khat[:, 1, :], GH), heads(khat[:, 0, :], GH),
                                   bc(small[:, 10, 0, :], GD), ALU.mult).then_inc(kd_done, 1)
                for q in range(4 * (LEVELS - 1)):
                    level, b = q // 4 + 1, q % 4
                    if q < 4:
                        pool.wait_ge(np_done, 2 * (b + 1))
                    if q == 0:
                        pool.wait_ge(chan_done, 24)
                    elif q >= 2:
                        pool.wait_ge(y_ps, q - 1)
                    pool.tensor_tensor(heads(NM[:, q % 2, :]), heads(Nm[:, b, :]), rows(lvl[:, level, :], HG),
                                       ALU.mult).then_inc(nm_ready, 1)
                link(pool.tensor_tensor(sm[14], sm[17], sm[17], ALU.mult))
                for m in range(2 * NG):
                    t, hg = divmod(m, NG)
                    hs = slice(hg * HG, hg * HG + HG)
                    pool.wait_ge(oss_done, m + 1)
                    r = small[:, 19, t, hs]
                    link(pool.tensor_tensor(r, small[:, 18, t, hs], small[:, 14, t, hs], ALU.mult))
                    link(power(r, r, 1.0 / GD, EPS, HG))
                    pool.tensor_tensor(r, r, small[:, 17, t, hs], ALU.mult).then_inc(ro_done, 1)

            def base_of_next(n, kind):
                if kind == "gdn":
                    pool.wait_ge(c3["r1"], NG)
                pool.wait_ge(gain_in[0], 16 * (n + 2))
                pool.wait_ge(gain_in[1], 16 * (n + 1))
                pool.tensor_tensor(gpair[kind], gain[:, 0, :], gain[:, 1, :], ALU.mult).then_inc(base_ready, 1)
                pool.wait_ge(xT_ps, 4 * TBASE[n + 1])
                for t in range(TT):
                    pool.tensor_tensor(xg[:, t, :], xs[:, t, :], gain[:, 0, :], ALU.mult).then_inc(base_ready, 1)

            for n, kind in enumerate(stages):
                for t in range(TT):
                    pool.wait_ge(xsq[t], n + 1)
                power(rstd[:], xss[:], 1.0 / D, EPS, TT).then_inc(rstd_ready, 1)
                pool.wait_ge(rstd_ready, n + 1)
                if n:
                    for t in range(TT):
                        pool.wait_ge(x_new[t], n)
                    gain_load(2 * n + 1)
                if n + 1 < len(stages):
                    if n:
                        pool.wait_ge(base_ready, 3 * n)
                    else:
                        pool.wait_ge(xg_ready, 4)
                    gain_load(2 * n + 2)
                if kind == "swa":
                    swa()
                if kind == "gdn":
                    gdn()
                if n + 1 < len(stages):
                    base_of_next(n, kind)
                for t in range(TT):
                    pool.wait_ge(ysq, TT * n + t + 1)
                    power(yrs[:, t:t + 1], yss[:, t:t + 1], 1.0 / D, EPS, 1, COEF[n]).then_inc(yrs_ready, 1)
                    pool.wait_ge(yrs_ready, TT * n + t + 1)
                if n + 1 < len(stages):
                    pool.wait_ge(ys_done, n + 1)
                    link(pool.tensor_tensor(junk[:, 0, :], junk[:, 0, :], gain[:, 1, :], ALU.mult))
                    pool.tensor_tensor(xs[:, 0, :], xs[:, 0, :], junk[:, 0, :], ALU.add).then_inc(x_new[0], 1)

        @block.scalar
        def _(act):
            act.dma_start(posi[:], positions.rearrange("a (t p) -> p (a t)", p=P),
                          allow_slow_non_contiguous=True).then_inc(const_in, 16)
            act.dma_start(sink[:], a_sinks.partition_broadcast(P)).then_inc(const_in, 16)
            act.dma_start(alog[:], b_A_log.partition_broadcast(P)).then_inc(const_in, 16)
            act.dma_start(dtb[:], b_dt_bias.partition_broadcast(P)).then_inc(const_in, 16)
            act.dma_start(cwr[0:TAPS * CT, :], b_conv_w.rearrange("t (c p) -> (t c) p", p=P)).then_inc(const_in, 16)

            def hi(u, c, n=UNIT):
                if isinstance(u, int) and u >= total:
                    return
                third = (u - c % 3) // 3 if isinstance(u, int) else None
                act.wait_ge(raw_in[c % 3], 32 * (third + 1))
                if u >= SLOTS:
                    act.wait_ge(w_used, u - SLOTS + 1)
                act.activation(whi[:, c % 3, 0:n], raw[:, c % 3, 0:n], ACT.Copy).then_inc(w_hi, 1)

            def hi_loop(base, j, c):
                act.wait_ge(raw_in[c % 3], j * 32 + 32 * (base // 3 + c // 3 + 1))
                act.wait_ge(w_used, j * 3 + (base + c - SLOTS + 1))
                act.activation(whi[:, c % 3, :], raw[:, c % 3, :], ACT.Copy).then_inc(w_hi, 1)

            def large_constants():
                act.dma_start(bias, a_b_in.partition_broadcast(P)).then_inc(const_in, 16)
                act.dma_start(nrm[:], b_norm.partition_broadcast(P)).then_inc(const_in, 16)

            def turned(ti, m):
                t, h = order(ti, m)
                act.wait_ge(xT_ps, 4 * ti + m + 1)
                act.activation(xh[:, 4 * h:4 * h + 4, t * P:(t + 1) * P], heads(PS[:, 6 + h, :]),
                               ACT.Copy).then_inc(xT_hi, 1)

            def square_y(n, t):
                tile_done(act, t, y_ready, n + 1, UBASE[n + 1])
                act.wait_ge(xsq[t], n + 1)
                act.activation(junk[:, t, :].rearrange("p (a b) -> p a b", a=2), PS[:, 2 * t:2 * t + 2, :],
                               ACT.Square, accum_out=yss[:, t:t + 1]).then_inc(ysq, 1)

            def enter(n):
                ti = TBASE[n]
                if n:
                    square_y(n - 1, 0)
                    hi(UBASE[n] + 1, 1)
                    turned(ti, 0)
                    square_y(n - 1, 1)
                    turned(ti, 1)
                    act.wait_ge(yrs_ready, TT * (n - 1) + 1)
                    act.activation(junk[:, 0, :].rearrange("p (a b) -> p a b", a=2), PS[:, 0:2, :], ACT.Copy,
                                   scale=yrs[:, 0:1]).then_inc(ys_done, 1)
                else:
                    turned(ti, 0)
                    turned(ti, 1)
                    hi(0, 0)
                    hi(1, 1)
                    large_constants()
                turned(ti, 2)
                turned(ti, 3)
                hi(UBASE[n] + 2, 2)
                if n:
                    act.wait_ge(x_new[0], n)
                else:
                    act.wait_ge(x_in[0], 16)
                act.activation(junk[:, 0, :], xs[:, 0, :], ACT.Square, accum_out=xss[:, 0:1]).then_inc(xsq[0], 1)

            def ffn(n):
                f, base = FFN_OF[n], UBASE[n]

                def silu(j, banks=HBANK):
                    for t in range(TT):
                        if t == 0:
                            act.wait_ge(h_ready, j + (STEPS * f + 1))
                        elif isinstance(j, int):
                            act.wait_ge(w_used, base + (3 * j + 1 if j else 2))
                        else:
                            act.wait_ge(w_used, j * 3 + (base + 1))
                        act.activation(sg[:, t, :], PS[:, banks[t], 0:FC], ACT.Silu,
                                       scale=rstd[:, t:t + 1]).then_inc(silu_done, 1)

                def turn(j, high=hTh[:, :, :]):
                    act.wait_ge(hT_ps, j + (STEPS * f + 1))
                    act.activation(high.rearrange("p k s -> p (k s)"), PS[:, 6, :], ACT.Copy).then_inc(hT_hi, 1)

                act.wait_ge(rstd_ready, n + 1)
                silu(0, HBANK0)
                hi(base + 3, 3)
                hi(base + 4, 4)
                with act.Fori(1, STEPS - 1) as j:
                    turn(j - 1)
                    hi_loop(base, j, 2)
                    silu(j)
                    hi_loop(base, j, 3)
                    hi_loop(base, j, 4)
                if n == 0:
                    act.wait_ge(dve_trig, 1)
                    act.activation(sn[:, :, :].rearrange("p t f -> p (t f)"), ang[:, 0, :], ACT.Sin)
                    act.activation(cs[:, :, :].rearrange("p t f -> p (t f)"), ang[:, 1, :], ACT.Sin
                                   ).then_inc(trig, 1)
                j = STEPS - 1
                turn(j - 1)
                hi(base + 3 * j + 2, 2)
                silu(j)
                turn(j, lasth)
                hi(base + 3 * j + 3, 3)

            def swa(n):
                base = UBASE[n]
                hi(base + 3, 3)
                hi(base + 4, 4)
                hi(base + 5, 5)
                hi(base + 6, 6)

                def turn(e):
                    act.wait_ge(sT_ps, e + 1)
                    if e == 0:
                        act.activation(kT.rearrange("p k s -> p (k s)"), PS[:, 6, :], ACT.Copy).then_inc(sT_done, 1)
                    else:
                        act.activation(qT[:, 2 * e - 2:2 * e, :].rearrange("p k s -> p (k s)"),
                                       PS[:, QBANK[e], :], ACT.Copy).then_inc(sT_done, 1)

                def sink_exp(kv):
                    act.wait_ge(snk_in, kv + 1)
                    v = es[:, :, kv * GQ:(kv + 1) * GQ]
                    act.activation(v, v, ACT.Exp).then_inc(es_done, 1)

                turn(0)
                turn(1)
                turn(2)
                for h in range(NH):
                    if h == 4:
                        hi(base + 7, 7)
                    if h == GQ + 1:
                        sink_exp(0)
                    if h == 3:
                        turn(3)
                        turn(4)
                    act.wait_ge(s_masked, 2 * h + 2)
                    if h >= 3:
                        act.wait_ge(pT_ps, h - 2)
                    act.activation(pr[:, h % 3, 0:P], sc[:, h % 2, 0:P], ACT.Exp, scale=-1.0,
                                   bias=nm[:, 0, h:h + 1], accum_out=rl[:, 0, h:h + 1])
                    act.activation(pr[:, h % 3, P:384], sc[:, h % 2, P:384], ACT.Exp, scale=-1.0,
                                   bias=nm[:, 1, h:h + 1], accum_out=rl[:, 1, h:h + 1]).then_inc(p_ready, 1)
                turned(TBASE[n] + 1, 0)
                sink_exp(1)
                for m in range(1, 4):
                    turned(TBASE[n] + 1, m)
                for c in range(8, 10):
                    hi(base + c, c)

            def gdn(n):
                base = UBASE[n]

                def f(i):
                    return small[:, i, :, :]
                hi(base + 3, 3)
                act.wait_ge(rstd_ready, n + 1)

                def turn_k(e):
                    hg, t = divmod(e, 2)
                    act.wait_ge(kT_ps, e + 1)
                    act.activation(khT[:, hg * HG:hg * HG + HG, t * P:(t + 1) * P], heads(PS[:, KBANK[e], :]),
                                   ACT.Copy).then_inc(kT_done, 1)

                for s in range(1, PROJ_UNITS):
                    c = s // 2
                    if s == 16:
                        turn_k(0)
                        turn_k(1)
                    if s % 2 == 0 and c <= 6:
                        for t in range(TT):
                            tile_done(act, t, ch_ready, c, base + (2 if c == 1 else s + 1))
                            if c > 1:
                                act.wait_ge(fT_ready, 2 * (c - 1))
                            act.activation(stage[:, t, :], PS[:, chunk_bank(c) + t, :], ACT.Copy,
                                           scale=rstd[:, t:t + 1]).then_inc(ch_evac, 1)
                    elif s % 2 == 0:
                        for t in range(TT):
                            tile_done(act, t, ch_ready, c, base + s + 1)
                            act.activation(zs[:, t, (c - 7) * 512:(c - 6) * 512], PS[:, chunk_bank(c) + t, :],
                                           ACT.Silu, scale=rstd[:, t:t + 1]).then_inc(z_done, 1)
                    c = (s - 1) // 2
                    if s % 2 == 1 and 1 <= c <= 6:
                        for i in range(4):
                            act.wait_ge(fT_ready, 2 * (c - 1) + i // 2 + 1)
                            if c > 1:
                                act.wait_ge(chan_done, 4 * (c - 2) + i + 1)
                            tile = CHUNKS[c][0] // P + i
                            act.activation(cacc[:, i, :], PS[:, 6 + i // 2, (i % 2) * S:(i % 2 + 1) * S], ACT.Copy,
                                           scale=cw[:, 3 * CT + tile:3 * CT + tile + 1]).then_inc(tap_done, 1)
                    c = (s - 3) // 2
                    if s % 2 == 1 and c in (1, 2):
                        for t in range(TT):
                            act.wait_ge(bT_ready, 2 * (c - 1) + t + 1)
                            if c == 2:
                                act.wait_ge(kss_done, t + 1)
                            act.activation(junk[:, t, 0:512], PS[:, 4 + t, :], ACT.Square).then_inc(ksq, 1)
                    if s == 16:
                        turn_k(2)
                        turn_k(3)
                    hi(base + s + 3, s + 3)
                    if s == 4:
                        act.wait_ge(gate_arg, 1)
                        act.activation(f(3), f(2), ACT.Exp).then_inc(gate_exp, 1)
                        act.activation(f(4), f(0), ACT.Exp, scale=-1.0).then_inc(gate_exp, 1)
                        act.wait_ge(const_in, 16 * 7)
                        act.activation(alog[:], alog[:], ACT.Exp).then_inc(gate_exp, 1)
                    if s == 5:
                        act.wait_ge(gate_u, 1)
                        act.activation(f(7), f(5), ACT.Ln).then_inc(gate_ln, 1)
                    c = (s - 2) // 2
                    if s % 2 == 0 and 1 <= c <= 6:
                        kind, hg = CHUNKS[c][1], (CHUNKS[c][0] % D) // 512
                        for i in range(4):
                            act.wait_ge(conv_done, 4 * (c - 1) + i + 1)
                            if c > 1:
                                act.wait_ge(bT_ready, 2 * (c - 1))
                            dst = gqT[:, hg * HG + i, :] if kind == "q" else rT[:, i, :]
                            act.activation(dst, cacc[:, i, :], ACT.Silu).then_inc(chan_done, 1)
                    if s == 7:
                        act.wait_ge(gdl, 2)
                        act.activation(f(11), f(9), ACT.Exp).then_inc(eg_done, 1)
                        act.activation(f(10), f(10), ACT.Exp).then_inc(ekd_done, 1)
                def start_t(b):
                    act.wait_ge(t0_ps, b + 1)
                    act.activation(Tm[:, 4 * b:4 * b + 4, :], heads(PS[:, 6 + b % 2, :]), ACT.Copy).then_inc(t0_done, 1)

                for b in range(4):
                    hg, t = divmod(b, 2)
                    act.wait_ge(d_ps, b + 1)
                    if b >= 2:
                        act.wait_ge(np_done, 2 * (b - 1))
                    if b == 3:
                        start_t(0)
                    for i in range(HG):
                        h = hg * HG + i
                        last = act.activation(Dm[:, b % 2, i * P:(i + 1) * P], PS[:, b % 2, i * P:(i + 1) * P],
                                              ACT.Exp, bias=small[:, 13, t, h:h + 1])
                    last.then_inc(d_exp, 1)
                start_t(1)
                for q in range(4 * (LEVELS - 1)):
                    if q in (1, 2):
                        start_t(q + 1)
                    act.wait_ge(y_ps, q + 1)
                    if q < 2:
                        act.wait_ge(np_done, 6 + 2 * q)
                    else:
                        act.wait_ge(wt_ps, q - 1)
                    act.activation(Dm[:, q % 2, :], PS[:, q % 2, :], ACT.Copy).then_inc(y_cp, 1)
                for hg in range(NG):
                    act.wait_ge(c3["s1p"], hg + 1)
                    act.activation(NM[:, hg, :], PS[:, 4 + hg, :], ACT.Copy).then_inc(c3["s1"], 1)

                def sumsq(t, hg, v):
                    for i in range(HG):
                        h = hg * HG + i
                        last = act.activation(osqv[t][:, h * P:(h + 1) * P], v[:, i * P:(i + 1) * P], ACT.Square,
                                              accum_out=small[:, 18, t, h:h + 1])
                    last.then_inc(oss_done, 1)

                for hg in range(NG):
                    act.wait_ge(c3["o0p"], hg + 1)
                    sumsq(0, hg, PS[:, 2 + hg, :])
                turned(TBASE[n] + 1, 0)
                for hg in range(NG):
                    act.wait_ge(c3["o1"], hg + 1)
                    sumsq(1, hg, a1v[hg])
                for m in range(1, 4):
                    turned(TBASE[n] + 1, m)
                for c in range(20, 22):
                    hi(base + c, c)

            for n, kind in enumerate(stages):
                enter(n)
                (ffn if kind == "ffn" else swa if kind == "swa" else gdn)(n)
            for t in range(TT):
                square_y(len(stages) - 1, t)

        @block.tensor
        def _(pe):
            def mm3(dst, sh, sl, wh, wl, start, stop):
                pe.matmul(dst, sh, wh, start=start, stop=False)
                pe.matmul(dst, sh, wl, start=False, stop=False)
                return pe.matmul(dst, sl, wh, start=False, stop=stop)

            def turn_x(ti, m):
                t, h = order(ti, m)
                pe.wait_ge(xg_ready, 4 * ti + m + 1)
                if t:
                    pe.wait_ge(xT_lo, 4 * ti + (m if ti in OUT_INPUTS else m - 1))
                for k in range(4):
                    last = pe.transpose(PS[:, 6 + h, k * P:(k + 1) * P],
                                        xg[:, t, (4 * h + k) * P:(4 * h + k + 1) * P], ident[:])
                last.then_inc(xT_ps, 1)

            def wide(c, t, bank, ncol, nk, k0, start, stop, ks=None):
                wh = whi[:, c % 3, 0:nk * ncol].rearrange("p (k n) -> p k n", k=nk)
                wl = wlo[:, c % 3, 0:nk * ncol].rearrange("p (k n) -> p k n", k=nk)
                for k in ks or range(nk):
                    tok = slice(t * P, (t + 1) * P)
                    last = mm3(bank, xh[:, k0 + k, tok], xl[:, k0 + k, tok], wh[:, k, :], wl[:, k, :],
                               start and k == 0, stop and k == nk - 1)
                return last

            def down(c, t, sh, sl, start, stop, ks=(0, 1)):
                for k in ks:
                    tok = slice(t * P, (t + 1) * P)
                    for h in range(2):
                        cols = slice(k * D + h * 512, k * D + h * 512 + 512)
                        pe.matmul(PS[:, 2 * t + h, :], sh[:, k, tok], whi[:, c % 3, cols],
                                  start=start and k == 0, stop=False)
                        pe.matmul(PS[:, 2 * t + h, :], sh[:, k, tok], wlo[:, c % 3, cols], start=False, stop=False)
                    for h in range(2):
                        cols = slice(k * D + h * 512, k * D + h * 512 + 512)
                        last = pe.matmul(PS[:, 2 * t + h, :], sl[:, k, tok], whi[:, c % 3, cols],
                                         start=False, stop=stop and k == 1)
                return last

            def begin(n):
                ti = TBASE[n]
                if n == 0:
                    turn_x(ti, 0)
                turn_x(ti, 1)
                pe.wait_ge(w_lo, UBASE[n] + 1)
                pe.wait_ge(xT_lo, 4 * ti + 1)

            def turn_next(n):
                if n + 1 < len(stages):
                    turn_x(TBASE[n + 1], 0)

            def ffn(n):
                f, base, ti = FFN_OF[n], UBASE[n], TBASE[n]

                def up(c, t, k0, banks=HBANK):
                    return wide(c, t, PS[:, banks[t], :], 512, 4, k0, k0 == 0, k0 == 4)

                def turn(j):
                    pe.wait_ge(g_done, j * 2 + (2 * STEPS * f + 2))
                    for k in range(2):
                        for t in range(TT):
                            last = pe.transpose(PS[:, 6, k * S + t * P:k * S + (t + 1) * P],
                                                gated[:, t, k * P:(k + 1) * P], ident[:])
                    last.then_inc(hT_ps, 1)

                def up_step(j, first=False):
                    pe.wait_ge(w_lo, j * 3 + base)
                    if first:
                        up(2, 1, 0)
                    for t in range(1 if first else TT):
                        pe.wait_ge(g_done, j * 2 + (2 * STEPS * f + t - 1))
                        last = up(2, t, 0)
                    last.then_inc(w_used, 1)
                    turn(j - 1)
                    pe.wait_ge(w_lo, j * 3 + (base + 1))
                    up(0, 0, 4).then_inc(h_ready, 1)
                    up(0, 1, 4).then_inc(w_used, 1)

                def step(j, first):
                    up_step(j, first)
                    pe.wait_ge(w_lo, j * 3 + (base + 2))
                    pe.wait_ge(hT_lo, j + STEPS * f)
                    for t in range(TT):
                        last = down(1, t, hTh, hTl, first, False)
                    last.then_inc(w_used, 1)

                def first_tile():
                    up(0, 0, 0)
                    pe.wait_ge(w_lo, base + 2)
                    pe.wait_ge(xT_lo, 4 * ti + 2)
                    wide(1, 0, PS[:, 4, :], 512, 4, 4, False, False, (0, 1))
                    turn_x(ti, 2)
                    wide(1, 0, PS[:, 4, :], 512, 4, 4, False, True, (2, 3)).then_inc(h_ready, 1)
                    turn_x(ti, 3)

                begin(n)
                first_tile()
                pe.wait_ge(xT_lo, 4 * ti + 3)
                if n:
                    pe.wait_ge(ys_done, n)
                up(0, 1, 0, HBANK0).then_inc(w_used, 1)
                pe.wait_ge(xT_lo, 4 * ti + 4)
                up(1, 1, 4, HBANK0).then_inc(w_used, 1)
                step(1, True)
                with pe.Fori(2, STEPS - 1) as j:
                    step(j, False)
                j = STEPS - 1
                up_step(j)
                pe.wait_ge(w_lo, base + 3 * j + 2)
                pe.wait_ge(hT_lo, STEPS * f + j)
                down(1, 0, hTh, hTl, False, False, (0,))
                turn(j)
                down(1, 0, hTh, hTl, False, False, (1,))
                pe.wait_ge(w_lo, base + 3 * j + 3)
                pe.wait_ge(hT_lo, STEPS * f + j + 1)
                down(2, 0, lasth, lastl, False, True).then_inc(y_ready, 1)
                down(1, 1, hTh, hTl, False, False).then_inc(w_used, 1)
                down(2, 1, lasth, lastl, False, True, (0,))
                turn_next(n)
                down(2, 1, lasth, lastl, False, True, (1,)).then_inc(w_used, 1)

            def out_proj(n, c0, turned=False):
                base, ti = UBASE[n], TBASE[n] + 1

                def part(i, t, ks=(0, 1)):
                    pe.wait_ge(xT_lo, 4 * ti + 2 * (i // 2) + t + 1)
                    return down(c0 + i, t, xh[:, 2 * i:2 * i + 2, :], xl[:, 2 * i:2 * i + 2, :], i == 0, i == 3,
                                ks)

                if not turned:
                    turn_x(ti, 0)
                for i in range(2):
                    pe.wait_ge(w_lo, base + c0 + i + 1)
                    part(i, 0)
                    if i == 0 and not turned:
                        turn_x(ti, 1)
                pe.wait_ge(xg_ready, 4 * ti + 4)
                turn_x(ti, 2)
                part(0, 1).then_inc(w_used, 1)
                turn_x(ti, 3)
                part(1, 1).then_inc(w_used, 1)
                pe.wait_ge(w_lo, base + c0 + 3)
                part(2, 0)
                pe.wait_ge(w_lo, base + c0 + 4)
                part(3, 0).then_inc(y_ready, 1)
                part(2, 1).then_inc(w_used, 1)
                part(3, 1, (0,))
                turn_next(n)
                part(3, 1, (1,)).then_inc(w_used, 1)

            def swa(n):
                base, ti = UBASE[n], TBASE[n]
                vcol = QC + P

                def turn_q(e):
                    for i in range(2):
                        for t in range(TT):
                            pair = 2 * e - 2 + i
                            last = pe.transpose(PS[:, QBANK[e], i * S + t * P:i * S + (t + 1) * P],
                                                qkv[:, t, pair * P:(pair + 1) * P], ident[:])
                    last.then_inc(sT_ps, 1)

                def scores(h):
                    pair, po, kv = h // 2, (h % 2) * DH, h // GQ
                    pe.wait_ge(sT_done, (2 if h < 4 else 3) if h < GQ else 5)
                    if h >= 2:
                        pe.wait_ge(s_masked, 2 * (h - 1))
                    q, k = qT[po:po + DH, pair, :], kT[po:po + DH, kv, :]
                    pe.matmul(PS[:, h % 2, 0:P], q[:, 0:P], k[:, 0:P], start=True, stop=True)
                    pe.matmul(PS[:, h % 2, P:384], q[:, P:S], k, start=True, stop=True).then_inc(s_ready, 1)

                kvbank = [PS[:, 4 + t, 0:2 * P] for t in range(TT)]
                begin(n)
                wide(0, 0, kvbank[0], 2 * P, KT, 0, True, False, range(4))
                pe.wait_ge(xT_lo, 4 * ti + 2)
                wide(0, 0, kvbank[0], 2 * P, KT, 0, False, True, range(4, KT)).then_inc(sp_ready, 1)
                pe.wait_ge(w_lo, base + 2)
                pe.wait_ge(ys_done, n)
                wide(1, 0, PS[:, 0, :], 512, 4, 0, True, False, (0, 1))
                turn_x(ti, 2)
                wide(1, 0, PS[:, 0, :], 512, 4, 0, False, False, (2, 3))
                turn_x(ti, 3)
                pe.wait_ge(xT_lo, 4 * ti + 3)
                wide(0, 1, kvbank[1], 2 * P, KT, 0, True, False, range(4))
                pe.wait_ge(xT_lo, 4 * ti + 4)
                wide(0, 1, kvbank[1], 2 * P, KT, 0, False, True, range(4, KT)).then_inc(w_used, 1)
                wide(1, 1, PS[:, 1, :], 512, 4, 0, True, False).then_inc(w_used, 1)
                for c in range(2, 5):
                    chunk, h = divmod(c - 1, 2)
                    pe.wait_ge(w_lo, base + c + 1)
                    if c == 3:
                        pe.wait_ge(x_new[1], n)
                    last = wide(c, 0, PS[:, 2 * chunk, :], 512, 4, 4 * h, h == 0, h == 1)
                    if h:
                        last.then_inc(sp_ready, 1)
                    if c == 4:
                        pe.wait_ge(sT_done, 3)
                        pe.wait_ge(qkv_ready, 4)
                        scores(0)
                        scores(1)
                    wide(c, 1, PS[:, 2 * chunk + 1, :], 512, 4, 4 * h, h == 0, h == 1).then_inc(w_used, 1)
                    if c == 3:
                        pe.wait_ge(rope_ready, 2)
                        for kv in range(KVH):
                            for t in range(TT):
                                last = pe.transpose(PS[:, 6, kv * S + t * P:kv * S + (t + 1) * P],
                                                    kdup[:, t, kv * P:(kv + 1) * P], ident[:])
                        last.then_inc(sT_ps, 1)
                        pe.wait_ge(const_in, 16 * 7)
                        pe.transpose(PS[:, 7, 0:TAPS * CT], cwr[0:TAPS * CT, :],
                                     ident[0:TAPS * CT, 0:TAPS * CT]).then_inc(cw_ps, 1)
                        pe.wait_ge(rope_ready, 4)
                        pe.wait_ge(qkv_ready, 2)
                        turn_q(1)
                        pe.wait_ge(cw_done, 1)
                        turn_q(2)
                for step in range(2, NH + 3):
                    if step == 2:
                        pe.wait_ge(qkv_ready, 6)
                    if step == 3:
                        pe.wait_ge(rope_ready, 6)
                        turn_q(3)
                        turn_q(4)
                    if step < NH:
                        scores(step)
                    g = step - 2
                    if 0 <= g < NH:
                        pe.wait_ge(p_ready, g + 1)
                        if g >= 2:
                            pe.wait_ge(pT_done, g - 1)
                        for i in range(3):
                            last = pe.matmul(PS[:, 2 + g % 2, i * P:(i + 1) * P], pr[:, g % 3, i * P:(i + 1) * P],
                                             ident[:], start=True, stop=True)
                        last.then_inc(pT_ps, 1)
                    g = step - 3
                    if g >= 0:
                        pe.wait_ge(pT_done, g + 1)
                        if g == 0:
                            pe.wait_ge(sT_done, 5)
                        kv = g // GQ
                        v = slice(vcol + kv * DH, vcol + (kv + 1) * DH)
                        at = slice((g % GQ) * DH, (g % GQ + 1) * DH)
                        pe.matmul(PS[:, 4 + kv, at], pT[:, g % 2, 0:P], qkv[:, 0, v], start=True, stop=True)
                        pe.matmul(PS[:, 6 + kv, at], pT[:, g % 2, P:2 * P], qkv[:, 0, v], start=True, stop=False)
                        pe.matmul(PS[:, 6 + kv, at], pT[:, g % 2, 2 * P:384], qkv[:, 1, v],
                                  start=False, stop=True).then_inc(pv_done, 1)
                    if step == NH - 1:
                        pe.wait_ge(xg_ready, 4 * ti + 6)
                        turn_x(ti + 1, 0)
                    if step == NH:
                        turn_x(ti + 1, 1)
                out_proj(n, 5, True)

            def gdn(n):
                base, ti = UBASE[n], TBASE[n]
                g_flat = small[:, 8, :, :].rearrange("p t h -> p (t h)")

                def col(i):
                    return slice(i * P, (i + 1) * P)

                def four(bank, lhs, rhs, start=True):
                    for i in range(HG):
                        last = pe.matmul(PS[:, bank, col(i)], lhs(i), rhs(i), start=start, stop=True)
                    return last

                def start_t(b):
                    pe.wait_ge(w0_done, b + 1)
                    if b >= 2:
                        pe.wait_ge(t0_done, b - 1)
                    for i in range(HG):
                        last = pe.transpose(PS[:, 6 + b % 2, col(i)], Wm[:, 4 * b + i, :], ident[:])
                    last.then_inc(t0_ps, 1)

                def turn_chunk(c):
                    pe.wait_ge(ch_evac, 2 * c)
                    if c > 1:
                        pe.wait_ge(conv_done, 4 * (c - 1))
                    for i in range(4):
                        for t in range(TT):
                            at = (i % 2) * S + t * P
                            last = pe.transpose(PS[:, 6 + i // 2, at:at + P], stage[:, t, col(i)], ident[:])
                        if i % 2:
                            last.then_inc(fT_ready, 1)

                def turn_back(c):
                    pe.wait_ge(chan_done, 4 * c)
                    free = {1: (ch_evac, 2), 2: (kh_done, 2), 3: (kh_done, 4), 4: (qss_done, 1), 5: (qss_done, 2),
                            6: (v_done, 2)}[c]
                    pe.wait_ge(*free)
                    if CHUNKS[c][1] == "q":
                        pe.wait_ge(qsq_done, 4 * (c - 2))
                        for t in range(TT):
                            for i in range(4):
                                last = pe.matmul(PS[:, 4, 4 * t + i:4 * t + i + 1], rT[:, i, t * P:(t + 1) * P],
                                                 ones[:, 0:1], start=True, stop=True)
                            last.then_inc(bT_ready, 1)
                    else:
                        for t in range(TT):
                            for i in range(4):
                                last = pe.transpose(PS[:, 4 + t, col(i)], rT[:, i, t * P:(t + 1) * P], ident[:])
                            last.then_inc(bT_ready, 1)

                def turn_k(e):
                    hg, t = divmod(e, 2)
                    pe.wait_ge(kh_done, e + 1)
                    if e < 2:
                        pe.wait_ge(conv_done, 24)
                    else:
                        pe.wait_ge(v_done, 4)
                    for i in range(HG):
                        at = (hg * HG + i) * P
                        last = pe.transpose(PS[:, KBANK[e], col(i)], khat[:, t, at:at + P], ident[:])
                    last.then_inc(kT_ps, 1)

                n2 = 2 * GH
                begin(n)
                wide(0, 0, PS[:, 4, :], 512, 4, 0, True, False)
                pe.wait_ge(w_lo, base + 2)
                pe.wait_ge(xT_lo, 4 * ti + 2)
                wide(1, 0, PS[:, 4, :], 512, 4, 4, False, False, (0, 1))
                turn_x(ti, 2)
                wide(1, 0, PS[:, 4, :], 512, 4, 4, False, True, (2, 3)).then_inc(ch_ready, 1)
                turn_x(ti, 3)
                pe.wait_ge(xT_lo, 4 * ti + 3)
                wide(0, 1, PS[:, 5, :], 512, 4, 0, True, False).then_inc(w_used, 1)
                pe.wait_ge(xT_lo, 4 * ti + 4)
                wide(1, 1, PS[:, 5, :], 512, 4, 4, False, True).then_inc(w_used, 1)
                pe.wait_ge(w_lo, base + 3)
                pe.wait_ge(ys_done, n)
                for k in range(KT):
                    w = slice(k * n2, (k + 1) * n2)
                    last = mm3(PS[0:n2, 0, 0:S], whi[:, 2, w], wlo[:, 2, w], xh[:, k, :], xl[:, k, :],
                               k == 0, k == KT - 1)
                last.then_inc(w_used, 1)
                for s in range(3, PROJ_UNITS):
                    c, h = (s + 1) // 2, (s + 1) % 2
                    pe.wait_ge(w_lo, base + s + 1)
                    if h == 0 and c == 2:
                        pe.wait_ge(x_new[1], n)
                    if h == 0 and c > 2:
                        pe.wait_ge(ch_evac, 2 * (c - 2))
                    if h == 0 and c == 5:
                        pe.wait_ge(gc_done, 2)
                    if h == 0 and c == 3:
                        pe.wait_ge(ba_rows, 2)
                    bank = chunk_bank(c)
                    last = wide(s, 0, PS[:, bank, :], 512, 4, 4 * h, h == 0, h == 1)
                    if h:
                        last.then_inc(ch_ready, 1)
                    if s == 7:
                        pe.wait_ge(g_ready, 1)
                        pe.wait_ge(ch_evac, 6)
                        pe.matmul(PS[:, 0, 0:n2], cumU[:], g_flat, start=True, stop=True)
                        pe.matmul(PS[:, 0, n2:2 * n2], ones[:], g_flat, start=True, stop=True).then_inc(gc_ps, 1)
                    wide(s, 1, PS[:, bank + 1, :], 512, 4, 4 * h, h == 0, h == 1).then_inc(w_used, 1)
                    if s == 3:
                        pe.wait_ge(ba_cols, 1)
                        for t in range(TT):
                            last = pe.transpose(PS[:, 1, t * n2:(t + 1) * n2], baT[:, t * P:(t + 1) * P],
                                                ident[0:n2, 0:n2])
                        last.then_inc(ba_ps, 1)
                    if s % 2 and 1 <= (s - 1) // 2 <= 6:
                        turn_chunk((s - 1) // 2)
                    if s % 2 and 1 <= (s - 3) // 2 <= 6:
                        turn_back((s - 3) // 2)
                    if s >= 15:
                        turn_k(2 * (s - 15))
                        turn_k(2 * (s - 15) + 1)
                pe.wait_ge(z_done, 4)
                pe.wait_ge(v_done, 4)
                for b in range(4):
                    hg, t = divmod(b, 2)
                    tok = slice(t * P, (t + 1) * P)
                    pe.wait_ge(kT_done, 2 * hg + t + 1)
                    if b >= 2:
                        pe.wait_ge(d_exp, b - 1)
                    pe.matmul(PS[:, b % 2, :], ident[:], rows(negL[:], HG), start=True, stop=False)
                    for i in range(HG):
                        h = hg * HG + i
                        last = pe.matmul(PS[:, b % 2, col(i)], small[:, 8, t, h:h + 1].to_broadcast([P, P]), cumU[:],
                                         start=False, stop=i == HG - 1)
                    last.then_inc(d_ps, 1)
                    if b >= 2:
                        pe.wait_ge(np_done, 2 * (b - 1))
                    four(2 + b % 2, lambda i: khT[:, hg * HG + i, tok], lambda i: khT[:, hg * HG + i, tok]
                         ).then_inc(n_ps, 1)
                    pe.wait_ge(kT_done, 4)
                    four(4 + b % 2, lambda i: khT[:, hg * HG + i, tok], lambda i: gqT[:, hg * HG + i, tok]
                         ).then_inc(n_ps, 1)
                    if b >= 2:
                        start_t(b - 2)
                nq = 4 * (LEVELS - 1)
                for q in range(nq + 1):
                    if q in (1, 2):
                        start_t(q + 1)
                    if q < nq:
                        b = q % 4
                        pe.wait_ge(nm_ready, q + 1)
                        if q < 4:
                            pe.wait_ge(t0_done, b + 1)
                        else:
                            pe.wait_ge(wt_done, q - 3)
                        if q < 2:
                            pe.wait_ge(d_exp, 4)
                        else:
                            pe.wait_ge(y_cp, q - 1)
                        four(q % 2, lambda i: NM[:, q % 2, col(i)], lambda i: Tm[:, 4 * b + i, :]).then_inc(y_ps, 1)
                    if q >= 1:
                        r = q - 1
                        b = r % 4
                        pe.wait_ge(y_cp, r + 1)
                        if r < 2:
                            pe.wait_ge(np_done, 8)
                        else:
                            pe.wait_ge(wt_done, r - 1)
                        last = four(2 + r % 2, lambda i: Dm[:, r % 2, col(i)], lambda i: Wm[:, 4 * b + i, :])
                        if r < nq - 4:
                            last = four(4 + r % 2, lambda i: Wm[:, 4 * b + i, :], lambda i: Dm[:, r % 2, col(i)])
                        last.then_inc(wt_ps, 1)
                pe.wait_ge(wt_done, nq)
                for hg in range(NG):
                    four(hg, lambda i: Wm[:, 8 * hg + i, :], lambda i: vb[:, 0, (hg * HG + i) * P:(hg * HG + i + 1) * P]
                         ).then_inc(c3["vn0p"], 1)
                pe.wait_ge(kd_done, 1)
                for hg in range(NG):
                    pe.wait_ge(c3["vn0"], hg + 1)
                    four(4 + hg, lambda i: khat[:, 1, (hg * HG + i) * P:(hg * HG + i + 1) * P],
                         lambda i: Dm[:, hg, col(i)]).then_inc(c3["s1p"], 1)
                for hg in range(NG):
                    four(2 + hg, lambda i: PTm[:, 2 * hg, col(i)], lambda i: Dm[:, hg, col(i)]).then_inc(c3["o0p"], 1)
                for hg in range(NG):
                    pe.wait_ge(c3["s1"], hg + 1)
                    four(6 + hg, lambda i: khT[:, hg * HG + i, P:S], lambda i: NM[:, hg, col(i)]).then_inc(c3["zp"], 1)
                for hg in range(NG):
                    four(hg, lambda i: gqT[:, hg * HG + i, P:S], lambda i: NM[:, hg, col(i)]).then_inc(c3["ap"], 1)
                for hg in range(NG):
                    pe.wait_ge(c3["r1"], hg + 1)
                    pe.wait_ge(c3["o0"], hg + 1)
                    four(2 + hg, lambda i: Wm[:, 8 * hg + 4 + i, :], lambda i: R1[:, hg, col(i)]
                         ).then_inc(c3["vn1p"], 1)
                for hg in range(NG):
                    pe.wait_ge(c3["vn1"], hg + 1)
                    four(4 + hg, lambda i: PTm[:, 2 * hg + 1, col(i)], lambda i: vn1v[hg][:, col(i)]
                         ).then_inc(c3["bp"], 1)
                out_proj(n, PROJ_UNITS)

            pe.wait_ge(ident_built, 1)
            for n, kind in enumerate(stages):
                (ffn if kind == "ffn" else swa if kind == "swa" else gdn)(n)

        @block.vector
        def _(dve):
            link = own(dve, dve_own)

            def lo(u, c):
                if isinstance(u, int) and u >= total:
                    return
                dve.wait_ge(w_hi, u + 1)
                dve.tensor_tensor(wlo[:, c % 3, :], raw[:, c % 3, :], whi[:, c % 3, :], ALU.subtract).then_inc(w_lo, 1)

            def turned(ti, m):
                t, h = order(ti, m)
                dve.wait_ge(xT_hi, 4 * ti + m + 1)
                at = (slice(None), slice(4 * h, 4 * h + 4), slice(t * P, (t + 1) * P))
                dve.tensor_tensor(xl[at], heads(PS[:, 6 + h, :]), xh[at], ALU.subtract).then_inc(xT_lo, 1)

            def scaled(n, t, g, out, h):
                dve.wait_ge(yrs_ready, TT * n + t + 1)
                return link(dve.scalar_tensor_tensor(out=out, in0=PS[:, 2 * t + h, :], scalar=yrs[:, t:t + 1],
                                                     in1=g[:, h * 512:h * 512 + 512], op0=ALU.mult, op1=ALU.mult),
                            wait=False)

            def angles():
                dve.wait_ge(const_in, 16 * 7)
                dve.wait_ge(tables, 1)
                dve.tensor_scalar(nsink[:], sink[:], -1.0, None, ALU.mult)
                link(dve.tensor_copy(ang[:, 2, 0:TT], posi[:]))
                for t in range(TT):
                    last = dve.tensor_scalar(ang[:, 3, t * HALF:(t + 1) * HALF], es[:, 0, 0:HALF], ang[:, 2, t:t + 1], None,
                                             ALU.mult)
                link(last)
                magic = 1.5 * 2.0 ** 23
                c1 = 6.28125
                c2 = float(np.float32(TWO_PI - c1).view(np.uint32).__and__(np.uint32(0xfffff000)).view(np.float32))
                c3_ = TWO_PI - c1 - c2
                turns = ang[:, 2, :]
                for i, quarter in enumerate((0.0, 0.25)):
                    r = ang[:, i, :]
                    link(dve.tensor_scalar(turns, ang[:, 3, :], 1.0 / TWO_PI, quarter, ALU.mult, ALU.add))
                    link(dve.tensor_scalar(turns, turns, magic, None, ALU.add))
                    link(dve.tensor_scalar(turns, turns, magic, None, ALU.subtract))
                    src = ang[:, 3, :]
                    for part in (c1, c2, c3_):
                        link(dve.scalar_tensor_tensor(out=r, in0=turns, scalar=-part, in1=src, op0=ALU.mult, op1=ALU.add))
                        src = r
                    if quarter:
                        link(dve.tensor_scalar(r, r, TWO_PI / 4, None, ALU.add))
                    ins = dve.tensor_scalar(r, r, PI_BELOW, -PI_BELOW, ALU.min, ALU.max)
                    if i == 0:
                        link(ins)
                ins.then_inc(dve_trig, 1)

            def next_input(n, t):
                dve.wait_ge(base_ready, 3 * (n + 1))
                if t:
                    dve.wait_ge(xg_ready, 4 * TBASE[n + 1] + 2)
                made = [scaled(n, t, gpair[stages[n]], tmp[:, h, :], h) for h in range(2)]
                for h in range(2):
                    cols = slice(h * 512, h * 512 + 512)
                    dve.wait_ge(dve_own, made[h])
                    dve.tensor_tensor(xg[:, t, cols], tmp[:, h, :], xg[:, t, cols], ALU.add).then_inc(xg_ready, 1)

            def enter(n):
                ti = TBASE[n]
                if n:
                    next_input(n - 1, 0)
                    turned(ti, 0)
                    lo(UBASE[n] + 1, 1)
                    turned(ti, 1)
                    next_input(n - 1, 1)
                else:
                    dve.wait_ge(gain_in[0], 16)
                    for t in range(TT):
                        dve.wait_ge(x_in[t], 16)
                        for h in range(2):
                            cols = slice(h * 512, h * 512 + 512)
                            dve.tensor_tensor(xg[:, t, cols], xs[:, t, cols], gain[:, 0, cols], ALU.mult
                                              ).then_inc(xg_ready, 1)
                        if t == 0:
                            turned(ti, 0)
                            lo(0, 0)
                            turned(ti, 1)
                    lo(1, 1)
                made = []
                for h in range(2):
                    if n:
                        made.append(scaled(n - 1, 1, gain[:, 1, :], junk[:, 1, h * 512:h * 512 + 512], h))
                        if h == 0:
                            turned(ti, 2)
                if n == 0:
                    turned(ti, 2)
                for h in range(2):
                    if n:
                        cols = slice(h * 512, h * 512 + 512)
                        dve.wait_ge(dve_own, made[h])
                        ins = dve.tensor_tensor(xs[:, 1, cols], xs[:, 1, cols], junk[:, 1, cols], ALU.add)
                if n:
                    ins.then_inc(x_new[1], 1)
                turned(ti, 3)
                if n:
                    dve.wait_ge(x_new[1], n)
                dve.tensor_tensor_reduce(out=junk[:, 1, :], in0=xs[:, 1, :], in1=xs[:, 1, :], scale=1.0, scalar=0.0,
                                         op0=ALU.mult, op1=ALU.add, accum_out=xss[:, 1:2]).then_inc(xsq[1], 1)
                lo(UBASE[n] + 2, 2)

            def ffn(n):
                f, base = FFN_OF[n], UBASE[n]

                def mul(j, banks=HBANK):
                    for t in range(TT):
                        dve.wait_ge(silu_done, j * 2 + (2 * STEPS * f + t + 1))
                        dve.scalar_tensor_tensor(out=gated[:, t, :], in0=PS[:, banks[t], FC:2 * FC],
                                                 scalar=rstd[:, t:t + 1], in1=sg[:, t, :],
                                                 op0=ALU.mult, op1=ALU.mult).then_inc(g_done, 1)

                def turn(j, high=hTh[:, :, :], low=hTl[:, :, :]):
                    dve.wait_ge(hT_hi, j + (STEPS * f + 1))
                    flat = "p k s -> p (k s)"
                    dve.tensor_tensor(low.rearrange(flat), PS[:, 6, :], high.rearrange(flat),
                                      ALU.subtract).then_inc(hT_lo, 1)

                mul(0, HBANK0)
                lo(base + 3, 3)
                lo(base + 4, 4)
                if n == 0:
                    angles()
                with dve.Fori(1, STEPS - 1) as j:
                    turn(j - 1)
                    lo(j * 3 + (base + 2), 2)
                    mul(j)
                    lo(j * 3 + (base + 3), 3)
                    lo(j * 3 + (base + 4), 4)
                j = STEPS - 1
                turn(j - 1)
                lo(base + 3 * j + 2, 2)
                mul(j)
                turn(j, lasth, lastl)
                lo(base + 3 * j + 3, 3)

            def swa(n):
                base = UBASE[n]
                scale = -DH ** -0.5

                def masked(h):
                    dve.wait_ge(s_ready, h + 1)
                    if h >= 2:
                        dve.wait_ge(p_ready, h - 1)
                    for t, cols in enumerate((slice(0, P), slice(P, 384))):
                        dve.tensor_tensor_reduce(out=sc[:, h % 2, cols], in0=PS[:, h % 2, cols],
                                                 in1=smask[:, cols], scale=scale, scalar=nsink[:, h:h + 1],
                                                 op0=ALU.add, op1=ALU.min,
                                                 accum_out=nm[:, t, h:h + 1]).then_inc(s_masked, 1)

                def normed(kv):
                    hs = slice(kv * GQ, (kv + 1) * GQ)
                    dve.wait_ge(den_done, kv + 1)
                    link(dve.reciprocal(es[:, :, hs], rl[:, :, hs]))
                    dve.wait_ge(pv_done, GQ * (kv + 1))
                    for t in range(TT):
                        dve.tensor_tensor(heads(xg[:, t, kv * 512:kv * 512 + 512], GQ),
                                          heads(PS[:, 4 + 2 * t + kv, :], GQ), bc(es[:, t, hs], DH), ALU.mult
                                          ).then_inc(xg_ready, 1)

                def rows_out(g, bank, c0, nc_, used, tiles=range(TT)):
                    for t in tiles:
                        tile_done(dve, t, sp_ready, g + 1, used)
                        dve.scalar_tensor_tensor(out=qkv[:, t, c0:c0 + nc_], in0=PS[:, bank(t), 0:nc_],
                                                 scalar=rstd[:, t:t + 1], in1=bias[:, c0:c0 + nc_],
                                                 op0=ALU.mult, op1=ALU.add).then_inc(qkv_ready, 1)

                dve.wait_ge(rstd_ready, n + 1)
                rows_out(0, lambda t: 4 + t, QC, QKVC - QC, base + 1)
                lo(base + 3, 3)
                lo(base + 4, 4)
                rows_out(1, lambda t: t, 0, 512, base + 3)
                lo(base + 5, 5)
                dve.wait_ge(cw_ps, 1)
                dve.tensor_copy(cw[:], PS[:, 7, 0:TAPS * CT]).then_inc(cw_done, 1)
                lo(base + 6, 6)
                rows_out(2, lambda t: 2 + t, 512, 512, base + 5, (0,))
                masked(0)
                masked(1)
                rows_out(2, lambda t: 2 + t, 512, 512, base + 5, (1,))
                for step in range(2, NH + 2):
                    if step == 6:
                        lo(base + 7, 7)
                    if step < NH:
                        masked(step)
                    g = step - 2
                    if g >= 0:
                        dve.wait_ge(pT_ps, g + 1)
                        dve.tensor_copy(pT[:, g % 2, :], PS[:, 2 + g % 2, 0:384]).then_inc(pT_done, 1)
                    if step == GQ + 4:
                        normed(0)
                    if step == NH:
                        turned(TBASE[n] + 1, 0)
                turned(TBASE[n] + 1, 1)
                normed(1)
                turned(TBASE[n] + 1, 2)
                turned(TBASE[n] + 1, 3)
                for c in range(8, 10):
                    lo(base + c, c)

            def gdn(n):
                base = UBASE[n]

                def f(i):
                    return small[:, i, :, :]

                dve.wait_ge(rstd_ready, n + 1)
                lo(base + 3, 3)
                for s in range(1, PROJ_UNITS):
                    if s == 2:
                        dve.wait_ge(w_used, base + 3)
                        dve.tensor_copy(baT, PS[0:2 * GH, 0, 0:S]).then_inc(ba_cols, 1)
                    if s == 5:
                        dve.wait_ge(gate_u, 1)
                        dve.reciprocal(f(12), f(4)).then_inc(beta_ready, 1)
                    if s == 7:
                        dve.wait_ge(gc_ps, 1)
                        for i in range(2):
                            dve.tensor_copy(f(9 + i), PS[:, 0, i * 2 * GH:(i + 1) * 2 * GH].rearrange(
                                "p (t h) -> p t h", t=TT)).then_inc(gc_done, 1)
                    c = (s - 3) // 2 if s % 2 else 0
                    kind = CHUNKS[c][1] if 1 <= c <= 6 else None
                    hg = (CHUNKS[c][0] % D) // 512 if kind else 0
                    hs = slice(hg * HG, hg * HG + HG)
                    cols = slice(hg * 512, hg * 512 + 512)
                    if kind == "k":
                        for t in range(TT):
                            dve.wait_ge(ksq, 2 * (c - 1) + t + 1)
                            dve.tensor_reduce(small[:, 14, t, hs], heads(junk[:, t, 0:512]), AX.X,
                                              ALU.add).then_inc(kss_done, 1)
                    if kind == "q":
                        dve.wait_ge(bT_ready, 2 * c)
                        dve.tensor_copy(small[:, 16, :, hs], PS[:, 4, 0:2 * HG].rearrange("p (t h) -> p t h", t=TT)
                                        ).then_inc(qss_done, 1)
                    if kind == "v":
                        for t in range(TT):
                            dve.wait_ge(bT_ready, 2 * (c - 1) + t + 1)
                            dve.tensor_copy(vb[:, t, cols], PS[:, 4 + t, :]).then_inc(v_done, 1)
                    lo(base + s + 3, s + 3)
                    if s == 3:
                        dve.wait_ge(ba_ps, 1)
                        for t in range(TT):
                            at = t * 2 * GH
                            dve.tensor_scalar(small[:, 0, t, :], PS[:, 1, at:at + GH], rstd[:, t:t + 1], None,
                                              ALU.mult)
                            dve.tensor_scalar(small[:, 1, t, :], PS[:, 1, at + GH:at + 2 * GH], rstd[:, t:t + 1],
                                              None, ALU.mult).then_inc(ba_rows, 1)
                    c = (s - 1) // 2
                    if s % 2 and 1 <= c <= 6:
                        for pair in range(2):
                            at = {}
                            for k in range(1, TAPS):
                                for i in (2 * pair, 2 * pair + 1):
                                    if k == 1:
                                        dve.wait_ge(tap_done, 4 * (c - 1) + i + 1)
                                    else:
                                        dve.wait_ge(dve_own, at[i])
                                    col = (TAPS - 1 - k) * CT + CHUNKS[c][0] // P + i
                                    x0 = (i % 2) * S
                                    ins = dve.scalar_tensor_tensor(
                                        out=cacc[:, i, k:], in0=PS[:, 6 + i // 2, x0:x0 + S - k],
                                        scalar=cw[:, col:col + 1], in1=cacc[:, i, k:], op0=ALU.mult, op1=ALU.add)
                                    if k == TAPS - 1:
                                        ins.then_inc(conv_done, 1)
                                    else:
                                        at[i] = link(ins, wait=False)
                    if kind == "k":
                        for t in range(TT):
                            dve.wait_ge(rk_done, 2 * ((s - 3) // 2 - 1) + t + 1)
                            dve.tensor_tensor(heads(khat[:, t, cols]), heads(PS[:, 4 + t, :]),
                                              bc(small[:, 15, t, hs], GD), ALU.mult).then_inc(kh_done, 1)
                def start_w(b):
                    v = Wm[:, 4 * b:4 * b + 4, :]
                    dve.wait_ge(np_done, 2 * b + 1)
                    link(dve.tensor_tensor(v, heads(Nm[:, b, :]), rows(lvl[:, 0, :], HG), ALU.mult))
                    dve.tensor_tensor(v, rows(ident[:], HG), v, ALU.subtract).then_inc(w0_done, 1)

                for b in range(4):
                    hg, t = divmod(b, 2)
                    dve.wait_ge(d_exp, b + 1)
                    dve.wait_ge(n_ps, 2 * b + 1)
                    for i in range(HG):
                        at, h = slice(i * P, (i + 1) * P), hg * HG + i
                        last = dve.scalar_tensor_tensor(out=Nm[:, b, at], in0=PS[:, 2 + b % 2, at],
                                                        scalar=small[:, 12, t, h:h + 1], in1=Dm[:, b % 2, at],
                                                        op0=ALU.mult, op1=ALU.mult)
                    last.then_inc(np_done, 1)
                    dve.wait_ge(n_ps, 2 * b + 2)
                    dve.tensor_tensor(PTm[:, b, :], PS[:, 4 + b % 2, :], Dm[:, b % 2, :], ALU.mult
                                      ).then_inc(np_done, 1)
                    start_w(b)
                nq = 4 * (LEVELS - 1)
                for r in range(nq):
                    b = r % 4
                    dve.wait_ge(wt_ps, r + 1)
                    if r < nq - 4:
                        v = Tm[:, 4 * b:4 * b + 4, :]
                        dve.tensor_tensor(v, v, heads(PS[:, 4 + r % 2, :]), ALU.subtract)
                    v = Wm[:, 4 * b:4 * b + 4, :]
                    dve.tensor_tensor(v, v, heads(PS[:, 2 + r % 2, :]), ALU.subtract).then_inc(wt_done, 1)
                dve.wait_ge(eg_done, 1)
                dve.wait_ge(zn_done, TT)

                def part_of(hg):
                    return slice(hg * HG, hg * HG + HG), slice(hg * 512, hg * 512 + 512)

                def output(t, hg):
                    hs, cols = part_of(hg)
                    dve.wait_ge(ro_done, 2 * t + hg + 1)
                    dve.tensor_tensor(heads(xg[:, t, cols]), heads(ov[t][:, cols]), bc(small[:, 19, t, hs], GD),
                                      ALU.mult).then_inc(xg_ready, 1)

                def new_values(t, hg, bank, dst, p_, done):
                    hs, cols = part_of(hg)
                    dve.wait_ge(c3[p_], hg + 1)
                    dve.tensor_tensor(heads(dst), heads(PS[:, bank + hg, :]), bc(small[:, 12, t, hs], GD), ALU.mult
                                      ).then_inc(c3[done], 1)

                for hg in range(NG):
                    new_values(0, hg, 0, Dm[:, hg, :], "vn0p", "vn0")
                for hg in range(NG):
                    hs, cols = part_of(hg)
                    dve.wait_ge(c3["o0p"], hg + 1)
                    dve.wait_ge(oss_done, hg + 1)
                    dve.tensor_tensor(khat[:, 0, cols], PS[:, 2 + hg, :], zs[:, 0, cols], ALU.mult
                                      ).then_inc(c3["o0"], 1)
                for hg in range(NG):
                    hs, cols = part_of(hg)
                    dve.wait_ge(c3["zp"], hg + 1)
                    link(dve.tensor_tensor(heads(R1[:, hg, :]), heads(PS[:, 6 + hg, :]), bc(small[:, 11, 1, hs], GD),
                                           ALU.mult))
                    dve.tensor_tensor(R1[:, hg, :], vb[:, 1, cols], R1[:, hg, :], ALU.subtract
                                      ).then_inc(c3["r1"], 1)
                for hg in range(NG):
                    if hg:
                        new_values(1, 0, 2, vn1v[0], "vn1p", "vn1")
                    hs, cols = part_of(hg)
                    dve.wait_ge(c3["ap"], hg + 1)
                    dve.tensor_tensor(heads(a1v[hg]), heads(PS[:, hg, :]), bc(small[:, 11, 1, hs], GD),
                                      ALU.mult).then_inc(c3["a1"], 1)
                new_values(1, 1, 2, vn1v[1], "vn1p", "vn1")
                output(0, 0)
                for hg in range(NG):
                    dve.wait_ge(c3["bp"], hg + 1)
                    dve.wait_ge(c3["a1"], hg + 1)
                    dve.tensor_tensor(a1v[hg], PS[:, 4 + hg, :], a1v[hg], ALU.add).then_inc(c3["o1"], 1)
                turned(TBASE[n] + 1, 0)
                for hg in range(NG):
                    hs, cols = part_of(hg)
                    dve.wait_ge(c3["o1"], hg + 1)
                    dve.tensor_tensor(vb[:, 0, cols], a1v[hg], zs[:, 1, cols], ALU.mult).then_inc(gated1, 1)
                dve.wait_ge(gated1, NG)
                output(1, 0)
                output(0, 1)
                turned(TBASE[n] + 1, 1)
                output(1, 1)
                turned(TBASE[n] + 1, 2)
                turned(TBASE[n] + 1, 3)
                for c in range(20, 22):
                    lo(base + c, c)

            for n, kind in enumerate(stages):
                enter(n)
                (ffn if kind == "ffn" else swa if kind == "swa" else gdn)(n)
            n = len(stages) - 1
            dve.wait_ge(gain_in[1], 16 * (n + 1))
            for t in range(TT):
                if t:
                    dve.wait_ge(x_out, 2)
                made = [scaled(n, t, gain[:, 1, :], tmp[:, h, :], h) for h in range(2)]
                for h in range(2):
                    cols = slice(h * 512, h * 512 + 512)
                    dve.wait_ge(dve_own, made[h])
                    dve.tensor_tensor(xs[:, t, cols], xs[:, t, cols], tmp[:, h, :], ALU.add).then_inc(x_out, 1)


_INS = ["x", "positions", "l0_norms", "l0_ffn_w_in", "l0_ffn_w_out", "a_w_in", "a_b_in", "a_sinks", "a_w_out",
        "l1_norms", "l1_ffn_w_in", "l1_ffn_w_out", "b_w_in", "b_conv_w", "b_A_log", "b_dt_bias", "b_norm", "b_w_out"]


def kernel(**inputs):
    import numpy as _np
    import concourse.bacc as _bacc
    from concourse import mybir as _mybir
    from concourse.bass_utils import run_bass_kernel_spmd as _run

    nc = _bacc.Bacc("TRN2", target_bir_lowering=False, num_devices=1)
    arrays, args = {}, []
    for name in _INS:
        a = _np.ascontiguousarray(inputs[name])
        arrays[f"in_{name}"] = a
        args.append(nc.dram_tensor(f"in_{name}", a.shape, _mybir.dt.from_np(a.dtype), kind="ExternalInput").ap())
    o = nc.dram_tensor("out_0", (1, S, D), F32, kind="ExternalOutput").ap()
    build(nc, *args, o)
    r = _run(nc, [arrays], core_ids=[0])
    return _np.asarray(r.results[0]["out_0"])
```
